# Optimizing a Trainium2 kernel written in Bass

```python
import jax, jax.numpy as jnp
from jax import lax
import numpy as np

D_MODEL = 1024
BATCH = 1
SEQ = 512
DEPTH = 1

CHUNK = 64
HEAD_DIM = 64
N_FOX_HEADS = D_MODEL // (2 * HEAD_DIM)
N_SB_HEADS = D_MODEL // (2 * HEAD_DIM)
N_HEADS = N_FOX_HEADS + N_SB_HEADS
D_FOX = N_FOX_HEADS * HEAD_DIM
D_SB = N_SB_HEADS * HEAD_DIM
D_MIX = D_FOX + D_SB
QBLOCK = 128
N_EXPERTS = 16
N_GROUPS = 4
EXPERTS_PER_GROUP = N_EXPERTS // N_GROUPS
TOP_K = 2
D_EXPERT = D_MODEL
EXPERT_BLOCK = 128
DEEPNORM_ALPHA = (2 * DEPTH) ** 0.25
DEEPNORM_BETA = (8 * DEPTH) ** -0.25
LN_EPS = 1e-5
RMS_EPS = 1e-6
N_MOD = 6
SPLIT_POINTS = (D_FOX, 2 * D_FOX, 3 * D_FOX, 4 * D_FOX, 4 * D_FOX + N_FOX_HEADS,
                4 * D_FOX + N_FOX_HEADS + D_SB, 4 * D_FOX + N_FOX_HEADS + 2 * D_SB)
N_IN = 4 * D_FOX + N_FOX_HEADS + 3 * D_SB

kernel_name = "hybrid_fox_stickbreak_grouped_moe_deepnorm"

def layer_norm(x, g, b):
    xf = x.astype(jnp.float32)
    mu = jnp.mean(xf, axis=-1, keepdims=True)
    var = jnp.mean(jnp.square(xf - mu), axis=-1, keepdims=True)
    return ((xf - mu) * lax.rsqrt(var + LN_EPS) * g + b).astype(x.dtype)

def _split_heads(t, n_heads):
    B, S, _ = t.shape
    return t.reshape(B, S, n_heads, HEAD_DIM).transpose(0, 2, 1, 3)

def forgetting_attention(q, k, v, log_f):
    B, H, S, Dh = q.shape
    nb = S // QBLOCK
    F = jnp.cumsum(log_f, axis=-1)
    q_blocks = q.reshape(B, H, nb, QBLOCK, Dh).transpose(2, 0, 1, 3, 4)
    F_blocks = F.reshape(B, H, nb, QBLOCK).transpose(2, 0, 1, 3)
    k_pos = jnp.arange(S)
    scale = HEAD_DIM ** -0.5

    def block(args):
        qb, Fb, start = args
        logits = jnp.einsum('bhqd,bhkd->bhqk', qb, k).astype(jnp.float32) * scale
        logits = logits + (Fb[..., :, None] - F[:, :, None, :])
        q_pos = start + jnp.arange(QBLOCK)
        causal = k_pos[None, :] <= q_pos[:, None]
        logits = jnp.where(causal, logits, -jnp.inf)
        p = jax.nn.softmax(logits, axis=-1)
        return jnp.einsum('bhqk,bhkd->bhqd', p.astype(v.dtype), v)

    out = lax.map(block, (q_blocks, F_blocks, jnp.arange(nb) * QBLOCK))
    return out.transpose(1, 2, 0, 3, 4).reshape(B, H, S, Dh)

def stick_breaking_attention(q, k, v):
    B, H, S, Dh = q.shape
    nb = S // QBLOCK
    q_blocks = q.reshape(B, H, nb, QBLOCK, Dh).transpose(2, 0, 1, 3, 4)
    k_pos = jnp.arange(S)
    scale = HEAD_DIM ** -0.5

    def block(args):
        qb, start = args
        z = jnp.einsum('bhqd,bhkd->bhqk', qb, k).astype(jnp.float32) * scale
        q_pos = start + jnp.arange(QBLOCK)
        strict = k_pos[None, :] < q_pos[:, None]
        log_beta = jax.nn.log_sigmoid(z)
        log_keep = jnp.where(strict, jax.nn.log_sigmoid(-z), 0.0)
        later = lax.cumsum(log_keep, axis=3, reverse=True) - log_keep
        w = jnp.where(strict, jnp.exp(log_beta + later), 0.0)
        return jnp.einsum('bhqk,bhkd->bhqd', w.astype(v.dtype), v)

    out = lax.map(block, (q_blocks, jnp.arange(nb) * QBLOCK))
    return out.transpose(1, 2, 0, 3, 4).reshape(B, H, S, Dh)

def hybrid_mixer(u, w_in, b_forget, out_norm_g, w_out):
    B, S, _ = u.shape
    proj = u @ w_in
    fq, fk, fv, fgate, fforget, sq, sk, sv = jnp.split(proj, SPLIT_POINTS, axis=-1)
    log_f = jax.nn.log_sigmoid((fforget + b_forget).astype(jnp.float32)).transpose(0, 2, 1)
    o_fox = forgetting_attention(_split_heads(fq, N_FOX_HEADS), _split_heads(fk, N_FOX_HEADS),
                                 _split_heads(fv, N_FOX_HEADS), log_f)
    o_sb = stick_breaking_attention(_split_heads(sq, N_SB_HEADS), _split_heads(sk, N_SB_HEADS),
                                    _split_heads(sv, N_SB_HEADS))
    o = jnp.concatenate([o_fox, o_sb], axis=1).transpose(0, 2, 1, 3)
    of = o.astype(jnp.float32)
    of = of * lax.rsqrt(jnp.mean(jnp.square(of), axis=-1, keepdims=True) + RMS_EPS)
    o = (of * out_norm_g.reshape(N_HEADS, HEAD_DIM)).astype(u.dtype).reshape(B, S, D_MIX)
    o = jnp.concatenate([o[..., :D_FOX] * jax.nn.sigmoid(fgate), o[..., D_FOX:]], axis=-1)
    return o @ w_out

def grouped_moe(h, w_router, b_router, w_gate, w_up, w_down):
    T, D = h.shape
    probs = jax.nn.softmax((h @ w_router).astype(jnp.float32), axis=-1)
    sel = probs + b_router
    group_score = lax.top_k(sel.reshape(T, N_GROUPS, EXPERTS_PER_GROUP), TOP_K)[0].sum(-1)
    best_group = jnp.argmax(group_score, axis=-1)
    in_group = (jnp.arange(N_EXPERTS) // EXPERTS_PER_GROUP)[None, :] == best_group[:, None]
    _, expert_idx = lax.top_k(jnp.where(in_group, sel, -jnp.inf), TOP_K)
    gate_w = jnp.take_along_axis(probs, expert_idx, axis=-1)
    gate_w = gate_w / jnp.sum(gate_w, axis=-1, keepdims=True)

    A = T * TOP_K
    flat_e = expert_idx.reshape(-1)
    flat_tok = jnp.repeat(jnp.arange(T), TOP_K)
    flat_w = gate_w.reshape(-1)
    order = jnp.argsort(flat_e)
    sorted_e = flat_e[order]
    sorted_tok = flat_tok[order]
    sorted_w = flat_w[order]
    counts = jnp.bincount(flat_e, length=N_EXPERTS)
    padded = (counts + EXPERT_BLOCK - 1) // EXPERT_BLOCK * EXPERT_BLOCK
    starts = jnp.cumsum(counts) - counts
    pad_ends = jnp.cumsum(padded)
    pad_starts = pad_ends - padded
    dest = pad_starts[sorted_e] + (jnp.arange(A) - starts[sorted_e])
    n_blocks = A // EXPERT_BLOCK + N_EXPERTS
    P = n_blocks * EXPERT_BLOCK
    row_tok = jnp.zeros((P,), jnp.int32).at[dest].set(sorted_tok.astype(jnp.int32))
    block_e = jnp.minimum(jnp.searchsorted(pad_ends, jnp.arange(n_blocks) * EXPERT_BLOCK, side='right'),
                          N_EXPERTS - 1)
    xs = h[row_tok].reshape(n_blocks, EXPERT_BLOCK, D)

    def expert_block(args):
        xb, e = args
        return (jax.nn.silu(xb @ w_gate[e]) * (xb @ w_up[e])) @ w_down[e]

    yb = lax.map(expert_block, (xs, block_e)).reshape(P, D)
    y_assign = yb[dest] * sorted_w[:, None].astype(h.dtype)
    return jax.ops.segment_sum(y_assign, sorted_tok, num_segments=T)

def setup_inputs(seed: int = 0) -> dict:
    key = jax.random.key(seed)
    ks = jax.random.split(key, 18)
    f32 = jnp.float32
    nrm = lambda k, shape, s: jax.random.normal(k, shape, f32) * s
    col_scale = jnp.concatenate([jnp.ones((2 * D_FOX,), f32), jnp.full((D_FOX,), DEEPNORM_BETA, f32),
                                 jnp.ones((D_FOX + N_FOX_HEADS + 2 * D_SB,), f32),
                                 jnp.full((D_SB,), DEEPNORM_BETA, f32)])
    return {
        "x": nrm(ks[0], (BATCH, SEQ, D_MODEL), 1.0),
        "c": nrm(ks[1], (BATCH, D_MODEL), 1.0),
        "w_mod": nrm(ks[2], (DEPTH, D_MODEL, N_MOD * D_MODEL), 0.5 * D_MODEL ** -0.5),
        "b_mod": nrm(ks[3], (DEPTH, N_MOD * D_MODEL), 0.02),
        "w_in": nrm(ks[4], (DEPTH, D_MODEL, N_IN), D_MODEL ** -0.5) * col_scale,
        "b_forget": jax.random.uniform(ks[5], (DEPTH, N_FOX_HEADS), f32, 1.0, 5.0),
        "out_norm_g": 1.0 + nrm(ks[6], (DEPTH, D_MIX), 0.02),
        "w_out": nrm(ks[7], (DEPTH, D_MIX, D_MODEL), D_MIX ** -0.5 * DEEPNORM_BETA),
        "ln1_g": 1.0 + nrm(ks[8], (DEPTH, D_MODEL), 0.02),
        "ln1_b": nrm(ks[9], (DEPTH, D_MODEL), 0.02),
        "w_router": nrm(ks[10], (D_MODEL, N_EXPERTS), D_MODEL ** -0.5),
        "b_router": nrm(ks[11], (N_EXPERTS,), 0.01),
        "w_gate": nrm(ks[12], (DEPTH, N_EXPERTS, D_MODEL, D_EXPERT), D_MODEL ** -0.5),
        "w_up": nrm(ks[13], (DEPTH, N_EXPERTS, D_MODEL, D_EXPERT), D_MODEL ** -0.5 * DEEPNORM_BETA),
        "w_down": nrm(ks[14], (DEPTH, N_EXPERTS, D_EXPERT, D_MODEL), D_EXPERT ** -0.5 * DEEPNORM_BETA),
        "ln2_g": 1.0 + nrm(ks[15], (DEPTH, D_MODEL), 0.02),
        "ln2_b": nrm(ks[16], (DEPTH, D_MODEL), 0.02),
    }

def reference(x, c, w_mod, b_mod, w_in, b_forget, out_norm_g, w_out, ln1_g, ln1_b,
              w_router, b_router, w_gate, w_up, w_down, ln2_g, ln2_b):
    B, S, D = x.shape
    cond = jax.nn.silu(c)
    for l in range(DEPTH):
        mod = (cond @ w_mod[l] + b_mod[l])[:, None, :]
        sh_a, sc_a, g_a, sh_f, sc_f, g_f = jnp.split(mod, N_MOD, axis=-1)
        u = x * (1.0 + sc_a) + sh_a
        y = hybrid_mixer(u, w_in[l], b_forget[l], out_norm_g[l], w_out[l])
        x = layer_norm(DEEPNORM_ALPHA * x + (1.0 + g_a) * y, ln1_g[l], ln1_b[l])
        u = x * (1.0 + sc_f) + sh_f
        y = grouped_moe(u.reshape(B * S, D), w_router, b_router, w_gate[l], w_up[l], w_down[l]).reshape(B, S, D)
        x = layer_norm(DEEPNORM_ALPHA * x + (1.0 + g_f) * y, ln2_g[l], ln2_b[l])
    return x


_drawn_inputs = setup_inputs


def setup_inputs(seed=0):
    import zlib

    import numpy as np

    out = dict(_drawn_inputs(seed))
    spreads = {}
    factors = {'out_norm_g': 4.424, 'ln2_g': 2.874, 'ln2_b': 2.858}
    for name, (base, spread) in spreads.items():
        noise = np.random.default_rng([zlib.crc32(name.encode()), seed]).standard_normal(out[name].shape)
        drawn = base * np.exp(spread * noise) if base else spread * noise
        out[name] = __import__('jax').numpy.asarray(drawn.astype(out[name].dtype))
    for name, factor in factors.items():
        out[name] = (out[name] * factor).astype(out[name].dtype)
    return out
```

```python
from contextlib import ExitStack

import concourse.bass as bass
import concourse.mybir as mybir
from concourse.alu_op_type import AluOpType as ALU

ACT = mybir.ActivationFunctionType
AX_X = mybir.AxisListType.X
F32 = mybir.dt.float32
BF16 = mybir.dt.bfloat16
I32 = mybir.dt.int32

P = 128
D = 1024
T = 512
KT = D // P
TB = T // P
HD = 64
HEADS = 8
DG = HEADS * HD
E = 16
EPG = 4
GROUPS = E // EPG
FC = P
MAX_CHUNKS = E + (2 * T - 1) // FC
ALPHA = 2.0 ** 0.25
LN_EPS = 1e-5
RMS_EPS = 1e-6
NEG = -1e30
BIG_Z = 40.0
WIDTHS = (64, 80, 96, 112, 128)

SB_OFF = 4 * DG + HEADS
GROUP_COLS = [0, DG, SB_OFF, SB_OFF + DG, 2 * DG, SB_OFF + 2 * DG, 3 * DG]
FQ, FK, SQ, SK, FV, SV, GATE = range(7)
UNITS = 4 * len(GROUP_COLS)

SH_A, SC_A, G_A, SH_F, SC_F, G_F = range(6)
MOD_ORDER = [SC_A, SH_A, G_A, SH_F, SC_F, G_F]

COL_BMOD, COL_C, COL_LNG, COL_LNB, COL_ONG, N_COLS = 0, 48, 56, 64, 72, 80


def build(nc, x, c, w_mod, b_mod, w_in, b_forget, out_norm_g, w_out, ln1_g, ln1_b,
          w_router, b_router, w_gate, w_up, w_down, ln2_g, ln2_b, out):
    normed_dram = nc.dram_tensor("normed_rows", [T, D], F32).ap()
    result_dram = nc.dram_tensor("expert_rows", [MAX_CHUNKS * FC, D], F32).ap()

    with ExitStack() as ctx:
        def sb(name, shape, dt=F32):
            return ctx.enter_context(nc.sbuf_tensor(name, shape, dt))

        def sem(name):
            return ctx.enter_context(nc.semaphore(name))

        W = sb("weights", [P, 24 * D])
        RA = sb("region_a", [P, KT * T])
        RB = sb("region_b", [P, 8192])
        RQ = sb("region_q", [P, 16 * T])
        RV = sb("region_v", [P, 8 * T])
        RG = sb("region_g", [P, 4 * T])

        mod_home = [W[:, s * 8192:(s + 1) * 8192].rearrange("p (c n) -> p c n", c=KT) for s in range(3)]
        gate_w, up_w, down_w = mod_home
        wout = mod_home[2]
        uT = RA[:, :].rearrange("p (c t) -> p c t", c=KT)
        o_tok = RA[:, :].rearrange("p (b n) -> p b n", b=TB)
        u2T = uT
        win_ring = [RB[:, s * 4096:(s + 1) * 4096].rearrange("p (c n) -> p c n", c=KT) for s in range(2)]
        x_tok = RQ[:, 0:4096].rearrange("p (b n) -> p b n", b=TB)
        qf, kf, qs, ks = (RQ[:, n * 2048:(n + 1) * 2048].rearrange("p (c t) -> p c t", c=4) for n in range(4))
        oT = RQ[:, 0:4096].rearrange("p (c t) -> p c t", c=KT)
        resid = RQ[:, 4096:8192].rearrange("p (b n) -> p b n", b=TB)
        vf, vs = (RV[:, n * 2048:(n + 1) * 2048].rearrange("p (b n) -> p b n", b=TB) for n in range(2))
        gate = RG[:, :].rearrange("p (b n) -> p b n", b=TB)

        def mod_sum(pos):
            return RV[:, pos * D:(pos + 1) * D] if pos < 4 else RG[:, (pos - 4) * D:(pos - 3) * D]

        fgt = [RQ[0:HEADS, 6144 + n * T:6144 + (n + 1) * T] for n in range(4)]

        def packed(base, width):
            offs = [base + sum(width(j) for j in range(i)) for i in range(TB)]
            return [RB[:, offs[i]:offs[i] + width(i)] for i in range(TB)]

        sp = packed(0, lambda i: (TB - i) * P)
        wT = packed(1280, lambda i: (TB - i) * P)
        pr = packed(2560, lambda b: (b + 1) * P)
        pT = packed(3840, lambda b: (b + 1) * P)
        def span(n):
            return slice(0, 3 * P) if n == 0 else slice(0, (n + 2) * P)

        sp_part, wT_part, z_part = ([], [], [])
        for n in range(3):
            at = (896, 512, 0)[n]
            sp_part.append(RB[:, at:at + span(n).stop])
            wT_part.append(RB[:, 1280 + at:1280 + at + span(n).stop])
        sq_fox = RB[:, 5120:5376]
        sq_sb = RB[:, 5376:5632]
        zeros = RB[:, 5632:6144]
        ga_row = RB[:, 6144:7168]
        ga_diag = RB[:, 7168:8192].rearrange("p (c n) -> p c n", c=KT)
        ln_tmp = RV[:, 0:D]

        rows_in = RB[:, 0:1024]
        rowsT = RB[:, 1024:2048].rearrange("p (c r) -> p c r", c=KT)
        hT = RB[:, 2048:3072].rearrange("p (c r) -> p c r", c=KT)
        yT = RB[:, 3072:4096].rearrange("p (c r) -> p c r", c=KT)
        rows_out = RB[:, 4096:5120]
        silu = RB[:, 5120:5632]
        ln_rows = [RV[:, n * D:(n + 1) * D] for n in range(4)]
        back = [[r[:, b * D:(b + 1) * D] for b in range(TB)] for r in (RQ, RA)]

        used = [0]

        def rt(n, *shape):
            a = RG[:, used[0]:used[0] + n]
            used[0] += n
            return a

        slot_hot = RG[:, 0:1024].rearrange("p (k s) -> p k s", k=2 * TB)
        used[0] = 1024
        chunk_tok = rt(2 * TB * (MAX_CHUNKS + 1)).rearrange("p (k s) -> p k s", k=2 * TB)
        prob, sel, selm, score = (rt(TB * E) for _ in range(4))
        hot = [rt(TB * E) for _ in range(2)]
        pair6 = rt(TB * GROUPS * 6).rearrange("p (g s) -> p g s", s=6)
        gscore, ghot, gtie = (rt(TB * GROUPS) for _ in range(3))
        where = [rt(TB * E) for _ in range(2)]
        rout = RV[:, 0:512]

        ident = sb("ident", [P, P])
        ident_b = sb("ident_b", [P, P], BF16)
        mask_fox = sb("mask_fox", [P, P], BF16)
        mask_sb = sb("mask_sb", [P, P], BF16)
        neg_tri = sb("neg_tri", [P, P])
        neg_ones = sb("neg_ones", [P, P])
        one_col = sb("one_col", [P, 1])
        before = ident_b
        head_sel = sb("head_sel", [P, HEADS, P], BF16)
        f_split = sb("f_split", [P, T], BF16)
        col_stage = sb("col_stage", [N_COLS, P])
        cols = sb("cols", [P, N_COLS])
        modc = sb("modc", [P, 48])
        cond = sb("cond", [P, 3, KT])
        w_forget = sb("w_forget", [P, KT, HEADS])
        bf_col = sb("bf_col", [HEADS, 1])
        lsum = sb("lsum", [P, HEADS, TB])
        nmax = sb("nmax", [P, 2, TB])
        rms_t = sb("rms_t", [P, 2, 3, TB])
        neg_half = sb("neg_half", [P, TB])
        stats = sb("stats", [P, 2, 6])
        mv = sb("mv", [P, TB, 2])
        rstd = sb("rstd", [P, 2, TB])
        in2 = sb("in2", [P, 2, KT])
        wr = f_split[:, 0:2 * KT * E].bitcast(F32).rearrange("p (c e) -> p c e", c=KT)
        small = sb("small", [P, 64])
        table = sb("table", [1, 64], I32)
        row_idx = sb("row_idx", [P, MAX_CHUNKS + 1], I32)
        row_now = sb("row_now", [P, 1], I32)
        dest = sb("dest", [P, 2 * TB], I32)
        ps = ctx.enter_context(nc.psum_tensor("ps", [P, 8, 512], F32))

        Z_AT = [(4, 0), (5, 0), (6, 0), (6, 2 * P)]
        z_part = [ps[:, (6, 5, 4)[n], span(n)] for n in range(3)]
        FOX_OUT, SB_OUT = 3, 7

        iota_r = head_sel[:, 0:2, :].rearrange("p h n -> p (h n)").bitcast(F32)
        iota_i = head_sel[:, 2:4, :].rearrange("p h n -> p (h n)").bitcast(I32)
        one_b = head_sel[:, 4, :]
        chosen = head_sel[:, 5, 0:TB * E].rearrange("p (b e) -> p b e", b=TB)
        fl = head_sel[:, 6:8, :].rearrange("p h n -> p (h n)").bitcast(F32)
        tie_e, tie_g, tok_id = fl[:, 0:E], fl[:, 16:16 + GROUPS], fl[:, 32:32 + TB]
        b_rout = fl[:, 48:48 + E]
        tok_i = fl[:, 64:64 + TB].bitcast(I32)

        S = {}
        for name in """rows_landed x_landed wf_landed bf_landed wout_landed xr_landed br_landed wr_landed
            lnrow_landed consts cols_up cols_ready cond_exp cond_ready mod_summed mod_up mod_ready
            xT_up uT_ready f_up f_abs f_exp f_ready unit_done unit_ready gate_ready
            z_ready clamped sp_log sp_ready r_ready stick_ready
            s_ready max_ready prob_ready t_up pT_ready fox_ready sb_ready
            fox_sq sb_sq rms_ask rms_got fox_freed sb_freed fox_gated qk_dead
            diag_ready ga_up ga_ready oT_up oT_ready y_up ln_freed ln_ask ln_got normed
            normed_stored nT_up u2T_ready logits_up rcopy_ready rank_up idx_up
            rconst routed_hot tables_ready idx_now dest_ready rexp slots_ready prob_e
            gathered xg_up xT_act xT_dve gu_up silu_done h_ready y2_up y2_act y2_dve yrow_up
            out_act out_dve rows_stored down_free x1_ready
            sp_exp row_set spare_cleared uT_ready_d gather_go oT_ready_d u2T_ready_d fin_ask fin_got fin_done out_stored dve_step act_step pool_step""".split():
            S[name] = sem(name)
        mod_landed = [sem(f"mod_landed_{s}") for s in range(6)]
        win_landed = [sem(f"win_landed_{s}") for s in range(2)]
        gu_landed = [sem(f"gate_up_landed_{s}") for s in range(4)]
        gu_free = sem("gate_up_free")
        dn_landed = [sem(f"down_landed_{s}") for s in range(2)]
        back_landed = [sem(f"back_landed_{s}") for s in range(2 * TB)]

        w_mod_v = w_mod[0].rearrange("(c p) n -> p c n", p=P)
        w_in_v = w_in[0].rearrange("(c p) n -> p c n", p=P)
        w_out_v = w_out[0].rearrange("(c p) n -> p c n", p=P)
        x_v = x[0].rearrange("(b p) n -> p b n", p=P)
        out_v = out[0].rearrange("(b p) n -> p b n", p=P)
        normed_v = normed_dram.rearrange("(b p) n -> p b n", p=P)

        block = ctx.enter_context(nc.Block())

        @block.sync
        def _(sp_):
            for r0, src in ((COL_BMOD, b_mod), (COL_C, c), (COL_LNG, ln1_g), (COL_LNB, ln1_b),
                            (COL_ONG, out_norm_g)):
                n = src.shape[1] // P
                sp_.dma_start(col_stage[r0:r0 + n, :], src.rearrange("a (r n) -> (a r) n", n=P)
                              ).then_inc(S["rows_landed"], 16)
            sp_.dma_start(x_tok, x_v).then_inc(S["x_landed"], 16)

            def load_mod(pos):
                seg = MOD_ORDER[pos]
                if pos >= 3:
                    sp_.wait_ge(S["mod_summed"], pos - 2)
                for half in range(2):
                    cs = slice(4 * half, 4 * half + 4)
                    sp_.dma_start(mod_home[pos % 3][:, cs, :], w_mod_v[:, cs, seg * D:(seg + 1) * D]
                                  ).then_inc(mod_landed[2 * (pos % 3) + half], 16)

            def load_win(g):
                if g >= 2:
                    sp_.wait_ge(S["unit_done"], 4 * (g - 1))
                sp_.dma_start(win_ring[g % 2], w_in_v[:, :, GROUP_COLS[g]:GROUP_COLS[g] + DG]
                              ).then_inc(win_landed[g % 2], 16)

            load_mod(0)
            load_mod(1)
            sp_.dma_start(w_forget[:], w_in_v[:, :, 4 * DG:4 * DG + HEADS]).then_inc(S["wf_landed"], 16)
            sp_.dma_start(bf_col[:], b_forget.rearrange("a h -> h a")).then_inc(S["bf_landed"], 16)
            load_win(0)
            load_win(1)
            for pos in range(2, 6):
                load_mod(pos)
            sp_.wait_ge(S["mod_summed"], 6)
            sp_.dma_start(wout, w_out_v).then_inc(S["wout_landed"], 16)

            def load_gate_up(e, piece):
                cs = slice(256 * piece, 256 * piece + 256)
                for home, w in ((gate_w, w_gate), (up_w, w_up)):
                    sp_.dma_start(home[:, :, cs], w[0, e].rearrange("(c p) f -> p c f", p=P)[:, :, cs]
                                  ).then_inc(gu_landed[piece], 16)

            def load_down(e, piece):
                cs = slice(4 * piece, 4 * piece + 4)
                sp_.dma_start(down_w[:, cs, :], w_down[0, e].rearrange("(c p) d -> p c d", p=P)[:, cs, :]
                              ).then_inc(dn_landed[piece], 16)

            for g in range(2, 7):
                load_win(g)
            for piece in range(4):
                load_gate_up(0, piece)
            sp_.wait_ge(S["qk_dead"], 1)
            sp_.dma_start(resid, x_v).then_inc(S["xr_landed"], 16)
            sp_.wait_ge(S["y_up"], TB)
            load_down(0, 0)
            load_down(0, 1)
            with sp_.Fori(0, E - 1) as used:
                for piece in range(4):
                    sp_.wait_ge(gu_free, 4 * used + piece + 1)
                    load_gate_up(used + 1, piece)
                for piece in range(2):
                    sp_.wait_ge(S["down_free"], 2 * used + piece + 1)
                    load_down(used + 1, piece)
            for b in range(TB):
                sp_.wait_ge(S["fin_done"], b + 1)
                sp_.dma_start(out_v[:, b, :], back[0][b]).then_inc(S["out_stored"], 16)
            sp_.wait_ge(S["out_stored"], 16 * TB)

        @block.gpsimd
        def _(pool):
            steps = [0]

            def step(ins):
                steps[0] += 1
                ins.then_inc(S["pool_step"], 1)
                pool.wait_ge(S["pool_step"], steps[0])

            pool.memset(ident[:], 0.0)
            pool.memset(ident_b[:], 0.0)
            pool.memset(mask_fox[:], 0.0)
            pool.memset(mask_sb[:], 0.0)
            pool.memset(neg_tri[:], -1.0)
            pool.memset(neg_ones[:], -1.0)
            pool.memset(one_col[:], 1.0)
            pool.memset(neg_half[:], -0.5)
            pool.memset(f_split[:], 0.0)
            step(pool.memset(head_sel[:], 0.0))
            pool.affine_select(out=ident[:], in_=ident[:], compare_op=ALU.not_equal, fill=1.0, base=0,
                               pattern=[[-1, P]], channel_multiplier=1)
            pool.affine_select(out=ident_b[:], in_=ident_b[:], compare_op=ALU.not_equal, fill=1.0, base=0,
                               pattern=[[-1, P]], channel_multiplier=1)
            pool.affine_select(out=mask_fox[:], in_=mask_fox[:], compare_op=ALU.is_ge, fill=NEG, base=0,
                               pattern=[[-1, P]], channel_multiplier=1)
            pool.affine_select(out=mask_sb[:], in_=mask_sb[:], compare_op=ALU.is_ge, fill=NEG, base=-1,
                               pattern=[[1, P]], channel_multiplier=-1)
            pool.affine_select(out=neg_tri[:], in_=neg_tri[:], compare_op=ALU.is_ge, fill=0.0, base=0,
                               pattern=[[-1, P]], channel_multiplier=1)
            for part in range(3):
                step(pool.affine_select(out=head_sel[:], in_=head_sel[:], compare_op=ALU.not_equal, fill=1.0,
                                        base=-32 * part, pattern=[[-1, HEADS], [0, P]],
                                        channel_multiplier=1))
            pool.memset(small[:], 0.0).then_inc(S["consts"], 1)

            pool.wait_ge(S["unit_done"], UNITS)
            step(pool.memset(zeros, 0.0))
            pool.dma_start(result_dram[E * FC:, :].rearrange("(p q) (h n) -> p (q h) n", p=P, n=512),
                           zeros.unsqueeze(1).broadcast_to([P, 2 * (MAX_CHUNKS - E), 512])
                           ).then_inc(S["spare_cleared"], 16)

            def rms_power(n):
                pool.wait_ge(S["rms_ask"], n + 1)
                pool.tensor_tensor(rms_t[:, n % 2, 2, :], rms_t[:, n % 2, 1, :], neg_half[:], ALU.pow
                                   ).then_inc(S["rms_got"], 1)

            def fox_gate(h):
                pool.wait_ge(S["fox_freed"], h + 1)
                pool.wait_ge(S["gate_ready"], 1)
                cs = slice(h * HD, (h + 1) * HD)
                pool.tensor_tensor(o_tok[:, :, cs], o_tok[:, :, cs], gate[:, :, cs], ALU.mult
                                   ).then_inc(S["fox_gated"], 1)

            for h in range(HEADS):
                if h:
                    rms_power(2 * h - 2)
                    rms_power(2 * h - 1)
                    fox_gate(h - 1)
            rms_power(2 * HEADS - 2)
            rms_power(2 * HEADS - 1)
            fox_gate(HEADS - 1)

            for b in range(TB):
                pool.wait_ge(S["ln_ask"], b + 1)
                pool.tensor_tensor(rstd[:, 1, b:b + 1], rstd[:, 0, b:b + 1], neg_half[:, 0:1], ALU.pow
                                   ).then_inc(S["ln_got"], 1)
                pool.wait_ge(S["normed"], b + 1)
                pool.dma_start(normed_v[:, b, :], resid[:, b, :]).then_inc(S["normed_stored"], 16)

            step(pool.iota(iota_i, [[1, P]], base=0, channel_multiplier=0))
            step(pool.iota(tok_i, [[P, TB]], base=0, channel_multiplier=1))
            pool.tensor_copy(iota_r, iota_i)
            pool.tensor_copy(tok_id, tok_i)
            pool.memset(one_b, 1.0)
            step(pool.memset(before[:], 1.0))
            step(pool.affine_select(out=before[:], in_=before[:], compare_op=ALU.is_ge, fill=0.0, base=-1,
                                    pattern=[[1, P]], channel_multiplier=-1))
            pool.tensor_scalar(tie_e, iota_r[:, 0:E], -1.0, float(E), ALU.mult, ALU.add)
            step(pool.tensor_scalar(tie_g, iota_r[:, 0:GROUPS], -1.0, float(GROUPS), ALU.mult, ALU.add))
            pool.dma_start(wr, w_router.rearrange("(c p) e -> p c e", p=P)).then_inc(S["wr_landed"], 16)
            pool.dma_start(b_rout, b_router.rearrange("(a e) -> a e", a=1).to_broadcast([P, E])
                           ).then_inc(S["br_landed"], 16)
            pool.memset(small[:], 0.0).then_inc(S["rconst"], 1)

            pool.wait_ge(S["slots_ready"], 1)
            for n, src in enumerate((ln1_g, ln1_b, ln2_g, ln2_b)):
                pool.dma_start(ln_rows[n], src.to_broadcast([P, D])).then_inc(S["lnrow_landed"], 16)

            def gather():
                pool.indirect_dma_start(out=rows_in, out_offset=None, in_=normed_dram,
                                        in_offset=bass.IndirectOffsetOnAxis(ap=row_now[:], axis=0)
                                        ).then_inc(S["gathered"], 16)

            pool.wait_ge(S["idx_now"], 1)
            pool.wait_ge(S["normed_stored"], 16 * TB)
            pool.tensor_copy(row_now[:], row_idx[:, 0:1]).then_inc(S["row_set"], 1)
            pool.wait_ge(S["row_set"], 1)
            gather()
            chunks = pool.value_load(table[0:1, 48:49], min_val=E, max_val=MAX_CHUNKS)
            with pool.Fori(0, chunks) as g:
                pool.wait_ge(S["gathered"], 16 * g + 16)
                pool.wait_ge(S["xg_up"], 2 * g + 2)
                pool.tensor_copy(row_now[:], row_idx[:, bass.ds(g + 1, 1)]).then_inc(S["row_set"], 1)
                pool.wait_ge(S["row_set"], g + 2)
                pool.sem_inc(S["gather_go"], 1)
                gather()

            pool.wait_ge(S["rows_stored"], 16 * chunks + 16)
            pool.sem_inc(S["gather_go"], 1)
            pool.wait_ge(S["x1_ready"], 1)
            for b in range(TB):
                for k in range(2):
                    pool.indirect_dma_start(out=back[k][b], out_offset=None, in_=result_dram,
                                            in_offset=bass.IndirectOffsetOnAxis(
                                                ap=dest[:, k * TB + b:k * TB + b + 1], axis=0)
                                            ).then_inc(back_landed[2 * b + k], 16)
            for b in range(TB):
                pool.wait_ge(S["fin_ask"], b + 1)
                pool.tensor_tensor(rstd[:, 1, b:b + 1], rstd[:, 0, b:b + 1], neg_half[:, 0:1], ALU.pow
                                   ).then_inc(S["fin_got"], 1)

        @block.scalar
        def _(act):
            act.wait_ge(S["cols_ready"], 1)
            act.activation(cond[:, 0, :], cols[:, COL_C:COL_C + KT], ACT.Exp, scale=-1.0
                           ).then_inc(S["cond_exp"], 1)

            act.wait_ge(S["mod_ready"], 2)
            for t in range(0, KT, 2):
                act.wait_ge(S["xT_up"], t + 1)
                act.activation(uT[:, t, :], ps[:, t % 6, :], ACT.Identity,
                               scale=modc[:, SC_A * KT + t:SC_A * KT + t + 1],
                               bias=modc[:, SH_A * KT + t:SH_A * KT + t + 1]).then_inc(S["uT_ready"], 1)

            act.wait_ge(S["f_abs"], 1)
            act.activation(fgt[1], fgt[1], ACT.Exp, scale=-1.0).then_inc(S["act_step"], 1)
            act.wait_ge(S["act_step"], 1)
            act.activation(fgt[1], fgt[1], ACT.Ln, bias=1.0).then_inc(S["f_exp"], 1)

            for u in range(UNITS):
                g, r = divmod(u, 4)
                if u == 4 * SK:
                    act.wait_ge(S["f_ready"], 1)
                act.wait_ge(S["unit_done"], u + 1)
                src = ps[:, u % 4, :]
                if g in (FQ, SQ):
                    ins = act.activation((qf if g == FQ else qs)[:, r, :], src, ACT.Copy, scale=HD ** -0.5)
                elif g in (FK, SK):
                    ins = act.activation((kf if g == FK else ks)[:, r, :], src, ACT.Copy)
                elif g in (FV, SV):
                    if u == 4 * FV:
                        act.wait_ge(S["mod_up"], 6)
                    ins = act.activation((vf if g == FV else vs)[:, r, :], src, ACT.Copy)
                else:
                    ins = act.activation(gate[:, r, :], src, ACT.Exp, scale=-1.0)
                ins.then_inc(S["unit_ready"], 1)

            def exp_clamped(h, n):
                act.wait_ge(S["clamped"], 3 * h + n + 1)
                act.activation(sp_part[n], sp_part[n], ACT.Exp).then_inc(S["sp_exp"], 1)

            def log_one(h, n):
                act.wait_ge(S["sp_exp"], 3 * h + n + 1)
                act.activation(sp_part[n], sp_part[n], ACT.Ln, bias=1.0).then_inc(S["sp_log"], 1)

            def stick(h, n):
                act.wait_ge(S["r_ready"], 3 * h + n + 1)
                if h:
                    act.wait_ge(S["sb_ready"], h)
                act.activation(wT_part[n], z_part[n], ACT.Exp).then_inc(S["stick_ready"], 1)

            def prob_exp(h, b):
                act.wait_ge(S["max_ready"], 4 * h + b + 1)
                if h:
                    act.wait_ge(S["t_up"], 4 * (h - 1) + b + 1)
                act.activation(pr[b], ps[:, b % 2, 0:(b + 1) * P], ACT.Exp, bias=nmax[:, h % 2, b:b + 1],
                               accum_out=lsum[:, h, b:b + 1]).then_inc(S["prob_ready"], 1)

            def square(kind, h):
                ready, done, freed, dst = ((S["fox_ready"], S["fox_sq"], S["rms_ask"], sq_fox),
                                           (S["sb_ready"], S["sb_sq"], S["rms_ask"], sq_sb))[kind]
                act.wait_ge(ready, h + 1)
                if h:
                    act.wait_ge(S["rms_ask"], 2 * h - 1 + kind)
                act.activation(dst, ps[:, (FOX_OUT, SB_OUT)[kind], 0:256], ACT.Square).then_inc(done, 1)

            for h in range(HEADS):
                for n in range(3):
                    exp_clamped(h, n)
                prob_exp(h, 0)
                if h:
                    square(0, h - 1)
                log_one(h, 0)
                prob_exp(h, 1)
                if h:
                    square(1, h - 1)
                log_one(h, 1)
                log_one(h, 2)
                prob_exp(h, 2)
                stick(h, 0)
                prob_exp(h, 3)
                stick(h, 1)
                stick(h, 2)
            square(0, HEADS - 1)
            square(1, HEADS - 1)

            for t in range(0, KT, 2):
                act.wait_ge(S["oT_up"], t + 1)
                act.activation(oT[:, t, :], ps[:, t % 4, :], ACT.Copy,
                               scale=cols[:, COL_ONG + t:COL_ONG + t + 1]).then_inc(S["oT_ready"], 1)
            for b in range(TB):
                act.wait_ge(S["nT_up"], 2 * b + 1)
                for t in range(4):
                    ins = act.activation(u2T[:, t, b * P:(b + 1) * P], ps[:, 0, t * P:(t + 1) * P],
                                         ACT.Identity, scale=in2[:, 0, t:t + 1], bias=in2[:, 1, t:t + 1])
                ins.then_inc(S["u2T_ready"], 1)
            act.wait_ge(S["rcopy_ready"], 1)
            act.activation(prob, prob, ACT.Exp).then_inc(S["rexp"], 1)

            def rowsT_half():
                for t in range(4):
                    ins = act.activation(rowsT[:, t, :], ps[:, 6, t * P:(t + 1) * P], ACT.Identity,
                                         scale=in2[:, 0, t:t + 1], bias=in2[:, 1, t:t + 1])
                ins.then_inc(S["xT_act"], 1)

            act.wait_ge(S["xg_up"], 1)
            rowsT_half()
            act.wait_ge(S["spare_cleared"], 16)
            act.sem_inc(S["rows_stored"], 16)
            act.sem_inc(S["out_act"], 1)
            chunks = act.value_load(table[0:1, 48:49], min_val=E, max_val=MAX_CHUNKS)
            with act.Fori(0, chunks) as g:
                for half in range(2):
                    act.wait_ge(S["gu_up"], 2 * g + half + 1)
                    act.wait_ge(S["h_ready"], 2 * g + half + 1)
                    act.activation(silu, ps[:, 2 * half, :], ACT.Silu).then_inc(S["silu_done"], 1)
                act.wait_ge(S["xg_up"], 2 * g + 3)
                rowsT_half()
                act.wait_ge(S["y2_up"], 2 * g + 1)
                for t in range(4):
                    ins = act.activation(yT[:, t, :], ps[:, 4, t * P:(t + 1) * P], ACT.Copy,
                                         scale=modc[:, G_F * KT + t:G_F * KT + t + 1])
                ins.then_inc(S["y2_act"], 1)
                act.wait_ge(S["yrow_up"], 2 * g + 1)
                act.wait_ge(S["rows_stored"], 16 * g + 16)
                act.activation(rows_out[:, 0:512], ps[:, 6, :], ACT.Copy).then_inc(S["out_act"], 1)
                act.wait_ge(S["out_act"], g + 2)
                act.wait_ge(S["out_dve"], g + 2)
                act.dma_start(result_dram[bass.ds(g * FC, FC), :], rows_out).then_inc(S["rows_stored"], 16)

        @block.tensor
        def _(pe):
            pe.wait_ge(S["consts"], 1)
            pe.wait_ge(S["rows_landed"], 80)
            pe.transpose(ps[:, 7, 0:N_COLS], col_stage[:], ident[0:N_COLS, 0:N_COLS]).then_inc(S["cols_up"], 1)
            pe.wait_ge(S["x_landed"], 16)

            def x_tile(t):
                for b in range(TB):
                    ins = pe.transpose(ps[:, t % 6, b * P:(b + 1) * P], x_tok[:, b, t * P:(t + 1) * P], ident[:])
                ins.then_inc(S["xT_up"], 1)

            def mod_column(pos):
                pe.wait_ge(S["mod_summed"], pos + 1)
                for t in range(KT):
                    ins = pe.matmul(ps[:, 6, pos * KT + t:pos * KT + t + 1], mod_sum(pos)[:, t * P:(t + 1) * P],
                                    one_col[:], start=True, stop=True)
                ins.then_inc(S["mod_up"], 1)

            for t in range(6):
                x_tile(t)
            mod_column(0)
            mod_column(1)
            pe.wait_ge(S["uT_ready"], 1)
            x_tile(6)
            pe.wait_ge(S["uT_ready_d"], 1)
            x_tile(7)
            pe.wait_ge(S["uT_ready"], KT // 2)
            pe.wait_ge(S["uT_ready_d"], KT // 2)
            pe.wait_ge(S["wf_landed"], 16)
            for t in range(KT):
                ins = pe.matmul(ps[0:HEADS, 7, :], w_forget[:, t, :], uT[:, t, :], start=(t == 0), stop=(t == KT - 1))
            ins.then_inc(S["f_up"], 1)

            for u in range(UNITS):
                g, r = divmod(u, 4)
                if r == 0:
                    pe.wait_ge(win_landed[g % 2], 16 * (g // 2 + 1))
                if u == 4 * FV:
                    for pos in range(2, 6):
                        mod_column(pos)
                if u >= 4:
                    pe.wait_ge(S["unit_ready"], u - 3)
                w = win_ring[g % 2]
                for t in range(KT):
                    if g in (FV, SV, GATE):
                        lhs, rhs = uT[:, t, r * P:(r + 1) * P], w[:, t, :]
                    else:
                        lhs, rhs = w[:, t, r * P:(r + 1) * P], uT[:, t, :]
                    ins = pe.matmul(ps[:, u % 4, :], lhs, rhs, start=(t == 0), stop=(t == KT - 1))
                ins.then_inc(S["unit_done"], 1)

            def place(h):
                return slice(HD * (h % 2), HD * (h % 2) + HD), h // 2

            def stick_scores(h, n):
                rows, t = place(h)
                if h:
                    pe.wait_ge(S["stick_ready"], 3 * (h - 1) + n + 1)
                for i in ((2, 3), (1,), (0,))[n]:
                    bank, at = Z_AT[i]
                    pe.matmul(ps[:, bank, at:at + P], ident_b[:], mask_sb[:], start=(i != 3), stop=False,
                              skip_group_check=True)
                    ins = pe.matmul(ps[:, bank, at:at + (TB - i) * P], ks[rows, t, i * P:(i + 1) * P],
                                    qs[rows, t, i * P:T], start=False, stop=True, skip_group_check=True)
                ins.then_inc(S["z_ready"], 1)

            def fox_scores(h, b):
                rows, t = place(h)
                n = 4 * h + b
                if n >= 2:
                    pe.wait_ge(S["prob_ready"], n - 1)
                cols_ = (b + 1) * P
                pe.matmul(ps[:, b % 2, b * P:cols_], ident_b[:], mask_fox[:], start=True, stop=False,
                          skip_group_check=True)
                pe.matmul(ps[:, b % 2, 0:cols_], head_sel[:, h, :], f_split[:, 0:cols_], start=False,
                          stop=False, skip_group_check=True)
                pe.matmul(ps[:, b % 2, 0:cols_], qf[rows, t, b * P:(b + 1) * P], kf[rows, t, 0:cols_],
                          start=False, stop=True, skip_group_check=True).then_inc(S["s_ready"], 1)

            def fox_turn(h, b):
                n = 4 * h + b
                pe.wait_ge(S["prob_ready"], n + 1)
                pe.wait_ge(S["pT_ready"], n)
                for i in range(b + 1):
                    ins = pe.transpose(ps[:, 2, i * P:(i + 1) * P], pr[b][:, i * P:(i + 1) * P], ident[:])
                ins.then_inc(S["t_up"], 1)

            def fox_values(h, b):
                n = 4 * h + b
                pe.wait_ge(S["pT_ready"], n + 1)
                if b == 0 and h:
                    pe.wait_ge(S["fox_freed"], h)
                for i in range(b + 1):
                    ins = pe.matmul(ps[:, FOX_OUT, b * HD:(b + 1) * HD], pT[b][:, i * P:(i + 1) * P],
                                    vf[:, i, h * HD:(h + 1) * HD], start=(i == 0), stop=(i == b))
                if b == TB - 1:
                    ins.then_inc(S["fox_ready"], 1)

            def stick_sums(h, n):
                pe.wait_ge(S["sp_ready"], 3 * h + n + 1)
                for i in ((3, 2), (1,), (0,))[n]:
                    bank, at = Z_AT[i]
                    end = at + (TB - i) * P
                    for j in range(i + 1, TB):
                        pe.matmul(ps[:, bank, at + (j - i) * P:end], neg_ones[:], sp[j], start=False,
                                  stop=False, skip_group_check=True)
                    ins = pe.matmul(ps[:, bank, at:end], neg_tri[:], sp[i], start=False, stop=True,
                                    skip_group_check=True)
                ins.then_inc(S["r_ready"], 1)

            def stick_values(h):
                pe.wait_ge(S["stick_ready"], 3 * h + 3)
                if h:
                    pe.wait_ge(S["sb_freed"], h)
                for b in range(TB):
                    for i in range(b + 1):
                        ins = pe.matmul(ps[:, SB_OUT, b * HD:(b + 1) * HD],
                                        wT[i][:, (b - i) * P:(b - i + 1) * P], vs[:, i, h * HD:(h + 1) * HD],
                                        start=(i == 0), stop=(i == b))
                ins.then_inc(S["sb_ready"], 1)

            pe.wait_ge(S["f_ready"], 1)
            pe.wait_ge(S["mod_ready"], 6)
            for h in range(HEADS):
                for n in range(3):
                    stick_scores(h, n)
                if h == 0:
                    pe.wait_ge(S["unit_ready"], UNITS)
                if h == HEADS - 1:
                    pe.wait_ge(S["z_ready"], 3 * HEADS)
                    pe.nop().then_inc(S["qk_dead"], 1)
                fox_scores(h, 0)
                fox_scores(h, 1)
                if h:
                    stick_values(h - 1)
                fox_turn(h, 0)
                fox_scores(h, 2)
                stick_sums(h, 0)
                fox_turn(h, 1)
                fox_values(h, 0)
                fox_scores(h, 3)
                stick_sums(h, 1)
                fox_turn(h, 2)
                fox_values(h, 1)
                stick_sums(h, 2)
                fox_turn(h, 3)
                fox_values(h, 2)
                fox_values(h, 3)
            stick_values(HEADS - 1)

            pe.wait_ge(S["diag_ready"], 1)
            pe.wait_ge(S["stick_ready"], 3 * HEADS)
            for t in range(KT):
                ins = pe.matmul(ps[:, 4 + t // 4, (t % 4) * P:(t % 4 + 1) * P], neg_ones[:], ga_diag[:, t, :],
                                start=True, stop=True)
            ins.then_inc(S["ga_up"], 1)

            pe.wait_ge(S["fox_gated"], HEADS)
            pe.wait_ge(S["sb_freed"], HEADS)
            for t in range(KT):
                if t >= 4:
                    pe.wait_ge(S["oT_ready"] if t % 2 == 0 else S["oT_ready_d"], (t - 4) // 2 + 1)
                for b in range(TB):
                    ins = pe.transpose(ps[:, t % 4, b * P:(b + 1) * P], o_tok[:, b, t * P:(t + 1) * P], ident[:])
                ins.then_inc(S["oT_up"], 1)
            pe.wait_ge(S["oT_ready"], KT // 2)
            pe.wait_ge(S["oT_ready_d"], KT // 2)
            pe.wait_ge(S["wout_landed"], 16)

            def project_out(b):
                bank = 6 - 2 * (b % 2)
                if b == 1:
                    pe.wait_ge(S["ga_ready"], 1)
                if b >= 2:
                    pe.wait_ge(S["ln_freed"], b - 1)
                for half in range(2):
                    for t in range(KT):
                        ins = pe.matmul(ps[:, bank + half, :], oT[:, t, b * P:(b + 1) * P],
                                        wout[:, t, half * 512:(half + 1) * 512], start=(t == 0), stop=(t == KT - 1))
                ins.then_inc(S["y_up"], 1)

            def turn_normed(b):
                pe.wait_ge(S["normed"], b + 1)
                for half in range(2):
                    if b:
                        pe.wait_ge((S["u2T_ready"], S["u2T_ready_d"])[half], b)
                    for t in range(4):
                        ins = pe.transpose(ps[:, half, t * P:(t + 1) * P],
                                           resid[:, b, (4 * half + t) * P:(4 * half + t + 1) * P], ident[:])
                    ins.then_inc(S["nT_up"], 1)

            def route(b):
                pe.wait_ge(S["u2T_ready"], b + 1)
                pe.wait_ge(S["u2T_ready_d"], b + 1)
                if b == 0:
                    pe.wait_ge(S["wr_landed"], 16)
                for t in range(KT):
                    ins = pe.matmul(ps[:, 2, b * E:(b + 1) * E], u2T[:, t, b * P:(b + 1) * P], wr[:, t, :],
                                    start=(t == 0), stop=(t == KT - 1))
                ins.then_inc(S["logits_up"], 1)

            project_out(0)
            project_out(1)
            turn_normed(0)
            project_out(2)
            turn_normed(1)
            project_out(3)
            turn_normed(2)
            turn_normed(3)
            for b in range(TB):
                route(b)

            pe.wait_ge(S["routed_hot"], 1)
            for b in range(TB):
                for prev in range(b):
                    pe.matmul(ps[:, 3, b * E:(b + 1) * E], one_b, chosen[:, prev, :], start=(prev == 0), stop=False)
                pe.matmul(ps[:, 3, b * E:(b + 1) * E], before[:], chosen[:, b, :], start=(b == 0), stop=True)
            for b in range(TB):
                ins = pe.matmul(ps[:, 3, TB * E:TB * E + E], one_b, chosen[:, b, :], start=(b == 0), stop=(b == TB - 1))
            ins.then_inc(S["rank_up"], 1)
            pe.wait_ge(S["slots_ready"], 1)
            for n in range(2 * TB):
                ins = pe.matmul(ps[:, 3, 128:128 + MAX_CHUNKS + 1], slot_hot[:, n, :], chunk_tok[:, n, :],
                                start=(n == 0), stop=(n == 2 * TB - 1))
            ins.then_inc(S["idx_up"], 1)

            def turn_rows(frees=False):
                for half in range(2):
                    for t in range(4):
                        ins = pe.transpose(ps[:, 6 + half, t * P:(t + 1) * P],
                                           rows_in[:, (4 * half + t) * P:(4 * half + t + 1) * P], ident[:])
                        if frees and half == 0 and t == 0:
                            ins.then_inc(gu_free, 1)
                    ins.then_inc(S["xg_up"], 1)

            def run_chunk(g, e, width, last):
                pe.wait_ge(S["xT_act"], g + 1)
                pe.wait_ge(S["xT_dve"], g + 1)
                for piece in range(4):
                    pe.wait_ge(gu_landed[piece], 32 * e + 32)
                    half = piece // 2
                    for f in (2 * piece, 2 * piece + 1):
                        at = (f % 4) * P
                        for w, bank in ((gate_w, 2 * half), (up_w, 2 * half + 1)):
                            for t in range(KT):
                                ins = pe.matmul(ps[:, bank, at:at + width], w[:, t, f * P:(f + 1) * P],
                                                rowsT[:, t, 0:width], start=(t == 0), stop=(t == KT - 1))
                                if last and piece and f % 2 == 0 and w is gate_w and t == 0:
                                    ins.then_inc(gu_free, 1)
                    if piece % 2:
                        ins.then_inc(S["gu_up"], 1)
                pe.wait_ge(S["gathered"], 16 * g + 32)
                pe.wait_ge(S["out_act"], g + 1)
                pe.wait_ge(S["out_dve"], g + 1)
                turn_rows(frees=last)
                for half in range(2):
                    pe.wait_ge(dn_landed[half], 16 * e + 16)
                    pe.wait_ge(S["h_ready"], 2 * g + half + 2)
                    for d in range(KT):
                        for f in range(4 * half, 4 * half + 4):
                            ins = pe.matmul(ps[:, 4 + d // 4, (d % 4) * P:(d % 4) * P + width],
                                            down_w[:, f, d * P:(d + 1) * P], hT[:, f, 0:width],
                                            start=(f == 0 and d % 4 == 0), stop=(f == KT - 1),
                                            skip_group_check=True)
                        if half and d % 4 == 3:
                            ins.then_inc(S["y2_up"], 1)
                    if last and not half:
                        ins.then_inc(S["down_free"], 1)
                for half in range(2):
                    pe.wait_ge((S["y2_act"], S["y2_dve"])[half], g + 1)
                    pe.wait_ge((S["xT_act"], S["xT_dve"])[half], g + 2)
                    for t in range(4):
                        ins = pe.transpose(ps[:, 6 + half, t * P:(t + 1) * P], yT[:, 4 * half + t, :], ident[:])
                        if last and half == 0 and t == 0:
                            ins.then_inc(S["down_free"], 1)
                    ins.then_inc(S["yrow_up"], 1)

            pe.wait_ge(S["gathered"], 16)
            turn_rows()
            pe.wait_ge(S["tables_ready"], 1)
            with pe.Fori(0, E) as e:
                more = pe.value_load(table[0:1, bass.ds(e, 1)], min_val=0, max_val=3)
                base = pe.value_load(table[0:1, bass.ds(e + 16, 1)], min_val=0, max_val=MAX_CHUNKS)
                rest = pe.value_load(table[0:1, bass.ds(e + 32, 1)], min_val=0, max_val=FC)
                with pe.If(more > 0):
                    with pe.Fori(0, more) as j:
                        run_chunk(base + j, e, FC, False)
                final = pe.snap(base + more)

                def narrowest(n):
                    if n == len(WIDTHS) - 1:
                        run_chunk(final, e, WIDTHS[n], True)
                        return
                    with pe.If(rest <= WIDTHS[n]):
                        run_chunk(final, e, WIDTHS[n], True)
                    with pe.Else():
                        narrowest(n + 1)

                narrowest(0)

        @block.vector
        def _(dve):
            steps = [0]

            def step(ins):
                steps[0] += 1
                ins.then_inc(S["dve_step"], 1)
                dve.wait_ge(S["dve_step"], steps[0])

            dve.wait_ge(S["cols_up"], 1)
            step(dve.tensor_copy(cols[:], ps[:, 7, 0:N_COLS]))
            dve.nop().then_inc(S["cols_ready"], 1)
            dve.wait_ge(S["cond_exp"], 1)
            step(dve.tensor_scalar(cond[:, 1, :], cond[:, 0, :], 1.0, None, ALU.add))
            step(dve.reciprocal(cond[:, 2, :], cond[:, 1, :]))
            step(dve.tensor_tensor(cond[:, 0, :], cond[:, 2, :], cols[:, COL_C:COL_C + KT], ALU.mult))

            def mod_segment(pos):
                home, acc = mod_home[pos % 3], mod_sum(pos)
                for t in range(KT):
                    if t % 4 == 0:
                        dve.wait_ge(mod_landed[2 * (pos % 3) + t // 4], 16 * (pos // 3 + 1))
                    if t == 0:
                        ins = dve.tensor_scalar(acc, home[:, 0, :], cond[:, 0, 0:1], None, ALU.mult)
                    else:
                        ins = dve.scalar_tensor_tensor(out=acc, in0=home[:, t, :], scalar=cond[:, 0, t:t + 1],
                                                       in1=acc, op0=ALU.mult, op1=ALU.add)
                    if t < KT - 1:
                        step(ins)
                ins.then_inc(S["mod_summed"], 1)

            def mod_column(pos):
                seg = MOD_ORDER[pos]
                cs = slice(seg * KT, (seg + 1) * KT)
                dve.scalar_tensor_tensor(out=modc[:, cs], in0=ps[:, 6, pos * KT:(pos + 1) * KT],
                                         scalar=0.0 if seg in (SH_A, SH_F) else 1.0, in1=cols[:, cs],
                                         op0=ALU.add, op1=ALU.add).then_inc(S["mod_ready"], 1)

            mod_segment(0)
            mod_segment(1)
            dve.wait_ge(S["mod_up"], 2)
            mod_column(0)
            mod_column(1)
            dve.wait_ge(S["mod_ready"], 2)
            for t in range(1, KT, 2):
                dve.wait_ge(S["xT_up"], t + 1)
                dve.tensor_scalar(uT[:, t, :], ps[:, t % 6, :], modc[:, SC_A * KT + t:SC_A * KT + t + 1],
                                  modc[:, SH_A * KT + t:SH_A * KT + t + 1], ALU.mult, ALU.add
                                  ).then_inc(S["uT_ready_d"], 1)

            dve.wait_ge(S["f_up"], 1)
            dve.wait_ge(S["bf_landed"], 16)
            step(dve.tensor_scalar(fgt[0], ps[0:HEADS, 7, :], bf_col[:, 0:1], None, ALU.add))
            dve.scalar_tensor_tensor(out=fgt[1], in0=fgt[0], scalar=-1.0, in1=fgt[0], op0=ALU.mult, op1=ALU.max
                                     ).then_inc(S["f_abs"], 1)
            step(dve.tensor_scalar(fgt[0], fgt[0], 0.0, None, ALU.min))
            dve.wait_ge(S["f_exp"], 1)
            step(dve.tensor_tensor(fgt[2], fgt[1], fgt[0], ALU.subtract))
            step(dve.memset(fgt[1], 1.0))
            step(dve.tensor_tensor_scan(fgt[3], fgt[1], fgt[2], 0.0, ALU.mult, ALU.add))
            cur, nxt = fgt[3], fgt[0]
            for part in range(3):
                dst = f_split[32 * part:32 * part + HEADS, :]
                if part == 2:
                    dve.tensor_copy(dst, cur).then_inc(S["f_ready"], 1)
                else:
                    step(dve.tensor_copy(dst, cur))
                    step(dve.tensor_copy(fgt[1], dst))
                    step(dve.tensor_tensor(nxt, cur, fgt[1], ALU.subtract))
                    cur, nxt = nxt, fgt[2]

            for pos in range(2, 6):
                mod_segment(pos)
            dve.wait_ge(S["mod_up"], 6)
            for pos in range(2, 6):
                mod_column(pos)
            dve.wait_ge(S["mod_ready"], 6)
            g_c, b_c = cols[:, COL_LNG:COL_LNG + KT], cols[:, COL_LNB:COL_LNB + KT]
            sc_c, sh_c = modc[:, SC_F * KT:(SC_F + 1) * KT], modc[:, SH_F * KT:(SH_F + 1) * KT]
            dve.tensor_tensor(in2[:, 0, :], g_c, sc_c, ALU.mult)
            step(dve.tensor_tensor(in2[:, 1, :], b_c, sc_c, ALU.mult))
            step(dve.tensor_tensor(in2[:, 1, :], in2[:, 1, :], sh_c, ALU.add))
            dve.wait_ge(S["unit_ready"], UNITS)
            step(dve.tensor_scalar(RG[:, :], RG[:, :], 1.0, None, ALU.add))
            dve.reciprocal(RG[:, :], RG[:, :]).then_inc(S["gate_ready"], 1)
            for t in range(KT):
                ins = dve.tensor_scalar(ga_diag[:, t, :], ident[:], modc[:, G_A * KT + t:G_A * KT + t + 1], -1.0,
                                        ALU.mult, ALU.mult)
            ins.then_inc(S["diag_ready"], 1)

            def clamp(h, n):
                dve.wait_ge(S["z_ready"], 3 * h + n + 1)
                dve.tensor_scalar(sp_part[n], z_part[n], BIG_Z, None, ALU.min).then_inc(S["clamped"], 1)

            def softplus(h, n):
                dve.wait_ge(S["sp_log"], 3 * h + n + 1)
                dve.tensor_tensor(sp_part[n], z_part[n], sp_part[n], ALU.max).then_inc(S["sp_ready"], 1)

            def row_max(h, b):
                dve.wait_ge(S["s_ready"], 4 * h + b + 1)
                dve.tensor_reduce(nmax[:, h % 2, b:b + 1], ps[:, b % 2, 0:(b + 1) * P], AX_X, ALU.max,
                                  negate=True).then_inc(S["max_ready"], 1)

            def turned(h, b):
                dve.wait_ge(S["t_up"], 4 * h + b + 1)
                dve.tensor_copy(pT[b], ps[:, 2, 0:(b + 1) * P]).then_inc(S["pT_ready"], 1)

            def rms_sum(kind, h):
                n = 2 * h + kind
                t = rms_t[:, n % 2]
                dve.wait_ge(S["fox_sq"] if kind == 0 else S["sb_sq"], h + 1)
                src = (sq_fox, sq_sb)[kind].rearrange("p (b n) -> p b n", b=TB)
                step(dve.tensor_reduce(t[:, 0, :], src, AX_X, ALU.add))
                if kind == 0:
                    l = lsum[:, h, :]
                    step(dve.scalar_tensor_tensor(out=lsum[:, h, :], in0=l, scalar=RMS_EPS, in1=l, op0=ALU.mult,
                                                  op1=ALU.mult))
                    dve.scalar_tensor_tensor(out=t[:, 1, :], in0=t[:, 0, :], scalar=1.0 / HD, in1=l,
                                             op0=ALU.mult, op1=ALU.add).then_inc(S["rms_ask"], 1)
                else:
                    dve.tensor_scalar(t[:, 1, :], t[:, 0, :], 1.0 / HD, RMS_EPS, ALU.mult, ALU.add
                                      ).then_inc(S["rms_ask"], 1)

            def rms_scale(kind, h):
                n = 2 * h + kind
                dve.wait_ge(S["rms_got"], n + 1)
                src = ps[:, (FOX_OUT, SB_OUT)[kind], 0:256].rearrange("p (b n) -> p b n", b=TB)
                dst = o_tok[:, :, kind * DG + h * HD:kind * DG + (h + 1) * HD]
                dve.tensor_tensor(dst, src, rms_t[:, n % 2, 2, :].unsqueeze(2).broadcast_to([P, TB, HD]), ALU.mult
                                  ).then_inc(S["fox_freed"] if kind == 0 else S["sb_freed"], 1)

            for h in range(HEADS):
                for n in range(3):
                    clamp(h, n)
                row_max(h, 0)
                row_max(h, 1)
                if h:
                    rms_sum(0, h - 1)
                turned(h, 0)
                softplus(h, 0)
                if h:
                    rms_scale(0, h - 1)
                row_max(h, 2)
                turned(h, 1)
                if h:
                    rms_sum(1, h - 1)
                softplus(h, 1)
                softplus(h, 2)
                row_max(h, 3)
                if h:
                    rms_scale(1, h - 1)
                turned(h, 2)
                turned(h, 3)
            for kind in range(2):
                rms_sum(kind, HEADS - 1)
                rms_scale(kind, HEADS - 1)

            dve.wait_ge(S["ga_up"], 1)
            dve.tensor_copy(ga_row, ps[:, 4:6, :].rearrange("p a n -> p (a n)")).then_inc(S["ga_ready"], 1)
            for t in range(1, KT, 2):
                dve.wait_ge(S["oT_up"], t + 1)
                dve.tensor_scalar(oT[:, t, :], ps[:, t % 4, :], cols[:, COL_ONG + t:COL_ONG + t + 1], None,
                                  ALU.mult).then_inc(S["oT_ready_d"], 1)

            def normalise(b, ask, got):
                for half in range(2):
                    ins = dve.bn_stats(stats[:, half, :], resid[:, b, half * 512:(half + 1) * 512])
                step(ins)
                step(dve.bn_aggr(mv[:, b, :], stats[:].rearrange("p a n -> p (a n)")))
                dve.tensor_scalar(rstd[:, 0, b:b + 1], mv[:, b, 1:2], LN_EPS, None, ALU.add).then_inc(ask, 1)
                dve.wait_ge(got, b + 1)

            def first_norm(b):
                bank = 6 - 2 * (b % 2)
                dve.wait_ge(S["y_up"], b + 1)
                ins = dve.tensor_tensor(ln_tmp, ps[:, bank:bank + 2, :].rearrange("p a n -> p (a n)"), ga_row,
                                        ALU.mult)
                ins.then_inc(S["ln_freed"], 1)
                dve.wait_ge(S["ln_freed"], b + 1)
                if b == 0:
                    dve.wait_ge(S["xr_landed"], 16)
                step(dve.scalar_tensor_tensor(out=resid[:, b, :], in0=resid[:, b, :], scalar=ALPHA, in1=ln_tmp,
                                              op0=ALU.mult, op1=ALU.add))
                normalise(b, S["ln_ask"], S["ln_got"])
                dve.tensor_scalar(resid[:, b, :], resid[:, b, :], mv[:, b, 0:1], rstd[:, 1, b:b + 1],
                                  ALU.subtract, ALU.mult).then_inc(S["normed"], 1)

            def u2_half(b):
                dve.wait_ge(S["nT_up"], 2 * b + 2)
                for t in range(4, KT):
                    ins = dve.tensor_scalar(u2T[:, t, b * P:(b + 1) * P], ps[:, 1, (t - 4) * P:(t - 3) * P],
                                            in2[:, 0, t:t + 1], in2[:, 1, t:t + 1], ALU.mult, ALU.add)
                ins.then_inc(S["u2T_ready_d"], 1)

            dve.wait_ge(S["ga_ready"], 1)
            first_norm(0)
            for b in range(1, TB):
                first_norm(b)
                u2_half(b - 1)
            u2_half(TB - 1)

            dve.wait_ge(S["logits_up"], TB)
            dve.wait_ge(S["rconst"], 1)
            dve.wait_ge(S["br_landed"], 16)

            def v3(a, s=E):
                return a.rearrange("p (b e) -> p b e", e=s)

            def wide(a, s=E):
                return a.unsqueeze(2).broadcast_to([P, a.shape[1], s])

            def over_b(a):
                return a.unsqueeze(1).broadcast_to([P, TB, a.shape[1]])

            m4, n16 = rout[:, 0:TB], rout[:, 16:16 + TB * GROUPS]
            logits = ps[:, 2, 0:TB * E]
            step(dve.tensor_reduce(m4, v3(logits), AX_X, ALU.max))
            dve.tensor_tensor(v3(prob), v3(logits), wide(m4), ALU.subtract).then_inc(S["rcopy_ready"], 1)
            dve.wait_ge(S["rexp"], 1)
            step(dve.tensor_reduce(m4, v3(prob), AX_X, ALU.add))
            step(dve.reciprocal(rout[:, 4:8], m4))
            step(dve.tensor_tensor(v3(prob), v3(prob), wide(rout[:, 4:8]), ALU.mult))
            step(dve.tensor_tensor(v3(sel), v3(prob), over_b(b_rout), ALU.add))
            s4 = v3(sel, EPG)
            n = TB * GROUPS
            dve.tensor_tensor(pair6[:, :, 0:3], s4[:, :, 1:4], s4[:, :, 0:1].broadcast_to([P, n, 3]), ALU.add)
            dve.tensor_tensor(pair6[:, :, 3:5], s4[:, :, 2:4], s4[:, :, 1:2].broadcast_to([P, n, 2]), ALU.add)
            step(dve.tensor_tensor(pair6[:, :, 5:6], s4[:, :, 3:4], s4[:, :, 2:3], ALU.add))
            step(dve.tensor_reduce(gscore, pair6, AX_X, ALU.max))

            def first_largest(dst, vals, tie, size):
                step(dve.tensor_reduce(m4, v3(vals, size), AX_X, ALU.max))
                step(dve.tensor_tensor(v3(dst, size), v3(vals, size), wide(m4, size), ALU.is_equal))
                step(dve.tensor_tensor(v3(dst, size), v3(dst, size), over_b(tie), ALU.mult))
                step(dve.tensor_reduce(m4, v3(dst, size), AX_X, ALU.max))
                step(dve.tensor_tensor(v3(dst, size), v3(dst, size), wide(m4, size), ALU.is_equal))

            first_largest(ghot, gscore, tie_g, GROUPS)
            step(dve.tensor_scalar(gtie, ghot, -NEG, NEG, ALU.mult, ALU.add))
            step(dve.tensor_tensor(v3(selm, EPG), s4, wide(ghot, EPG), ALU.mult))
            step(dve.tensor_tensor(v3(selm, EPG), v3(selm, EPG), wide(gtie, EPG), ALU.add))
            first_largest(hot[0], selm, tie_e, E)
            step(dve.scalar_tensor_tensor(out=selm, in0=hot[0], scalar=2.0 * NEG, in1=selm, op0=ALU.mult,
                                          op1=ALU.add))
            first_largest(hot[1], selm, tie_e, E)
            dve.tensor_tensor(chosen, v3(hot[0]), v3(hot[1]), ALU.add).then_inc(S["routed_hot"], 1)
            weights = small[:, 16:16 + 2 * TB]
            for k in range(2):
                step(dve.tensor_tensor(score, hot[k], prob, ALU.mult))
                step(dve.tensor_reduce(rout[:, 32 + 4 * k:36 + 4 * k], v3(score), AX_X, ALU.add))
            step(dve.tensor_tensor(m4, rout[:, 32:36], rout[:, 36:40], ALU.add))
            step(dve.reciprocal(rout[:, 4:8], m4))
            for k in range(2):
                dve.tensor_tensor(weights[:, k * TB:(k + 1) * TB], rout[:, 32 + 4 * k:36 + 4 * k],
                                  rout[:, 4:8], ALU.mult)

            def overflow(dst, src):
                op = ALU.is_ge if dst is where[1] else ALU.is_gt
                step(dve.tensor_scalar(dst, src, float(FC), None, op))
                for k in (2, 3):
                    step(dve.scalar_tensor_tensor(out=dst, in0=src, scalar=float(k * FC), in1=dst, op0=op,
                                                  op1=ALU.add))

            dve.wait_ge(S["rank_up"], 1)
            count, more, base, upto = (rout[:, 64 + 16 * n:80 + 16 * n] for n in range(4))
            rest, one16 = rout[:, 128:144], rout[:, 144:160]
            rank = score
            dve.memset(one16, 1.0)
            dve.tensor_copy(rank, ps[:, 3, 0:TB * E])
            step(dve.tensor_copy(count, ps[:, 3, TB * E:TB * E + E]))
            overflow(more, count)
            step(dve.tensor_scalar(base, more, 1.0, None, ALU.add))
            step(dve.tensor_tensor_scan(upto, one16, base, 0.0, ALU.mult, ALU.add))
            dve.tensor_tensor(base, upto, base, ALU.subtract)
            step(dve.scalar_tensor_tensor(out=rest, in0=more, scalar=-float(FC), in1=count, op0=ALU.mult,
                                          op1=ALU.add))
            dve.tensor_copy(table[0:1, 0:16], more[0:1, :])
            dve.tensor_copy(table[0:1, 16:32], base[0:1, :])
            dve.tensor_copy(table[0:1, 32:48], rest[0:1, :])
            step(dve.tensor_copy(table[0:1, 48:49], upto[0:1, 15:16]))
            overflow(where[1], rank)
            step(dve.scalar_tensor_tensor(out=where[0], in0=where[1], scalar=-float(FC), in1=rank, op0=ALU.mult,
                                          op1=ALU.add))
            step(dve.tensor_tensor(v3(where[1]), v3(where[1]), over_b(base), ALU.add))
            pos8, chunk8, dest8 = rout[:, 160:168], rout[:, 168:176], rout[:, 176:184]
            for k in range(2):
                for dst, val in ((pos8, where[0]), (chunk8, where[1])):
                    step(dve.tensor_tensor(selm, hot[k], val, ALU.mult))
                    step(dve.tensor_reduce(dst[:, k * TB:(k + 1) * TB], v3(selm), AX_X, ALU.add))
            dve.tensor_tensor(slot_hot, iota_r.unsqueeze(1).broadcast_to([P, 2 * TB, P]), wide(pos8, P), ALU.is_equal)
            nch = MAX_CHUNKS + 1
            step(dve.tensor_tensor(chunk_tok, iota_r[:, 0:nch].unsqueeze(1).broadcast_to([P, 2 * TB, nch]),
                                   wide(chunk8, nch), ALU.is_equal))
            for k in range(2):
                ins = dve.tensor_tensor(chunk_tok[:, k * TB:(k + 1) * TB, :], chunk_tok[:, k * TB:(k + 1) * TB, :],
                                        wide(tok_id, nch), ALU.mult)
            step(ins)
            step(dve.scalar_tensor_tensor(out=dest8, in0=chunk8, scalar=float(FC), in1=pos8, op0=ALU.mult,
                                          op1=ALU.add))
            step(dve.tensor_copy(dest[:], dest8))
            dve.nop().then_inc(S["slots_ready"], 1)
            dve.wait_ge(S["idx_up"], 1)
            step(dve.tensor_copy(row_idx[:], ps[:, 3, 128:128 + nch]))
            dve.nop().then_inc(S["idx_now"], 1)
            dve.nop().then_inc(S["tables_ready"], 1)

            def rowsT_half():
                for t in range(4, KT):
                    ins = dve.tensor_scalar(rowsT[:, t, :], ps[:, 7, (t - 4) * P:(t - 3) * P], in2[:, 0, t:t + 1],
                                            in2[:, 1, t:t + 1], ALU.mult, ALU.add)
                ins.then_inc(S["xT_dve"], 1)

            dve.wait_ge(S["xg_up"], 2)
            rowsT_half()
            dve.wait_ge(S["lnrow_landed"], 64)
            for b in range(TB):
                step(dve.scalar_tensor_tensor(out=resid[:, b, :], in0=resid[:, b, :], scalar=ALPHA,
                                              in1=ln_rows[0], op0=ALU.mult, op1=ALU.mult))
                step(dve.scalar_tensor_tensor(out=resid[:, b, :], in0=ln_rows[1], scalar=ALPHA,
                                              in1=resid[:, b, :], op0=ALU.mult, op1=ALU.add))
            dve.nop().then_inc(S["x1_ready"], 1)

            dve.sem_inc(S["out_dve"], 1)
            dve.sem_inc(S["h_ready"], 1)
            chunks = dve.value_load(table[0:1, 48:49], min_val=E, max_val=MAX_CHUNKS)
            with dve.Fori(0, chunks) as g:
                for half in range(2):
                    dve.wait_ge(S["silu_done"], 2 * g + half + 1)
                    dve.tensor_tensor(hT[:, 4 * half:4 * half + 4, :].rearrange("p c r -> p (c r)"), silu,
                                      ps[:, 2 * half + 1, :], ALU.mult).then_inc(S["h_ready"], 1)
                dve.wait_ge(S["xg_up"], 2 * g + 4)
                rowsT_half()
                dve.wait_ge(S["y2_up"], 2 * g + 2)
                gf = modc[:, G_F * KT + 4:G_F * KT + 8]
                dve.tensor_tensor(yT[:, 4:8, :], ps[:, 5, :].rearrange("p (c r) -> p c r", c=4), wide(gf, P), ALU.mult
                                  ).then_inc(S["y2_dve"], 1)
                dve.wait_ge(S["yrow_up"], 2 * g + 2)
                dve.wait_ge(S["rows_stored"], 16 * g + 16)
                dve.tensor_copy(rows_out[:, 512:1024], ps[:, 7, :]).then_inc(S["out_dve"], 1)

            def combine(b):
                for k in range(2):
                    dve.wait_ge(back_landed[2 * b + k], 16)
                    step(dve.scalar_tensor_tensor(out=resid[:, b, :], in0=back[k][b],
                                                  scalar=weights[:, k * TB + b:k * TB + b + 1], in1=resid[:, b, :],
                                                  op0=ALU.mult, op1=ALU.add))
                normalise(b, S["fin_ask"], S["fin_got"])
                step(dve.tensor_scalar(back[0][b], resid[:, b, :], mv[:, b, 0:1], rstd[:, 1, b:b + 1],
                                       ALU.subtract, ALU.mult))
                step(dve.tensor_tensor(back[0][b], back[0][b], ln_rows[2], ALU.mult))
                dve.tensor_tensor(back[0][b], back[0][b], ln_rows[3], ALU.add).then_inc(S["fin_done"], 1)

            for b in range(TB):
                combine(b)


_INS = ['x', 'c', 'w_mod', 'b_mod', 'w_in', 'b_forget', 'out_norm_g', 'w_out', 'ln1_g', 'ln1_b',
        'w_router', 'b_router', 'w_gate', 'w_up', 'w_down', 'ln2_g', 'ln2_b']


def kernel(**inputs):
    import numpy as _np
    import concourse.bacc as _bacc
    from concourse import mybir as _mybir
    from concourse.bass_utils import run_bass_kernel_spmd as _run

    nc = _bacc.Bacc("TRN2", target_bir_lowering=False, num_devices=1)
    arrays, args = {}, []
    for name in _INS:
        a = _np.ascontiguousarray(inputs[name])
        arrays[f"in_{name}_dram"] = a
        args.append(nc.dram_tensor(f"in_{name}_dram", a.shape, _mybir.dt.from_np(a.dtype), kind="ExternalInput").ap())
    out = nc.dram_tensor("out_0_dram", (1, T, D), _mybir.dt.float32, kind="ExternalOutput").ap()
    build(nc, *args, out)
    r = _run(nc, [arrays], core_ids=[0])
    return r.results[0]["out_0_dram"]
```

```python
from contextlib import ExitStack

import concourse.bass as bass
import concourse.mybir as mybir
from concourse.alu_op_type import AluOpType as ALU

ACT = mybir.ActivationFunctionType
AX_X = mybir.AxisListType.X
F32 = mybir.dt.float32
F32R = mybir.dt.float32r
BF16 = mybir.dt.bfloat16
I32 = mybir.dt.int32

P = 128
D = 1024
T = 512
KT = D // P
TB = T // P
HD = 64
HEADS = 8
DG = HEADS * HD
E = 16
EPG = 4
GROUPS = E // EPG
FC = P
MAX_CHUNKS = E + (2 * T - 1) // FC
ALPHA = 2.0 ** 0.25
LN_EPS = 1e-5
RMS_EPS = 1e-6
NEG = -1e30
BIG_Z = 40.0
PIECE = 2 * D
RAW_SLOTS = 6
SPLIT_SLOTS = 4
GU_PIECES = 8
DN_PIECES = 4
CHUNK_PIECES = GU_PIECES + DN_PIECES

SB_OFF = 4 * DG + HEADS
GROUP_COLS = [0, DG, SB_OFF, SB_OFF + DG, 2 * DG, SB_OFF + 2 * DG, 3 * DG]
FQ, FK, SQ, SK, FV, SV, GATE = range(7)
UNITS = 4 * len(GROUP_COLS)
WIN_PIECES = 2 * len(GROUP_COLS)

SH_A, SC_A, G_A, SH_F, SC_F, G_F = range(6)
MOD_ORDER = [SC_A, SH_A, G_A, SH_F, SC_F, G_F]

COL_BMOD, COL_C, COL_LNG, COL_LNB, COL_ONG, N_COLS = 0, 48, 56, 64, 72, 80
G_COL = MAX_CHUNKS + 1
U2_SCALE, U2_SHIFT, N_ROWS = 6, 7, 8


def front_stream():
    order = [("mod", n) for n in range(8)] + [("win", 0), ("win", 1)]
    for n in range(2, WIN_PIECES):
        mods = range(2 * n + 4, min(2 * n + 6, 24))
        order += [("mod", m) for m in mods] + [("win", n)]
    return order


FRONT = front_stream()
MOD_BEFORE = {2 * pos - 1: pos for pos in range(2, 6)}
FRONT_AT = {item: n for n, item in enumerate(FRONT)}


def build(nc, x, c, w_mod, b_mod, w_in, b_forget, out_norm_g, w_out, ln1_g, ln1_b,
          w_router, b_router, w_gate, w_up, w_down, ln2_g, ln2_b, out):
    u2_dram = nc.dram_tensor("u2_rows", [T, D], F32).ap()
    mod_dram = nc.dram_tensor("mod_rows", [N_ROWS, D], F32).ap()
    result_dram = nc.dram_tensor("expert_rows", [(1 + MAX_CHUNKS) * FC, D], F32).ap()

    with ExitStack() as ctx:
        def sb(name, shape, dt=F32):
            return ctx.enter_context(nc.sbuf_tensor(name, shape, dt))

        def sem(name):
            return ctx.enter_context(nc.semaphore(name))

        sizes = dict(RAW=RAW_SLOTS * PIECE, SPLIT=SPLIT_SLOTS * 2 * PIECE, RQ=16 * T, RV=8 * T, RA=KT * T,
                     RE=KT * T, RG=4 * T)
        with ExitStack() as first_view:
            M = {name: first_view.enter_context(nc.sbuf_tensor(f"{name}_f32", [P, n], F32))
                 for name, n in sizes.items()}
        MR = {name: sb(f"{name}_f32r", [P, n], F32R) for name, n in sizes.items()}

        def region(view, name):
            return view[name][:, :]

        RAW, RQ, RV, RA, RG = (region(M, n) for n in ("RAW", "RQ", "RV", "RA", "RG"))
        RB = RAW

        def raw_piece(slot):
            return RAW[:, slot * PIECE:(slot + 1) * PIECE]

        def split_piece(slot, part):
            at = (2 * slot + part) * PIECE
            return region(MR, "SPLIT")[:, at:at + PIECE]

        def as_f32(a):
            return a.bitcast(F32)

        def tiles(a, c=KT):
            return a.rearrange("p (c t) -> p c t", c=c)

        uT_split = [tiles(region(MR, n)) for n in ("RA", "RE")]
        oT_split = [tiles(region(MR, "RE")), tiles(region(MR, "RQ")[:, 0:4096])]
        o_tok = tiles(RA, TB)
        u2T = tiles(RA)
        x_tok = tiles(RQ[:, 0:4096], TB)
        uT = tiles(RQ[:, 4096:8192])
        qf, kf, qs, ks = (tiles(RQ[:, n * 2048:(n + 1) * 2048], 4) for n in range(4))
        resid = tiles(RQ[:, 4096:8192], TB)
        vf, vs = (tiles(RV[:, n * 2048:(n + 1) * 2048], TB) for n in range(2))
        gate = tiles(RG[:, :], TB)

        def mod_sum(pos):
            return RG[:, pos % 2 * D:(pos % 2 + 1) * D]

        fgt = [RQ[0:HEADS, 6144 + n * T:6144 + (n + 1) * T] for n in range(4)]

        def packed(base, width):
            offs = [base + sum(width(j) for j in range(i)) for i in range(TB)]
            return [RB[:, offs[i]:offs[i] + width(i)] for i in range(TB)]

        sp = packed(0, lambda i: (TB - i) * P)
        wT = packed(1280, lambda i: (TB - i) * P)
        pr = packed(2560, lambda b: (b + 1) * P)
        pT = packed(3840, lambda b: (b + 1) * P)
        def span(n):
            return slice(0, 3 * P) if n == 0 else slice(0, (n + 2) * P)

        sp_part, wT_part, z_part = ([], [], [])
        for n in range(3):
            at = (896, 512, 0)[n]
            sp_part.append(RB[:, at:at + span(n).stop])
            wT_part.append(RB[:, 1280 + at:1280 + at + span(n).stop])
        sq_fox = RB[:, 5120:5376]
        sq_sb = RB[:, 5376:5632]
        zeros = RB[:, 5632:6144]
        ga_row = RB[:, 6144:7168]
        mod_rows = RB[0:N_ROWS * KT, 7168:7168 + P]
        ln_tmp = RV[:, 0:D]
        u2_rows = [RAW[:, 8192 + n * D:8192 + (n + 1) * D] for n in range(2)]
        u2_tok = [RAW[:, 10240 + n * D:10240 + (n + 1) * D] for n in range(2)]

        rows_in, h_tok, rows_out = (RA[:, n * D:(n + 1) * D] for n in range(3))
        silu, gf_row = (RQ[:, n * D:(n + 1) * D] for n in range(2))

        def re_part(n):
            return region(MR, "RE")[:, n * D:(n + 1) * D]

        XH, XL, HH, HL = range(4)
        ln_rows = [RV[:, n * D:(n + 1) * D] for n in range(4)]
        back = [[RAW[:, (4 * k + b) * D:(4 * k + b + 1) * D] for b in range(TB)] for k in range(2)]

        used = [0]

        def rt(n, *shape):
            a = RG[:, used[0]:used[0] + n]
            used[0] += n
            return a

        slot_hot = RG[:, 0:1024].rearrange("p (k s) -> p k s", k=2 * TB)
        used[0] = 1024
        chunk_tok = rt(2 * TB * (MAX_CHUNKS + 1)).rearrange("p (k s) -> p k s", k=2 * TB)
        prob, sel, selm, score = (rt(TB * E) for _ in range(4))
        hot = [rt(TB * E) for _ in range(2)]
        pair6 = rt(TB * GROUPS * 6).rearrange("p (g s) -> p g s", s=6)
        gscore, ghot, gtie = (rt(TB * GROUPS) for _ in range(3))
        where = [rt(TB * E) for _ in range(2)]
        rout = RV[:, 0:512]

        ident = sb("ident", [P, P])
        ident_b = sb("ident_b", [P, P], BF16)
        mask_fox = sb("mask_fox", [P, P], BF16)
        mask_sb = sb("mask_sb", [P, P], BF16)
        neg_tri = sb("neg_tri", [P, P])
        neg_ones = sb("neg_ones", [P, P])
        one_col = sb("one_col", [P, 1])
        before = ident_b
        head_sel = sb("head_sel", [P, HEADS, P], BF16)
        f_split = sb("f_split", [P, T], BF16)
        col_stage = sb("col_stage", [N_COLS, P])
        cols = sb("cols", [P, N_COLS])
        modc = sb("modc", [P, N_ROWS * KT])
        cond = sb("cond", [P, 3, KT])
        w_forget = sb("w_forget", [P, KT, HEADS])
        bf_col = sb("bf_col", [HEADS, 1])
        lsum = sb("lsum", [P, HEADS, TB])
        nmax = sb("nmax", [P, 2, TB])
        rms_t = sb("rms_t", [P, 2, 3, TB])
        neg_half = sb("neg_half", [P, TB])
        stats = sb("stats", [P, 2, 6])
        mv = sb("mv", [P, TB, 2])
        rstd = sb("rstd", [P, 2, TB])
        in2 = modc[:, U2_SCALE * KT:(U2_SHIFT + 1) * KT].rearrange("p (a c) -> p a c", a=2)
        wr = f_split[:, 0:2 * KT * E].bitcast(F32).rearrange("p (c e) -> p c e", c=KT)
        small = sb("small", [P, 64])
        table = sb("table", [1, 64], I32)
        row_idx = sb("row_idx", [P, MAX_CHUNKS + 1], I32)
        row_now = sb("row_now", [P, 1], I32)
        dest = sb("dest", [P, 2 * TB], I32)
        ps = ctx.enter_context(nc.psum_tensor("ps", [P, 8, 512], F32))

        Z_AT = [(4, 0), (5, 0), (6, 0), (6, 2 * P)]
        z_part = [ps[:, (6, 5, 4)[n], span(n)] for n in range(3)]

        def wide_bank(n):
            return ps[:, n:n + 2, :].rearrange("p a n -> p (a n)")

        FOX_OUT, SB_OUT = 3, 7

        iota_r = head_sel[:, 0:2, :].rearrange("p h n -> p (h n)").bitcast(F32)
        iota_i = head_sel[:, 2:4, :].rearrange("p h n -> p (h n)").bitcast(I32)
        one_b = head_sel[:, 4, :]
        chosen = head_sel[:, 5, 0:TB * E].rearrange("p (b e) -> p b e", b=TB)
        fl = head_sel[:, 6:8, :].rearrange("p h n -> p (h n)").bitcast(F32)
        tie_e, tie_g, tok_id = fl[:, 0:E], fl[:, 16:16 + GROUPS], fl[:, 32:32 + TB]
        b_rout = fl[:, 48:48 + E]
        tok_i = fl[:, 64:64 + TB].bitcast(I32)

        S = {}
        for name in """rows_landed x_landed wf_landed bf_landed xr_landed br_landed wr_landed
            lnrow_landed consts cols_up cols_ready cond_exp cond_ready mod_summed mod_up mod_ready
            xT_up uT_ready f_up f_abs f_exp f_ready unit_done unit_ready gate_ready
            z_ready clamped sp_log sp_ready r_ready stick_ready
            s_ready max_ready prob_ready t_up pT_ready fox_ready sb_ready
            fox_sq sb_sq rms_ask rms_got fox_freed sb_freed fox_gated qk_dead
            oT_up oT_ready y_up ln_freed ln_ask ln_got normed
            nT_up u2T_ready logits_up rcopy_ready rank_up idx_up
            rconst routed_hot tables_ready idx_now dest_ready rexp slots_ready prob_e
            gathered rows_up xT_high xT_ready silu_done h_ready h_up hT_high hT_ready y_out rows_stored
            front_split_h front_freed first_half_used uT_high uT_split_done rows_turned rows_copied mod_stored
            ga_landed u2row_landed gf_landed wout_split wout_free raw_freed split_h split_l piece_used u2_made oT_high
            sp_exp row_set spare_cleared uT_ready_d gather_go u2T_ready_d fin_ask fin_got fin_done out_stored dve_step act_step pool_step""".split():
            S[name] = sem(name)
        front_landed = [sem(f"front_landed_{s}") for s in range(RAW_SLOTS)]
        wout_landed = [sem(f"wout_landed_{s}") for s in range(2)]
        u2_stored = [sem(f"u2_stored_{s}") for s in range(2)]
        raw_landed = [sem(f"raw_landed_{s}") for s in range(RAW_SLOTS)]
        back_landed = [sem(f"back_landed_{s}") for s in range(2 * TB)]

        w_mod_v = w_mod[0].rearrange("(c p) n -> p c n", p=P)
        w_in_v = w_in[0].rearrange("(c p) n -> p c n", p=P)
        w_out_v = w_out[0].rearrange("(c p) n -> p c n", p=P)
        x_v = x[0].rearrange("(b p) n -> p b n", p=P)
        out_v = out[0].rearrange("(b p) n -> p b n", p=P)
        u2_v = u2_dram.rearrange("(b p) n -> p b n", p=P)

        def piece_source(w, e, n):
            return w[0, e, 2 * n * P:(2 * n + 2) * P, :].rearrange("(c p) n -> p c n", p=P)

        block = ctx.enter_context(nc.Block())

        @block.sync
        def _(sp_):
            for r0, src in ((COL_BMOD, b_mod), (COL_C, c), (COL_LNG, ln1_g), (COL_LNB, ln1_b),
                            (COL_ONG, out_norm_g)):
                n = src.shape[1] // P
                sp_.dma_start(col_stage[r0:r0 + n, :], src.rearrange("a (r n) -> (a r) n", n=P)
                              ).then_inc(S["rows_landed"], 16)
            sp_.dma_start(x_tok, x_v).then_inc(S["x_landed"], 16)

            for n, (kind, m) in enumerate(FRONT):
                if n >= RAW_SLOTS:
                    sp_.wait_ge(S["front_freed"], n - RAW_SLOTS + 1)
                if kind == "mod":
                    seg, part = MOD_ORDER[m // 4], m % 4
                    src = w_mod_v[:, 2 * part:2 * part + 2, seg * D:(seg + 1) * D]
                    dst = tiles(raw_piece(n % RAW_SLOTS), 2)
                else:
                    col = GROUP_COLS[m // 2]
                    src = w_in_v[:, 4 * (m % 2):4 * (m % 2) + 4, col:col + DG]
                    dst = tiles(raw_piece(n % RAW_SLOTS), 4)
                sp_.dma_start(dst, src).then_inc(front_landed[n % RAW_SLOTS], 16)

            sp_.wait_ge(S["front_freed"], len(FRONT))
            for n in range(4):
                if n >= 2:
                    sp_.wait_ge(S["wout_split"], 2 * (n - 1))
                sp_.dma_start(tiles(raw_piece(4 + n % 2), 2), w_out_v[:, 2 * n:2 * n + 2, :]
                              ).then_inc(wout_landed[n % 2], 16)
                if n == 1:
                    sp_.wait_ge(S["mod_stored"], 16)
                    sp_.dma_start(ga_row, mod_dram[G_A:G_A + 1, :].to_broadcast([P, D])
                                  ).then_inc(S["ga_landed"], 16)
            sp_.wait_ge(S["qk_dead"], 1)
            sp_.dma_start(resid, x_v).then_inc(S["xr_landed"], 16)
            sp_.wait_ge(S["wout_split"], 8)
            for n in range(2):
                sp_.dma_start(u2_rows[n], mod_dram[U2_SCALE + n:U2_SCALE + n + 1, :].to_broadcast([P, D])
                              ).then_inc(S["u2row_landed"], 16)

            def load_piece(slot, w, e, m):
                sp_.dma_start(tiles(raw_piece(slot), 2),
                              w[0, e, :, :].rearrange("(c p) n -> p c n", p=P)[:, 2 * m:2 * m + 2, :]
                              ).then_inc(raw_landed[slot], 16)

            def load_gate_up(e, j, slot):
                load_piece(slot, (w_gate, w_up)[j % 2], e, j // 2)

            sp_.wait_ge(S["fox_freed"], HEADS)
            sp_.wait_ge(S["sb_freed"], HEADS)
            sp_.wait_ge(S["spare_cleared"], 16)
            for j in range(3):
                load_gate_up(0, j, j)
            sp_.wait_ge(S["ln_ask"], TB)
            load_gate_up(0, 3, 3)
            sp_.wait_ge(S["y_up"], TB)
            sp_.dma_start(gf_row, mod_dram[G_F:G_F + 1, :].to_broadcast([P, D])).then_inc(S["gf_landed"], 16)
            sp_.wait_ge(S["u2_made"], TB)
            load_gate_up(0, 4, 4)
            for n in range(2):
                sp_.wait_ge(u2_stored[n], 32)
            load_gate_up(0, 5, 5)
            for j in range(6, GU_PIECES):
                sp_.wait_ge(S["split_l"], j + 1 - RAW_SLOTS)
                load_gate_up(0, j, j % RAW_SLOTS)

            sp_.wait_ge(S["tables_ready"], 1)
            last = sp_.value_load(table[0:1, G_COL:G_COL + 1], min_val=E - 1, max_val=MAX_CHUNKS - 1)
            with sp_.Fori(0, last) as i:
                e_next = sp_.value_load(table[0:1, bass.ds(i + 1, 1)], min_val=0, max_val=E - 1)
                for j in range(GU_PIECES):
                    sp_.wait_ge(S["split_l"], CHUNK_PIECES * i + GU_PIECES + j + 1 - RAW_SLOTS)
                    load_gate_up(e_next, j, (GU_PIECES + j) % RAW_SLOTS)
                e_now = sp_.value_load(table[0:1, bass.ds(i, 1)], min_val=0, max_val=E - 1)
                for j in range(GU_PIECES, CHUNK_PIECES):
                    sp_.wait_ge(S["split_l"], CHUNK_PIECES * i + GU_PIECES + j + 1 - RAW_SLOTS)
                    load_piece((GU_PIECES + j) % RAW_SLOTS, w_down, e_now, j - GU_PIECES)
            e_last = sp_.value_load(table[0:1, bass.ds(last, 1)], min_val=0, max_val=E - 1)
            for j in range(DN_PIECES):
                sp_.wait_ge(S["split_l"], CHUNK_PIECES * last + GU_PIECES + j + 1 - RAW_SLOTS)
                load_piece((GU_PIECES + j) % RAW_SLOTS, w_down, e_last, j)
            for b in range(TB):
                sp_.wait_ge(S["fin_done"], b + 1)
                sp_.dma_start(out_v[:, b, :], back[0][b]).then_inc(S["out_stored"], 16)
            sp_.wait_ge(S["out_stored"], 16 * TB)

        @block.gpsimd
        def _(pool):
            steps = [0]

            def step(ins):
                steps[0] += 1
                ins.then_inc(S["pool_step"], 1)
                pool.wait_ge(S["pool_step"], steps[0])

            pool.memset(ident[:], 0.0)
            pool.memset(ident_b[:], 0.0)
            pool.memset(mask_fox[:], 0.0)
            pool.memset(mask_sb[:], 0.0)
            pool.memset(neg_tri[:], -1.0)
            pool.memset(neg_ones[:], -1.0)
            pool.memset(one_col[:], 1.0)
            pool.memset(neg_half[:], -0.5)
            pool.memset(f_split[:], 0.0)
            step(pool.memset(head_sel[:], 0.0))
            pool.affine_select(out=ident[:], in_=ident[:], compare_op=ALU.not_equal, fill=1.0, base=0,
                               pattern=[[-1, P]], channel_multiplier=1)
            pool.affine_select(out=ident_b[:], in_=ident_b[:], compare_op=ALU.not_equal, fill=1.0, base=0,
                               pattern=[[-1, P]], channel_multiplier=1)
            pool.affine_select(out=mask_fox[:], in_=mask_fox[:], compare_op=ALU.is_ge, fill=NEG, base=0,
                               pattern=[[-1, P]], channel_multiplier=1)
            pool.affine_select(out=mask_sb[:], in_=mask_sb[:], compare_op=ALU.is_ge, fill=NEG, base=-1,
                               pattern=[[1, P]], channel_multiplier=-1)
            pool.affine_select(out=neg_tri[:], in_=neg_tri[:], compare_op=ALU.is_ge, fill=0.0, base=0,
                               pattern=[[-1, P]], channel_multiplier=1)
            for part in range(3):
                step(pool.affine_select(out=head_sel[:], in_=head_sel[:], compare_op=ALU.not_equal, fill=1.0,
                                        base=-32 * part, pattern=[[-1, HEADS], [0, P]],
                                        channel_multiplier=1))
            pool.memset(small[:], 0.0).then_inc(S["consts"], 1)

            pool.wait_ge(S["rows_copied"], 1)
            pool.dma_start(mod_dram.rearrange("s (c p) -> (s c) p", p=P), mod_rows).then_inc(S["mod_stored"], 16)

            pool.wait_ge(S["front_freed"], len(FRONT))
            step(pool.memset(zeros, 0.0))
            pool.dma_start(result_dram[(E + 1) * FC:, :].rearrange("(p q) (h n) -> p (q h) n", p=P, n=512),
                           zeros.unsqueeze(1).broadcast_to([P, 2 * (MAX_CHUNKS - E), 512])
                           ).then_inc(S["spare_cleared"], 16)

            def rms_power(n):
                pool.wait_ge(S["rms_ask"], n + 1)
                pool.tensor_tensor(rms_t[:, n % 2, 2, :], rms_t[:, n % 2, 1, :], neg_half[:], ALU.pow
                                   ).then_inc(S["rms_got"], 1)

            def fox_gate(h):
                pool.wait_ge(S["fox_freed"], h + 1)
                pool.wait_ge(S["gate_ready"], TB)
                cs = slice(h * HD, (h + 1) * HD)
                pool.tensor_tensor(o_tok[:, :, cs], o_tok[:, :, cs], gate[:, :, cs], ALU.mult
                                   ).then_inc(S["fox_gated"], 1)

            def split_wout(h):
                n, cs = h // 2, slice(h % 2 * D, (h % 2 + 1) * D)
                pool.wait_ge(wout_landed[n % 2], 16 * (n // 2 + 1))
                pool.wait_ge(S["unit_done"], UNITS)
                raw = raw_piece(4 + n % 2)[:, cs]
                step(pool.tensor_copy(split_piece(n, 0)[:, cs], raw))
                pool.tensor_tensor(split_piece(n, 1)[:, cs], raw, as_f32(split_piece(n, 0)[:, cs]), ALU.subtract
                                   ).then_inc(S["wout_split"], 1)

            for h in range(HEADS):
                if h:
                    rms_power(2 * h - 2)
                    rms_power(2 * h - 1)
                    fox_gate(h - 1)
                split_wout(h)
            rms_power(2 * HEADS - 2)
            rms_power(2 * HEADS - 1)
            fox_gate(HEADS - 1)

            pool.wait_ge(S["oT_up"], 1)
            step(pool.iota(iota_i, [[1, P]], base=0, channel_multiplier=0))
            step(pool.iota(tok_i, [[P, TB]], base=0, channel_multiplier=1))
            pool.tensor_copy(iota_r, iota_i)
            pool.tensor_copy(tok_id, tok_i)
            pool.memset(one_b, 1.0)
            step(pool.memset(before[:], 1.0))
            step(pool.affine_select(out=before[:], in_=before[:], compare_op=ALU.is_ge, fill=0.0, base=-1,
                                    pattern=[[1, P]], channel_multiplier=-1))
            pool.tensor_scalar(tie_e, iota_r[:, 0:E], -1.0, float(E), ALU.mult, ALU.add)
            step(pool.tensor_scalar(tie_g, iota_r[:, 0:GROUPS], -1.0, float(GROUPS), ALU.mult, ALU.add))
            pool.dma_start(wr, w_router.rearrange("(c p) e -> p c e", p=P)).then_inc(S["wr_landed"], 16)
            pool.dma_start(b_rout, b_router.rearrange("(a e) -> a e", a=1).to_broadcast([P, E])
                           ).then_inc(S["br_landed"], 16)
            pool.memset(small[:], 0.0).then_inc(S["rconst"], 1)

            for b in range(TB):
                pool.wait_ge(S["ln_ask"], b + 1)
                pool.tensor_tensor(rstd[:, 1, b:b + 1], rstd[:, 0, b:b + 1], neg_half[:, 0:1], ALU.pow
                                   ).then_inc(S["ln_got"], 1)
                if b == 0:
                    pool.wait_ge(S["u2row_landed"], 32)
                if b >= 2:
                    pool.wait_ge(u2_stored[b % 2], 16)
                pool.wait_ge(S["normed"], b + 1)
                step(pool.tensor_tensor(u2_tok[b % 2], resid[:, b, :], u2_rows[0], ALU.mult))
                pool.tensor_tensor(u2_tok[b % 2], u2_tok[b % 2], u2_rows[1], ALU.add).then_inc(S["u2_made"], 1)
                pool.wait_ge(S["u2_made"], b + 1)
                pool.dma_start(u2_v[:, b, :], u2_tok[b % 2]).then_inc(u2_stored[b % 2], 16)

            for j in range(SPLIT_SLOTS):
                pool.wait_ge(S["split_h"], j + 1)
                pool.tensor_tensor(split_piece(j, 1), raw_piece(j), as_f32(split_piece(j, 0)), ALU.subtract
                                   ).then_inc(S["split_l"], 1)


            pool.wait_ge(S["slots_ready"], 1)
            for n, src in enumerate((ln1_g, ln1_b, ln2_g, ln2_b)):
                pool.dma_start(ln_rows[n], src.to_broadcast([P, D])).then_inc(S["lnrow_landed"], 16)

            def gather():
                pool.indirect_dma_start(out=rows_in, out_offset=None, in_=u2_dram,
                                        in_offset=bass.IndirectOffsetOnAxis(ap=row_now[:], axis=0)
                                        ).then_inc(S["gathered"], 16)

            pool.wait_ge(S["idx_now"], 1)
            for n in range(2):
                pool.wait_ge(u2_stored[n], 32)
            pool.tensor_copy(row_now[:], row_idx[:, 0:1]).then_inc(S["row_set"], 1)
            pool.wait_ge(S["row_set"], 1)
            gather()
            last = pool.value_load(table[0:1, G_COL:G_COL + 1], min_val=E - 1, max_val=MAX_CHUNKS - 1)
            with pool.Fori(0, last + 1) as g:
                pool.wait_ge(S["gathered"], 16 * g + 16)
                pool.wait_ge(S["rows_up"], g + 1)
                pool.tensor_copy(row_now[:], row_idx[:, bass.ds(g + 1, 1)]).then_inc(S["row_set"], 1)
                pool.wait_ge(S["row_set"], g + 2)
                pool.sem_inc(S["gather_go"], 1)
                gather()

            pool.wait_ge(S["rows_stored"], 16 * last + 48)
            pool.wait_ge(S["split_l"], CHUNK_PIECES * last + CHUNK_PIECES)
            pool.sem_inc(S["gather_go"], 1)
            for b in range(TB):
                for k in range(2):
                    pool.indirect_dma_start(out=back[k][b], out_offset=None, in_=result_dram,
                                            in_offset=bass.IndirectOffsetOnAxis(
                                                ap=dest[:, k * TB + b:k * TB + b + 1], axis=0)
                                            ).then_inc(back_landed[2 * b + k], 16)
            for b in range(TB):
                pool.wait_ge(S["fin_ask"], b + 1)
                pool.tensor_tensor(rstd[:, 1, b:b + 1], rstd[:, 0, b:b + 1], neg_half[:, 0:1], ALU.pow
                                   ).then_inc(S["fin_got"], 1)

        @block.scalar
        def _(act):
            act.dma_start(w_forget[:], w_in_v[:, :, 4 * DG:4 * DG + HEADS]).then_inc(S["wf_landed"], 16)
            act.dma_start(bf_col[:], b_forget.rearrange("a h -> h a")).then_inc(S["bf_landed"], 16)
            act.wait_ge(S["cols_ready"], 1)
            act.activation(cond[:, 0, :], cols[:, COL_C:COL_C + KT], ACT.Exp, scale=-1.0
                           ).then_inc(S["cond_exp"], 1)

            def win_high(m):
                n = FRONT_AT["win", m]
                act.wait_ge(front_landed[n % RAW_SLOTS], 16 * (n // RAW_SLOTS + 1))
                if m >= SPLIT_SLOTS:
                    g = (m - SPLIT_SLOTS) // 2
                    act.wait_ge(*((S["first_half_used"], g + 1) if m % 2 == 0 else (S["unit_done"], 4 * g + 4)))
                act.activation(split_piece(m % SPLIT_SLOTS, 0), raw_piece(n % RAW_SLOTS), ACT.Copy
                               ).then_inc(S["front_split_h"], 1)

            win_high(0)
            win_high(1)
            act.wait_ge(S["mod_ready"], 2)
            for t in range(0, KT, 2):
                act.wait_ge(S["xT_up"], t + 1)
                act.activation(uT[:, t, :], ps[:, t % 6, :], ACT.Identity,
                               scale=modc[:, SC_A * KT + t:SC_A * KT + t + 1],
                               bias=modc[:, SH_A * KT + t:SH_A * KT + t + 1]).then_inc(S["uT_ready"], 1)
            for t in range(0, KT, 2):
                act.wait_ge(S["uT_ready"], t // 2 + 1)
                act.wait_ge(S["uT_ready_d"], t // 2 + 1)
                act.activation(uT_split[0][:, t:t + 2, :], uT[:, t:t + 2, :], ACT.Copy).then_inc(S["uT_high"], 1)

            act.wait_ge(S["f_abs"], 1)
            act.activation(fgt[1], fgt[1], ACT.Exp, scale=-1.0).then_inc(S["act_step"], 1)
            act.wait_ge(S["act_step"], 1)
            act.activation(fgt[1], fgt[1], ACT.Ln, bias=1.0).then_inc(S["f_exp"], 1)

            def unit_out(u):
                g, r = divmod(u, 4)
                if u == 4 * SK:
                    act.wait_ge(S["f_ready"], 1)
                if u == 4 * GATE:
                    act.wait_ge(S["mod_up"], 6)
                act.wait_ge(S["unit_done"], u + 1)
                src = ps[:, u % 4, :]
                if g in (FQ, SQ):
                    ins = act.activation((qf if g == FQ else qs)[:, r, :], src, ACT.Copy, scale=HD ** -0.5)
                elif g in (FK, SK):
                    ins = act.activation((kf if g == FK else ks)[:, r, :], src, ACT.Copy)
                elif g in (FV, SV):
                    ins = act.activation((vf if g == FV else vs)[:, r, :], src, ACT.Copy)
                else:
                    ins = act.activation(gate[:, r, :], src, ACT.Exp, scale=-1.0)
                ins.then_inc(S["unit_ready"], 1)

            win_high(2)
            win_high(3)
            for g in range(len(GROUP_COLS)):
                if 2 * g + 4 < WIN_PIECES:
                    win_high(2 * g + 4)
                for r in range(4):
                    unit_out(4 * g + r)
                if 2 * g + 5 < WIN_PIECES:
                    win_high(2 * g + 5)

            def exp_clamped(h, n):
                act.wait_ge(S["clamped"], 3 * h + n + 1)
                act.activation(sp_part[n], sp_part[n], ACT.Exp).then_inc(S["sp_exp"], 1)

            def log_one(h, n):
                act.wait_ge(S["sp_exp"], 3 * h + n + 1)
                act.activation(sp_part[n], sp_part[n], ACT.Ln, bias=1.0).then_inc(S["sp_log"], 1)

            def stick(h, n):
                act.wait_ge(S["r_ready"], 3 * h + n + 1)
                if h:
                    act.wait_ge(S["sb_ready"], h)
                act.activation(wT_part[n], z_part[n], ACT.Exp).then_inc(S["stick_ready"], 1)

            def prob_exp(h, b):
                act.wait_ge(S["max_ready"], 4 * h + b + 1)
                if h:
                    act.wait_ge(S["t_up"], 4 * (h - 1) + b + 1)
                act.activation(pr[b], ps[:, b % 2, 0:(b + 1) * P], ACT.Exp, bias=nmax[:, h % 2, b:b + 1],
                               accum_out=lsum[:, h, b:b + 1]).then_inc(S["prob_ready"], 1)

            def square(kind, h):
                ready, done, freed, dst = ((S["fox_ready"], S["fox_sq"], S["rms_ask"], sq_fox),
                                           (S["sb_ready"], S["sb_sq"], S["rms_ask"], sq_sb))[kind]
                act.wait_ge(ready, h + 1)
                if h:
                    act.wait_ge(S["rms_ask"], 2 * h - 1 + kind)
                act.activation(dst, ps[:, (FOX_OUT, SB_OUT)[kind], 0:256], ACT.Square).then_inc(done, 1)

            for h in range(HEADS):
                for n in range(3):
                    exp_clamped(h, n)
                prob_exp(h, 0)
                if h:
                    square(0, h - 1)
                log_one(h, 0)
                prob_exp(h, 1)
                if h:
                    square(1, h - 1)
                log_one(h, 1)
                log_one(h, 2)
                prob_exp(h, 2)
                stick(h, 0)
                prob_exp(h, 3)
                stick(h, 1)
                stick(h, 2)
            square(0, HEADS - 1)
            square(1, HEADS - 1)

            act.wait_ge(S["sb_freed"], HEADS)
            for t in range(KT):
                act.wait_ge(S["oT_up"], t + 1)
                act.activation(oT_split[0][:, t, :], ps[:, t % 4, :], ACT.Copy,
                               scale=cols[:, COL_ONG + t:COL_ONG + t + 1]).then_inc(S["oT_high"], 1)
            for b in range(TB):
                act.wait_ge(S["nT_up"], 2 * b + 1)
                for t in range(4):
                    ins = act.activation(u2T[:, t, b * P:(b + 1) * P], ps[:, 0, t * P:(t + 1) * P],
                                         ACT.Identity, scale=in2[:, 0, t:t + 1], bias=in2[:, 1, t:t + 1])
                ins.then_inc(S["u2T_ready"], 1)
            act.wait_ge(S["rcopy_ready"], 1)
            act.activation(prob, prob, ACT.Exp).then_inc(S["rexp"], 1)

            def high(turn, j):
                n0 = j if turn is None else GU_PIECES + j
                landed = 16 * (n0 // RAW_SLOTS + 1)
                act.wait_ge(raw_landed[n0 % RAW_SLOTS],
                            landed if turn is None else 16 * (CHUNK_PIECES // RAW_SLOTS) * turn + landed)
                if turn is not None:
                    act.wait_ge(S["piece_used"], CHUNK_PIECES * turn + n0 - SPLIT_SLOTS + 1)
                elif j >= SPLIT_SLOTS:
                    act.wait_ge(S["piece_used"], j - SPLIT_SLOTS + 1)
                act.activation(split_piece(n0 % SPLIT_SLOTS, 0), raw_piece(n0 % RAW_SLOTS), ACT.Copy
                               ).then_inc(S["split_h"], 1)

            def hidden_silu(used, before=None):
                act.wait_ge(S["piece_used"], used)
                if before is not None:
                    act.wait_ge(S["h_ready"], before)
                act.activation(silu, wide_bank(0), ACT.Silu).then_inc(S["silu_done"], 1)

            def turned_high(up, count, part, done):
                act.wait_ge(up, count)
                act.activation(re_part(part), wide_bank(6), ACT.Copy).then_inc(done, 1)

            def store_rows(made, count):
                act.wait_ge(S["y_out"], count)
                act.dma_start(result_dram[made, :], rows_out).then_inc(S["rows_stored"], 16)

            act.wait_ge(S["y_up"], TB)
            for j in range(SPLIT_SLOTS):
                high(None, j)
            turned_high(S["rows_up"], 1, XH, S["xT_high"])
            for j in range(SPLIT_SLOTS, GU_PIECES):
                high(None, j)
            hidden_silu(GU_PIECES)
            turned_high(S["rows_up"], 2, XH, S["xT_high"])
            act.wait_ge(S["spare_cleared"], 16)
            act.sem_inc(S["rows_stored"], 16)
            last = act.value_load(table[0:1, G_COL:G_COL + 1], min_val=E - 1, max_val=MAX_CHUNKS - 1)
            with act.Fori(0, last) as i:
                for j in range(4):
                    high(i, j)
                turned_high(S["h_up"], i + 1, HH, S["hT_high"])
                for j in range(4, 7):
                    high(i, j)
                store_rows(bass.ds(i * FC, FC), i + 1)
                for j in range(7, CHUNK_PIECES):
                    high(i, j)
                hidden_silu(CHUNK_PIECES * i + 2 * GU_PIECES, before=i + 1)
                turned_high(S["rows_up"], i + 3, XH, S["xT_high"])
            for j in range(DN_PIECES):
                high(last, j)
            turned_high(S["h_up"], last + 1, HH, S["hT_high"])
            store_rows(bass.ds(last * FC, FC), last + 1)
            store_rows(bass.ds(last * FC + FC, FC), last + 2)

        @block.tensor
        def _(pe):
            pe.wait_ge(S["consts"], 1)
            pe.wait_ge(S["rows_landed"], 80)
            pe.transpose(ps[:, 7, 0:N_COLS], col_stage[:], ident[0:N_COLS, 0:N_COLS]).then_inc(S["cols_up"], 1)
            pe.wait_ge(S["x_landed"], 16)

            def x_tile(t):
                for b in range(TB):
                    ins = pe.transpose(ps[:, t % 6, b * P:(b + 1) * P], x_tok[:, b, t * P:(t + 1) * P], ident[:])
                ins.then_inc(S["xT_up"], 1)

            def mod_column(pos):
                pe.wait_ge(S["mod_summed"], pos + 1)
                for t in range(KT):
                    ins = pe.matmul(ps[:, 6, pos * KT + t:pos * KT + t + 1], mod_sum(pos)[:, t * P:(t + 1) * P],
                                    one_col[:], start=True, stop=True)
                ins.then_inc(S["mod_up"], 1)

            for t in range(6):
                x_tile(t)
            mod_column(0)
            mod_column(1)
            pe.wait_ge(S["uT_ready"], 1)
            x_tile(6)
            pe.wait_ge(S["uT_ready_d"], 1)
            x_tile(7)
            pe.wait_ge(S["uT_ready"], KT // 2)
            pe.wait_ge(S["uT_ready_d"], KT // 2)
            pe.wait_ge(S["wf_landed"], 16)
            for t in range(KT):
                ins = pe.matmul(ps[0:HEADS, 7, :], w_forget[:, t, :], uT[:, t, :], start=(t == 0), stop=(t == KT - 1))
            ins.then_inc(S["f_up"], 1)

            def product(out, lhs, rhs, first, last):
                for n, (a, b) in enumerate(((0, 0), (0, 1), (1, 0))):
                    ins = pe.matmul(out, lhs[a], rhs[b], start=first and n == 0, stop=last and n == 2)
                return ins

            for m in range(WIN_PIECES):
                g, part = divmod(m, 2)
                if m in MOD_BEFORE:
                    mod_column(MOD_BEFORE[m])
                pe.wait_ge(S["front_freed"], FRONT_AT["win", m] + 1)
                w = [tiles(split_piece(m % SPLIT_SLOTS, n), 4) for n in range(2)]
                pe.wait_ge(S["uT_split_done"], 2 * part + 2 if m < 2 else 4)
                for r in range(4):
                    u = 4 * g + r
                    if g and part == 0:
                        pe.wait_ge(S["unit_ready"], u - 3)
                    for k in range(4):
                        t = 4 * part + k
                        tok = [uT_split[n][:, t, r * P:(r + 1) * P] for n in range(2)]
                        if g in (FV, SV, GATE):
                            lhs, rhs = tok, [w[n][:, k, :] for n in range(2)]
                        else:
                            lhs = [w[n][:, k, r * P:(r + 1) * P] for n in range(2)]
                            rhs = [uT_split[n][:, t, :] for n in range(2)]
                        ins = product(ps[:, r, :], lhs, rhs, t == 0, t == KT - 1)
                    if part == 1:
                        ins.then_inc(S["unit_done"], 1)
                if part == 0:
                    ins.then_inc(S["first_half_used"], 1)
            pe.wait_ge(S["mod_ready"], 7)
            pe.transpose(ps[0:N_ROWS * KT, 7, 0:P], modc[:], ident[:]).then_inc(S["rows_turned"], 1)

            def place(h):
                return slice(HD * (h % 2), HD * (h % 2) + HD), h // 2

            def stick_scores(h, n):
                rows, t = place(h)
                if h:
                    pe.wait_ge(S["stick_ready"], 3 * (h - 1) + n + 1)
                for i in ((2, 3), (1,), (0,))[n]:
                    bank, at = Z_AT[i]
                    pe.matmul(ps[:, bank, at:at + P], ident_b[:], mask_sb[:], start=(i != 3), stop=False,
                              skip_group_check=True)
                    ins = pe.matmul(ps[:, bank, at:at + (TB - i) * P], ks[rows, t, i * P:(i + 1) * P],
                                    qs[rows, t, i * P:T], start=False, stop=True, skip_group_check=True)
                ins.then_inc(S["z_ready"], 1)

            def fox_scores(h, b):
                rows, t = place(h)
                n = 4 * h + b
                if n >= 2:
                    pe.wait_ge(S["prob_ready"], n - 1)
                cols_ = (b + 1) * P
                pe.matmul(ps[:, b % 2, b * P:cols_], ident_b[:], mask_fox[:], start=True, stop=False,
                          skip_group_check=True)
                pe.matmul(ps[:, b % 2, 0:cols_], head_sel[:, h, :], f_split[:, 0:cols_], start=False,
                          stop=False, skip_group_check=True)
                pe.matmul(ps[:, b % 2, 0:cols_], qf[rows, t, b * P:(b + 1) * P], kf[rows, t, 0:cols_],
                          start=False, stop=True, skip_group_check=True).then_inc(S["s_ready"], 1)

            def fox_turn(h, b):
                n = 4 * h + b
                pe.wait_ge(S["prob_ready"], n + 1)
                pe.wait_ge(S["pT_ready"], n)
                for i in range(b + 1):
                    ins = pe.transpose(ps[:, 2, i * P:(i + 1) * P], pr[b][:, i * P:(i + 1) * P], ident[:])
                ins.then_inc(S["t_up"], 1)

            def fox_values(h, b):
                n = 4 * h + b
                pe.wait_ge(S["pT_ready"], n + 1)
                if b == 0 and h:
                    pe.wait_ge(S["fox_freed"], h)
                for i in range(b + 1):
                    ins = pe.matmul(ps[:, FOX_OUT, b * HD:(b + 1) * HD], pT[b][:, i * P:(i + 1) * P],
                                    vf[:, i, h * HD:(h + 1) * HD], start=(i == 0), stop=(i == b))
                if b == TB - 1:
                    ins.then_inc(S["fox_ready"], 1)

            def stick_sums(h, n):
                pe.wait_ge(S["sp_ready"], 3 * h + n + 1)
                for i in ((3, 2), (1,), (0,))[n]:
                    bank, at = Z_AT[i]
                    end = at + (TB - i) * P
                    for j in range(i + 1, TB):
                        pe.matmul(ps[:, bank, at + (j - i) * P:end], neg_ones[:], sp[j], start=False,
                                  stop=False, skip_group_check=True)
                    ins = pe.matmul(ps[:, bank, at:end], neg_tri[:], sp[i], start=False, stop=True,
                                    skip_group_check=True)
                ins.then_inc(S["r_ready"], 1)

            def stick_values(h):
                pe.wait_ge(S["stick_ready"], 3 * h + 3)
                if h:
                    pe.wait_ge(S["sb_freed"], h)
                for b in range(TB):
                    for i in range(b + 1):
                        ins = pe.matmul(ps[:, SB_OUT, b * HD:(b + 1) * HD],
                                        wT[i][:, (b - i) * P:(b - i + 1) * P], vs[:, i, h * HD:(h + 1) * HD],
                                        start=(i == 0), stop=(i == b))
                ins.then_inc(S["sb_ready"], 1)

            pe.wait_ge(S["f_ready"], 1)
            pe.wait_ge(S["mod_ready"], 6)
            for h in range(HEADS):
                for n in range(3):
                    stick_scores(h, n)
                if h == 0:
                    pe.wait_ge(S["unit_ready"], UNITS)
                if h == HEADS - 1:
                    pe.wait_ge(S["z_ready"], 3 * HEADS)
                    pe.nop().then_inc(S["qk_dead"], 1)
                fox_scores(h, 0)
                fox_scores(h, 1)
                if h:
                    stick_values(h - 1)
                fox_turn(h, 0)
                fox_scores(h, 2)
                stick_sums(h, 0)
                fox_turn(h, 1)
                fox_values(h, 0)
                fox_scores(h, 3)
                stick_sums(h, 1)
                fox_turn(h, 2)
                fox_values(h, 1)
                stick_sums(h, 2)
                fox_turn(h, 3)
                fox_values(h, 2)
                fox_values(h, 3)
            stick_values(HEADS - 1)

            pe.wait_ge(S["fox_gated"], HEADS)
            pe.wait_ge(S["sb_freed"], HEADS)
            for t in range(KT):
                if t >= 4:
                    pe.wait_ge(S["oT_ready"], t - 3)
                for b in range(TB):
                    ins = pe.transpose(ps[:, t % 4, b * P:(b + 1) * P], o_tok[:, b, t * P:(t + 1) * P], ident[:])
                ins.then_inc(S["oT_up"], 1)
            pe.wait_ge(S["oT_ready"], KT)
            pe.wait_ge(S["wout_split"], 8)

            def project_out(b):
                bank = 6 - 2 * (b % 2)
                if b >= 2:
                    pe.wait_ge(S["ln_freed"], b - 1)
                for half in range(2):
                    for t in range(KT):
                        at = (t % 2) * D + half * 512
                        ins = product(ps[:, bank + half, :], [oT_split[n][:, t, b * P:(b + 1) * P] for n in range(2)],
                                      [split_piece(t // 2, n)[:, at:at + 512] for n in range(2)],
                                      t == 0, t == KT - 1)
                ins.then_inc(S["y_up"], 1)

            def turn_normed(b):
                pe.wait_ge(S["normed"], b + 1)
                for half in range(2):
                    if b:
                        pe.wait_ge((S["u2T_ready"], S["u2T_ready_d"])[half], b)
                    for t in range(4):
                        ins = pe.transpose(ps[:, half, t * P:(t + 1) * P],
                                           resid[:, b, (4 * half + t) * P:(4 * half + t + 1) * P], ident[:])
                    ins.then_inc(S["nT_up"], 1)

            def route(b):
                pe.wait_ge(S["u2T_ready"], b + 1)
                pe.wait_ge(S["u2T_ready_d"], b + 1)
                if b == 0:
                    pe.wait_ge(S["wr_landed"], 16)
                for t in range(KT):
                    ins = pe.matmul(ps[:, 2, b * E:(b + 1) * E], u2T[:, t, b * P:(b + 1) * P], wr[:, t, :],
                                    start=(t == 0), stop=(t == KT - 1))
                ins.then_inc(S["logits_up"], 1)

            project_out(0)
            project_out(1)
            turn_normed(0)
            project_out(2)
            turn_normed(1)
            project_out(3)
            turn_normed(2)
            turn_normed(3)
            for b in range(TB):
                route(b)

            pe.wait_ge(S["routed_hot"], 1)
            for b in range(TB):
                for prev in range(b):
                    pe.matmul(ps[:, 3, b * E:(b + 1) * E], one_b, chosen[:, prev, :], start=(prev == 0), stop=False)
                pe.matmul(ps[:, 3, b * E:(b + 1) * E], before[:], chosen[:, b, :], start=(b == 0), stop=True)
            for b in range(TB):
                ins = pe.matmul(ps[:, 3, TB * E:TB * E + E], one_b, chosen[:, b, :], start=(b == 0), stop=(b == TB - 1))
            ins.then_inc(S["rank_up"], 1)
            pe.wait_ge(S["slots_ready"], 1)
            for n in range(2 * TB):
                ins = pe.matmul(ps[:, 3, 128:128 + MAX_CHUNKS + 1], slot_hot[:, n, :], chunk_tok[:, n, :],
                                start=(n == 0), stop=(n == 2 * TB - 1))
            ins.then_inc(S["idx_up"], 1)

            def use_piece(split, j, x, x_tile, bank, first, last):
                pe.wait_ge(S["split_l"], split)
                for k in range(2):
                    for half in range(2):
                        at = k * D + half * 512
                        t = x_tile + k
                        ins = product(ps[:, bank + half, :],
                                      [re_part(x + n)[:, t * P:(t + 1) * P] for n in range(2)],
                                      [split_piece(j % SPLIT_SLOTS, n)[:, at:at + 512] for n in range(2)],
                                      first and k == 0, last and k == 1)
                ins.then_inc(S["piece_used"], 1)

            def gate_up(split, j):
                use_piece(split, j, XH, j // 2 * 2, (0, 2)[j % 2], j < 2, j >= GU_PIECES - 2)

            def down(split, j):
                use_piece(split, j, HH, 2 * j, 4, j == 0, j == DN_PIECES - 1)

            def turn(src, up):
                for t in range(KT):
                    ins = pe.transpose(ps[:, 6 + t // 4, (t % 4) * P:(t % 4 + 1) * P], src[:, t * P:(t + 1) * P],
                                       ident[:])
                ins.then_inc(up, 1)

            pe.wait_ge(S["gathered"], 16)
            turn(rows_in, S["rows_up"])
            pe.wait_ge(S["xT_ready"], 1)
            for j in range(GU_PIECES):
                gate_up(j + 1, j)
            pe.wait_ge(S["gathered"], 32)
            turn(rows_in, S["rows_up"])
            pe.wait_ge(S["h_ready"], 1)
            pe.wait_ge(S["xT_ready"], 2)
            turn(h_tok, S["h_up"])
            pe.wait_ge(S["tables_ready"], 1)
            last = pe.value_load(table[0:1, G_COL:G_COL + 1], min_val=E - 1, max_val=MAX_CHUNKS - 1)
            with pe.Fori(0, last) as i:
                split = pe.snap(CHUNK_PIECES * i + GU_PIECES + 1)
                for j in range(GU_PIECES):
                    gate_up(split + j, j)
                pe.wait_ge(S["gathered"], 16 * i + 48)
                pe.wait_ge(S["hT_ready"], i + 1)
                turn(rows_in, S["rows_up"])
                pe.wait_ge(S["y_out"], i + 1)
                for j in range(DN_PIECES):
                    down(split + GU_PIECES + j, j)
                pe.wait_ge(S["h_ready"], i + 2)
                pe.wait_ge(S["xT_ready"], i + 3)
                turn(h_tok, S["h_up"])
            pe.wait_ge(S["hT_ready"], last + 1)
            pe.wait_ge(S["y_out"], last + 1)
            split = pe.snap(CHUNK_PIECES * last + GU_PIECES + 1)
            for j in range(DN_PIECES):
                down(split + j, j)

        @block.vector
        def _(dve):
            steps = [0]

            def step(ins):
                steps[0] += 1
                ins.then_inc(S["dve_step"], 1)
                dve.wait_ge(S["dve_step"], steps[0])

            dve.wait_ge(S["cols_up"], 1)
            step(dve.tensor_copy(cols[:], ps[:, 7, 0:N_COLS]))
            dve.nop().then_inc(S["cols_ready"], 1)
            dve.wait_ge(S["cond_exp"], 1)
            step(dve.tensor_scalar(cond[:, 1, :], cond[:, 0, :], 1.0, None, ALU.add))
            step(dve.reciprocal(cond[:, 2, :], cond[:, 1, :]))
            step(dve.tensor_tensor(cond[:, 0, :], cond[:, 2, :], cols[:, COL_C:COL_C + KT], ALU.mult))

            def mod_segment(pos):
                for part in range(4):
                    mod_piece(4 * pos + part)

            def mod_piece(m):
                pos, part = divmod(m, 4)
                n, acc = FRONT_AT["mod", m], mod_sum(pos)
                home = tiles(raw_piece(n % RAW_SLOTS), 2)
                dve.wait_ge(front_landed[n % RAW_SLOTS], 16 * (n // RAW_SLOTS + 1))
                if part == 0 and pos >= 2:
                    dve.wait_ge(S["mod_up"], pos - 1)
                for k in range(2):
                    t = 2 * part + k
                    if t == 0:
                        step(dve.tensor_scalar(acc, home[:, 0, :], cond[:, 0, 0:1], None, ALU.mult))
                    else:
                        step(dve.scalar_tensor_tensor(out=acc, in0=home[:, k, :], scalar=cond[:, 0, t:t + 1],
                                                      in1=acc, op0=ALU.mult, op1=ALU.add))
                if part == 3:
                    dve.nop().then_inc(S["mod_summed"], 1)
                dve.nop().then_inc(S["front_freed"], 1)

            def win_low(m):
                n = FRONT_AT["win", m]
                dve.wait_ge(S["front_split_h"], m + 1)
                dve.tensor_tensor(split_piece(m % SPLIT_SLOTS, 1), raw_piece(n % RAW_SLOTS),
                                  as_f32(split_piece(m % SPLIT_SLOTS, 0)), ALU.subtract).then_inc(S["front_freed"], 1)

            def uT_low(pair):
                dve.wait_ge(S["uT_high"], pair + 1)
                ts = slice(2 * pair, 2 * pair + 2)
                dve.tensor_tensor(uT_split[1][:, ts, :], uT[:, ts, :], as_f32(uT_split[0][:, ts, :]), ALU.subtract
                                  ).then_inc(S["uT_split_done"], 1)

            def mod_column(pos):
                seg = MOD_ORDER[pos]
                cs = slice(seg * KT, (seg + 1) * KT)
                dve.scalar_tensor_tensor(out=modc[:, cs], in0=ps[:, 6, pos * KT:(pos + 1) * KT],
                                         scalar=0.0 if seg in (SH_A, SH_F) else 1.0, in1=cols[:, cs],
                                         op0=ALU.add, op1=ALU.add).then_inc(S["mod_ready"], 1)

            mod_segment(0)
            mod_segment(1)
            dve.wait_ge(S["mod_up"], 2)
            mod_column(0)
            mod_column(1)
            dve.wait_ge(S["mod_ready"], 2)
            for t in range(1, KT, 2):
                dve.wait_ge(S["xT_up"], t + 1)
                dve.tensor_scalar(uT[:, t, :], ps[:, t % 6, :], modc[:, SC_A * KT + t:SC_A * KT + t + 1],
                                  modc[:, SH_A * KT + t:SH_A * KT + t + 1], ALU.mult, ALU.add
                                  ).then_inc(S["uT_ready_d"], 1)

            uT_low(0)
            uT_low(1)
            win_low(0)
            uT_low(2)
            uT_low(3)
            win_low(1)

            dve.wait_ge(S["f_up"], 1)
            dve.wait_ge(S["uT_split_done"], KT // 2)
            dve.wait_ge(S["bf_landed"], 16)
            step(dve.tensor_scalar(fgt[0], ps[0:HEADS, 7, :], bf_col[:, 0:1], None, ALU.add))
            dve.scalar_tensor_tensor(out=fgt[1], in0=fgt[0], scalar=-1.0, in1=fgt[0], op0=ALU.mult, op1=ALU.max
                                     ).then_inc(S["f_abs"], 1)
            step(dve.tensor_scalar(fgt[0], fgt[0], 0.0, None, ALU.min))
            dve.wait_ge(S["f_exp"], 1)
            step(dve.tensor_tensor(fgt[2], fgt[1], fgt[0], ALU.subtract))
            step(dve.memset(fgt[1], 1.0))
            step(dve.tensor_tensor_scan(fgt[3], fgt[1], fgt[2], 0.0, ALU.mult, ALU.add))
            cur, nxt = fgt[3], fgt[0]
            for part in range(3):
                dst = f_split[32 * part:32 * part + HEADS, :]
                if part == 2:
                    dve.tensor_copy(dst, cur).then_inc(S["f_ready"], 1)
                else:
                    step(dve.tensor_copy(dst, cur))
                    step(dve.tensor_copy(fgt[1], dst))
                    step(dve.tensor_tensor(nxt, cur, fgt[1], ALU.subtract))
                    cur, nxt = nxt, fgt[2]

            for kind, m in FRONT[10:]:
                (mod_piece if kind == "mod" else win_low)(m)
            dve.wait_ge(S["mod_up"], 6)
            for pos in range(2, 6):
                mod_column(pos)
            dve.wait_ge(S["mod_ready"], 6)
            g_c, b_c = cols[:, COL_LNG:COL_LNG + KT], cols[:, COL_LNB:COL_LNB + KT]
            sc_c, sh_c = modc[:, SC_F * KT:(SC_F + 1) * KT], modc[:, SH_F * KT:(SH_F + 1) * KT]
            dve.tensor_tensor(in2[:, 0, :], g_c, sc_c, ALU.mult)
            step(dve.tensor_tensor(in2[:, 1, :], b_c, sc_c, ALU.mult))
            dve.tensor_tensor(in2[:, 1, :], in2[:, 1, :], sh_c, ALU.add).then_inc(S["mod_ready"], 1)
            for r in range(TB):
                dve.wait_ge(S["unit_ready"], 4 * GATE + r + 1)
                step(dve.tensor_scalar(gate[:, r, :], gate[:, r, :], 1.0, None, ALU.add))
                dve.reciprocal(gate[:, r, :], gate[:, r, :]).then_inc(S["gate_ready"], 1)
            dve.wait_ge(S["rows_turned"], 1)
            dve.tensor_copy(mod_rows, ps[0:N_ROWS * KT, 7, 0:P]).then_inc(S["rows_copied"], 1)

            def clamp(h, n):
                dve.wait_ge(S["z_ready"], 3 * h + n + 1)
                dve.tensor_scalar(sp_part[n], z_part[n], BIG_Z, None, ALU.min).then_inc(S["clamped"], 1)

            def softplus(h, n):
                dve.wait_ge(S["sp_log"], 3 * h + n + 1)
                dve.tensor_tensor(sp_part[n], z_part[n], sp_part[n], ALU.max).then_inc(S["sp_ready"], 1)

            def row_max(h, b):
                dve.wait_ge(S["s_ready"], 4 * h + b + 1)
                dve.tensor_reduce(nmax[:, h % 2, b:b + 1], ps[:, b % 2, 0:(b + 1) * P], AX_X, ALU.max,
                                  negate=True).then_inc(S["max_ready"], 1)

            def turned(h, b):
                dve.wait_ge(S["t_up"], 4 * h + b + 1)
                dve.tensor_copy(pT[b], ps[:, 2, 0:(b + 1) * P]).then_inc(S["pT_ready"], 1)

            def rms_sum(kind, h):
                n = 2 * h + kind
                t = rms_t[:, n % 2]
                dve.wait_ge(S["fox_sq"] if kind == 0 else S["sb_sq"], h + 1)
                src = (sq_fox, sq_sb)[kind].rearrange("p (b n) -> p b n", b=TB)
                step(dve.tensor_reduce(t[:, 0, :], src, AX_X, ALU.add))
                if kind == 0:
                    l = lsum[:, h, :]
                    step(dve.scalar_tensor_tensor(out=lsum[:, h, :], in0=l, scalar=RMS_EPS, in1=l, op0=ALU.mult,
                                                  op1=ALU.mult))
                    dve.scalar_tensor_tensor(out=t[:, 1, :], in0=t[:, 0, :], scalar=1.0 / HD, in1=l,
                                             op0=ALU.mult, op1=ALU.add).then_inc(S["rms_ask"], 1)
                else:
                    dve.tensor_scalar(t[:, 1, :], t[:, 0, :], 1.0 / HD, RMS_EPS, ALU.mult, ALU.add
                                      ).then_inc(S["rms_ask"], 1)

            def rms_scale(kind, h):
                n = 2 * h + kind
                dve.wait_ge(S["rms_got"], n + 1)
                src = ps[:, (FOX_OUT, SB_OUT)[kind], 0:256].rearrange("p (b n) -> p b n", b=TB)
                dst = o_tok[:, :, kind * DG + h * HD:kind * DG + (h + 1) * HD]
                dve.tensor_tensor(dst, src, rms_t[:, n % 2, 2, :].unsqueeze(2).broadcast_to([P, TB, HD]), ALU.mult
                                  ).then_inc(S["fox_freed"] if kind == 0 else S["sb_freed"], 1)

            for h in range(HEADS):
                for n in range(3):
                    clamp(h, n)
                row_max(h, 0)
                row_max(h, 1)
                if h:
                    rms_sum(0, h - 1)
                turned(h, 0)
                softplus(h, 0)
                if h:
                    rms_scale(0, h - 1)
                row_max(h, 2)
                turned(h, 1)
                if h:
                    rms_sum(1, h - 1)
                softplus(h, 1)
                softplus(h, 2)
                row_max(h, 3)
                if h:
                    rms_scale(1, h - 1)
                turned(h, 2)
                turned(h, 3)
            for kind in range(2):
                rms_sum(kind, HEADS - 1)
                rms_scale(kind, HEADS - 1)

            for t in range(KT):
                dve.wait_ge(S["oT_high"], t + 1)
                dve.scalar_tensor_tensor(out=oT_split[1][:, t, :], in0=ps[:, t % 4, :],
                                         scalar=cols[:, COL_ONG + t:COL_ONG + t + 1], in1=as_f32(oT_split[0][:, t, :]),
                                         op0=ALU.mult, op1=ALU.subtract).then_inc(S["oT_ready"], 1)

            def normalise(b, ask, got):
                for half in range(2):
                    ins = dve.bn_stats(stats[:, half, :], resid[:, b, half * 512:(half + 1) * 512])
                step(ins)
                step(dve.bn_aggr(mv[:, b, :], stats[:].rearrange("p a n -> p (a n)")))
                dve.tensor_scalar(rstd[:, 0, b:b + 1], mv[:, b, 1:2], LN_EPS, None, ALU.add).then_inc(ask, 1)
                dve.wait_ge(got, b + 1)

            def first_norm(b):
                bank = 6 - 2 * (b % 2)
                dve.wait_ge(S["y_up"], b + 1)
                ins = dve.tensor_tensor(ln_tmp, ps[:, bank:bank + 2, :].rearrange("p a n -> p (a n)"), ga_row,
                                        ALU.mult)
                ins.then_inc(S["ln_freed"], 1)
                dve.wait_ge(S["ln_freed"], b + 1)
                if b == 0:
                    dve.wait_ge(S["xr_landed"], 16)
                step(dve.scalar_tensor_tensor(out=resid[:, b, :], in0=resid[:, b, :], scalar=ALPHA, in1=ln_tmp,
                                              op0=ALU.mult, op1=ALU.add))
                normalise(b, S["ln_ask"], S["ln_got"])
                dve.tensor_scalar(resid[:, b, :], resid[:, b, :], mv[:, b, 0:1], rstd[:, 1, b:b + 1],
                                  ALU.subtract, ALU.mult).then_inc(S["normed"], 1)

            def u2_half(b):
                dve.wait_ge(S["nT_up"], 2 * b + 2)
                for t in range(4, KT):
                    ins = dve.tensor_scalar(u2T[:, t, b * P:(b + 1) * P], ps[:, 1, (t - 4) * P:(t - 3) * P],
                                            in2[:, 0, t:t + 1], in2[:, 1, t:t + 1], ALU.mult, ALU.add)
                ins.then_inc(S["u2T_ready_d"], 1)

            dve.wait_ge(S["ga_landed"], 16)
            first_norm(0)
            for b in range(1, TB):
                first_norm(b)
                u2_half(b - 1)
            u2_half(TB - 1)

            dve.wait_ge(S["logits_up"], TB)
            dve.wait_ge(S["rconst"], 1)
            dve.wait_ge(S["br_landed"], 16)

            def v3(a, s=E):
                return a.rearrange("p (b e) -> p b e", e=s)

            def wide(a, s=E):
                return a.unsqueeze(2).broadcast_to([P, a.shape[1], s])

            def over_b(a):
                return a.unsqueeze(1).broadcast_to([P, TB, a.shape[1]])

            m4, n16 = rout[:, 0:TB], rout[:, 16:16 + TB * GROUPS]
            logits = ps[:, 2, 0:TB * E]
            step(dve.tensor_reduce(m4, v3(logits), AX_X, ALU.max))
            dve.tensor_tensor(v3(prob), v3(logits), wide(m4), ALU.subtract).then_inc(S["rcopy_ready"], 1)
            dve.wait_ge(S["rexp"], 1)
            step(dve.tensor_reduce(m4, v3(prob), AX_X, ALU.add))
            step(dve.reciprocal(rout[:, 4:8], m4))
            step(dve.tensor_tensor(v3(prob), v3(prob), wide(rout[:, 4:8]), ALU.mult))
            step(dve.tensor_tensor(v3(sel), v3(prob), over_b(b_rout), ALU.add))
            s4 = v3(sel, EPG)
            n = TB * GROUPS
            dve.tensor_tensor(pair6[:, :, 0:3], s4[:, :, 1:4], s4[:, :, 0:1].broadcast_to([P, n, 3]), ALU.add)
            dve.tensor_tensor(pair6[:, :, 3:5], s4[:, :, 2:4], s4[:, :, 1:2].broadcast_to([P, n, 2]), ALU.add)
            step(dve.tensor_tensor(pair6[:, :, 5:6], s4[:, :, 3:4], s4[:, :, 2:3], ALU.add))
            step(dve.tensor_reduce(gscore, pair6, AX_X, ALU.max))

            def first_largest(dst, vals, tie, size):
                step(dve.tensor_reduce(m4, v3(vals, size), AX_X, ALU.max))
                step(dve.tensor_tensor(v3(dst, size), v3(vals, size), wide(m4, size), ALU.is_equal))
                step(dve.tensor_tensor(v3(dst, size), v3(dst, size), over_b(tie), ALU.mult))
                step(dve.tensor_reduce(m4, v3(dst, size), AX_X, ALU.max))
                step(dve.tensor_tensor(v3(dst, size), v3(dst, size), wide(m4, size), ALU.is_equal))

            first_largest(ghot, gscore, tie_g, GROUPS)
            step(dve.tensor_scalar(gtie, ghot, -NEG, NEG, ALU.mult, ALU.add))
            step(dve.tensor_tensor(v3(selm, EPG), s4, wide(ghot, EPG), ALU.mult))
            step(dve.tensor_tensor(v3(selm, EPG), v3(selm, EPG), wide(gtie, EPG), ALU.add))
            first_largest(hot[0], selm, tie_e, E)
            step(dve.scalar_tensor_tensor(out=selm, in0=hot[0], scalar=2.0 * NEG, in1=selm, op0=ALU.mult,
                                          op1=ALU.add))
            first_largest(hot[1], selm, tie_e, E)
            dve.tensor_tensor(chosen, v3(hot[0]), v3(hot[1]), ALU.add).then_inc(S["routed_hot"], 1)
            weights = small[:, 16:16 + 2 * TB]
            for k in range(2):
                step(dve.tensor_tensor(score, hot[k], prob, ALU.mult))
                step(dve.tensor_reduce(rout[:, 32 + 4 * k:36 + 4 * k], v3(score), AX_X, ALU.add))
            step(dve.tensor_tensor(m4, rout[:, 32:36], rout[:, 36:40], ALU.add))
            step(dve.reciprocal(rout[:, 4:8], m4))
            for k in range(2):
                dve.tensor_tensor(weights[:, k * TB:(k + 1) * TB], rout[:, 32 + 4 * k:36 + 4 * k],
                                  rout[:, 4:8], ALU.mult)

            def overflow(dst, src):
                op = ALU.is_ge if dst is where[1] else ALU.is_gt
                step(dve.tensor_scalar(dst, src, float(FC), None, op))
                for k in (2, 3):
                    step(dve.scalar_tensor_tensor(out=dst, in0=src, scalar=float(k * FC), in1=dst, op0=op,
                                                  op1=ALU.add))

            dve.wait_ge(S["rank_up"], 1)
            count, more, base, upto = (rout[:, 64 + 16 * n:80 + 16 * n] for n in range(4))
            one16 = rout[:, 144:160]
            rank = score
            dve.memset(one16, 1.0)
            dve.tensor_copy(rank, ps[:, 3, 0:TB * E])
            step(dve.tensor_copy(count, ps[:, 3, TB * E:TB * E + E]))
            overflow(more, count)
            step(dve.tensor_scalar(base, more, 1.0, None, ALU.add))
            step(dve.tensor_tensor_scan(upto, one16, base, 0.0, ALU.mult, ALU.add))
            step(dve.tensor_tensor(base, upto, base, ALU.subtract))
            of_chunk = RV[0:1, 512:512 + G_COL * E].rearrange("p (c e) -> p c e", e=E)
            step(dve.tensor_tensor(of_chunk, iota_r[0:1, 0:G_COL].unsqueeze(2).broadcast_to([1, G_COL, E]),
                                   upto[0:1, :].unsqueeze(1).broadcast_to([1, G_COL, E]), ALU.is_ge))
            step(dve.tensor_reduce(rout[0:1, 192:192 + G_COL], of_chunk, AX_X, ALU.add))
            dve.tensor_scalar(table[0:1, 0:G_COL], rout[0:1, 192:192 + G_COL], float(E - 1), None, ALU.min)
            step(dve.tensor_scalar(table[0:1, G_COL:G_COL + 1], upto[0:1, E - 1:E], -1.0, None, ALU.add))
            overflow(where[1], rank)
            step(dve.scalar_tensor_tensor(out=where[0], in0=where[1], scalar=-float(FC), in1=rank, op0=ALU.mult,
                                          op1=ALU.add))
            step(dve.tensor_tensor(v3(where[1]), v3(where[1]), over_b(base), ALU.add))
            pos8, chunk8, dest8 = rout[:, 160:168], rout[:, 168:176], rout[:, 176:184]
            for k in range(2):
                for dst, val in ((pos8, where[0]), (chunk8, where[1])):
                    step(dve.tensor_tensor(selm, hot[k], val, ALU.mult))
                    step(dve.tensor_reduce(dst[:, k * TB:(k + 1) * TB], v3(selm), AX_X, ALU.add))
            dve.tensor_tensor(slot_hot, iota_r.unsqueeze(1).broadcast_to([P, 2 * TB, P]), wide(pos8, P), ALU.is_equal)
            nch = MAX_CHUNKS + 1
            step(dve.tensor_tensor(chunk_tok, iota_r[:, 0:nch].unsqueeze(1).broadcast_to([P, 2 * TB, nch]),
                                   wide(chunk8, nch), ALU.is_equal))
            for k in range(2):
                ins = dve.tensor_tensor(chunk_tok[:, k * TB:(k + 1) * TB, :], chunk_tok[:, k * TB:(k + 1) * TB, :],
                                        wide(tok_id, nch), ALU.mult)
            step(ins)
            step(dve.scalar_tensor_tensor(out=dest8, in0=chunk8, scalar=float(FC), in1=pos8, op0=ALU.mult,
                                          op1=ALU.add))
            step(dve.tensor_scalar(dest8, dest8, float(FC), None, ALU.add))
            step(dve.tensor_copy(dest[:], dest8))
            dve.nop().then_inc(S["slots_ready"], 1)
            dve.wait_ge(S["idx_up"], 1)
            step(dve.tensor_copy(row_idx[:], ps[:, 3, 128:128 + nch]))
            dve.nop().then_inc(S["idx_now"], 1)
            dve.nop().then_inc(S["tables_ready"], 1)

            def low(turn, j):
                n0 = j if turn is None else GU_PIECES + j
                dve.wait_ge(S["split_h"], n0 + 1 if turn is None else CHUNK_PIECES * turn + n0 + 1)
                dve.tensor_tensor(split_piece(n0 % SPLIT_SLOTS, 1), raw_piece(n0 % RAW_SLOTS),
                                  as_f32(split_piece(n0 % SPLIT_SLOTS, 0)), ALU.subtract).then_inc(S["split_l"], 1)

            def turned_low(high, count, part, done):
                dve.wait_ge(high, count)
                dve.tensor_tensor(re_part(part + 1), wide_bank(6), as_f32(re_part(part)), ALU.subtract).then_inc(done, 1)

            def hidden(count):
                dve.wait_ge(S["silu_done"], count)
                dve.tensor_tensor(h_tok, silu, wide_bank(2), ALU.mult).then_inc(S["h_ready"], 1)

            def result(used, stored):
                dve.wait_ge(S["piece_used"], used)
                dve.wait_ge(S["rows_stored"], stored)
                dve.tensor_tensor(rows_out, wide_bank(4), gf_row, ALU.mult).then_inc(S["y_out"], 1)

            turned_low(S["xT_high"], 1, XH, S["xT_ready"])
            dve.wait_ge(S["split_l"], SPLIT_SLOTS)
            for j in range(SPLIT_SLOTS, GU_PIECES):
                low(None, j)
            hidden(1)
            turned_low(S["xT_high"], 2, XH, S["xT_ready"])
            dve.wait_ge(S["lnrow_landed"], 64)
            for b in range(TB):
                step(dve.scalar_tensor_tensor(out=resid[:, b, :], in0=resid[:, b, :], scalar=ALPHA,
                                              in1=ln_rows[0], op0=ALU.mult, op1=ALU.mult))
                step(dve.scalar_tensor_tensor(out=resid[:, b, :], in0=ln_rows[1], scalar=ALPHA,
                                              in1=resid[:, b, :], op0=ALU.mult, op1=ALU.add))

            dve.wait_ge(S["gf_landed"], 16)
            last = dve.value_load(table[0:1, G_COL:G_COL + 1], min_val=E - 1, max_val=MAX_CHUNKS - 1)
            with dve.Fori(0, last) as i:
                for j in range(4):
                    low(i, j)
                result(CHUNK_PIECES * i + GU_PIECES, 16 * i + 16)
                turned_low(S["hT_high"], i + 1, HH, S["hT_ready"])
                for j in range(4, CHUNK_PIECES):
                    low(i, j)
                hidden(i + 2)
                turned_low(S["xT_high"], i + 3, XH, S["xT_ready"])
            for j in range(DN_PIECES):
                low(last, j)
            result(CHUNK_PIECES * last + GU_PIECES, 16 * last + 16)
            turned_low(S["hT_high"], last + 1, HH, S["hT_ready"])
            result(CHUNK_PIECES * last + CHUNK_PIECES, 16 * last + 32)

            def combine(b):
                for k in range(2):
                    dve.wait_ge(back_landed[2 * b + k], 16)
                    step(dve.scalar_tensor_tensor(out=resid[:, b, :], in0=back[k][b],
                                                  scalar=weights[:, k * TB + b:k * TB + b + 1], in1=resid[:, b, :],
                                                  op0=ALU.mult, op1=ALU.add))
                normalise(b, S["fin_ask"], S["fin_got"])
                step(dve.tensor_scalar(back[0][b], resid[:, b, :], mv[:, b, 0:1], rstd[:, 1, b:b + 1],
                                       ALU.subtract, ALU.mult))
                step(dve.tensor_tensor(back[0][b], back[0][b], ln_rows[2], ALU.mult))
                dve.tensor_tensor(back[0][b], back[0][b], ln_rows[3], ALU.add).then_inc(S["fin_done"], 1)

            for b in range(TB):
                combine(b)


_INS = ['x', 'c', 'w_mod', 'b_mod', 'w_in', 'b_forget', 'out_norm_g', 'w_out', 'ln1_g', 'ln1_b',
        'w_router', 'b_router', 'w_gate', 'w_up', 'w_down', 'ln2_g', 'ln2_b']


def kernel(**inputs):
    import numpy as _np
    import concourse.bacc as _bacc
    from concourse import mybir as _mybir
    from concourse.bass_utils import run_bass_kernel_spmd as _run

    nc = _bacc.Bacc("TRN2", target_bir_lowering=False, num_devices=1)
    arrays, args = {}, []
    for name in _INS:
        a = _np.ascontiguousarray(inputs[name])
        arrays[f"in_{name}_dram"] = a
        args.append(nc.dram_tensor(f"in_{name}_dram", a.shape, _mybir.dt.from_np(a.dtype), kind="ExternalInput").ap())
    out = nc.dram_tensor("out_0_dram", (1, T, D), _mybir.dt.float32, kind="ExternalOutput").ap()
    build(nc, *args, out)
    r = _run(nc, [arrays], core_ids=[0])
    return r.results[0]["out_0_dram"]
```

```python
from contextlib import ExitStack

import concourse.bass as bass
import concourse.mybir as mybir
from concourse.alu_op_type import AluOpType as ALU

ACT = mybir.ActivationFunctionType
AX_X = mybir.AxisListType.X
F32 = mybir.dt.float32
F32R = mybir.dt.float32r
BF16 = mybir.dt.bfloat16
I32 = mybir.dt.int32

P = 128
D = 1024
T = 512
KT = D // P
TB = T // P
HD = 64
HEADS = 8
DG = HEADS * HD
E = 16
EPG = 4
GROUPS = E // EPG
FC = P
MAX_CHUNKS = E + (2 * T - 1) // FC
ALPHA = 2.0 ** 0.25
LN_EPS = 1e-5
RMS_EPS = 1e-6
NEG = -1e30
BIG_Z = 40.0
PIECE = 2 * D
RAW_SLOTS = 6
SPLIT_SLOTS = 4
GU_PIECES = 8
DN_PIECES = 4
CHUNK_PIECES = GU_PIECES + DN_PIECES

SB_OFF = 4 * DG + HEADS
GROUP_COLS = [0, DG, SB_OFF, SB_OFF + DG, 3 * DG, 2 * DG, SB_OFF + 2 * DG]
FQ, FK, SQ, SK, GATE, FV, SV = range(7)
UNITS = 4 * len(GROUP_COLS)
WIN_PIECES = 2 * len(GROUP_COLS)

SH_A, SC_A, G_A, SH_F, SC_F, G_F = range(6)
MOD_ORDER = [SC_A, SH_A, G_A, SH_F, SC_F, G_F]

COL_BMOD, COL_C, COL_LNG, COL_LNB, COL_ONG, N_COLS = 0, 48, 56, 64, 72, 80
OT_ORDER = (0, 1, 2, 4, 5, 6, 3, 7)
G_COL = MAX_CHUNKS + 1
U2_SCALE, U2_SHIFT, N_ROWS = 6, 7, 8


def front_stream():
    order = [("mod", n) for n in range(8)] + [("win", 0), ("win", 1)]
    for n in range(2, WIN_PIECES):
        mods = range(2 * n + 4, min(2 * n + 6, 24))
        order += [("mod", m) for m in mods] + [("win", n)]
    return order


FRONT = front_stream()
MOD_BEFORE = {2 * pos - 1: pos for pos in range(2, 6)}
FRONT_AT = {item: n for n, item in enumerate(FRONT)}


def build(nc, x, c, w_mod, b_mod, w_in, b_forget, out_norm_g, w_out, ln1_g, ln1_b,
          w_router, b_router, w_gate, w_up, w_down, ln2_g, ln2_b, out):
    u2_dram = nc.dram_tensor("u2_rows", [T, D], F32).ap()
    mod_dram = nc.dram_tensor("mod_rows", [N_ROWS, D], F32).ap()
    result_dram = nc.dram_tensor("expert_rows", [(1 + MAX_CHUNKS) * FC, D], F32).ap()

    with ExitStack() as ctx:
        def sb(name, shape, dt=F32):
            return ctx.enter_context(nc.sbuf_tensor(name, shape, dt))

        def sem(name):
            return ctx.enter_context(nc.semaphore(name))

        sizes = dict(RAW=RAW_SLOTS * PIECE, SPLIT=SPLIT_SLOTS * 2 * PIECE, RQ=16 * T, RV=8 * T, RA=KT * T,
                     RE=KT * T, RG=4 * T)
        with ExitStack() as first_view:
            M = {name: first_view.enter_context(nc.sbuf_tensor(f"{name}_f32", [P, n], F32))
                 for name, n in sizes.items()}
        MR = {name: sb(f"{name}_f32r", [P, n], F32R) for name, n in sizes.items()}

        def region(view, name):
            return view[name][:, :]

        RAW, RQ, RV, RA, RG = (region(M, n) for n in ("RAW", "RQ", "RV", "RA", "RG"))
        RB = RAW

        def raw_piece(slot):
            return RAW[:, slot * PIECE:(slot + 1) * PIECE]

        def split_piece(slot, part):
            at = (2 * slot + part) * PIECE
            return region(MR, "SPLIT")[:, at:at + PIECE]

        def as_f32(a):
            return a.bitcast(F32)

        def tiles(a, c=KT):
            return a.rearrange("p (c t) -> p c t", c=c)

        uT_split = [tiles(region(MR, n)) for n in ("RA", "RE")]
        oT_split = [tiles(region(MR, "RE")), tiles(region(MR, "RQ")[:, 0:4096])]
        o_tok = tiles(RA, TB)
        u2T = tiles(RA)
        x_tok = tiles(RQ[:, 0:4096], TB)
        uT = tiles(RQ[:, 4096:8192])
        qf, kf, qs, ks = (tiles(RQ[:, n * 2048:(n + 1) * 2048], 4) for n in range(4))
        resid = tiles(RQ[:, 4096:8192], TB)
        vf, vs = (tiles(RV[:, n * 2048:(n + 1) * 2048], TB) for n in range(2))
        gate = tiles(RG[:, :], TB)

        def mod_sum(pos):
            return RG[:, pos % 2 * D:(pos % 2 + 1) * D]

        fgt = [RQ[0:HEADS, 6144 + n * T:6144 + (n + 1) * T] for n in range(4)]

        def packed(base, width):
            offs = [base + sum(width(j) for j in range(i)) for i in range(TB)]
            return [RB[:, offs[i]:offs[i] + width(i)] for i in range(TB)]

        sp = packed(0, lambda i: (TB - i) * P)
        wT = packed(1280, lambda i: (TB - i) * P)
        pr = packed(2560, lambda b: (b + 1) * P)
        pT = packed(3840, lambda b: (b + 1) * P)
        sp_split = [[region(MR, "RE")[:, n * 1280 + at:n * 1280 + at + (TB - i) * P]
                     for i, at in enumerate((0, 512, 896, 1152))] for n in range(2)]
        tri_made, ones_made = (region(M, "RE")[:, n * P:(n + 1) * P] for n in range(2))
        def span(n):
            return slice(0, 3 * P) if n == 0 else slice(0, (n + 2) * P)

        sp_part, sp_split_part, wT_part = ([], [], [])
        for n in range(3):
            at = (896, 512, 0)[n]
            sp_part.append(RB[:, at:at + span(n).stop])
            wT_part.append(RB[:, 1280 + at:1280 + at + span(n).stop])
            sp_split_part.append([region(MR, "RE")[:, k * 1280 + at:k * 1280 + at + span(n).stop] for k in range(2)])
        sq_fox = RB[:, 5120:5376]
        sq_sb = RB[:, 5376:5632]
        zeros = RB[:, 5632:6144]
        ga_row = RB[:, 6144:7168]
        mod_rows = RB[0:N_ROWS * KT, 7168:7168 + P]
        ln_tmp = RV[:, 0:D]
        u2_rows = [RAW[:, 8192 + n * D:8192 + (n + 1) * D] for n in range(2)]
        u2_tok = [RAW[:, 10240 + n * D:10240 + (n + 1) * D] for n in range(2)]

        rows_in, h_tok, rows_out = (RA[:, n * D:(n + 1) * D] for n in range(3))
        silu, gf_row = (RQ[:, n * D:(n + 1) * D] for n in range(2))

        def re_part(n):
            return region(MR, "RE")[:, n * D:(n + 1) * D]

        XH, XL, HH, HL = range(4)
        ln_rows = [RV[:, n * D:(n + 1) * D] for n in range(4)]
        back = [[RAW[:, (4 * k + b) * D:(4 * k + b + 1) * D] for b in range(TB)] for k in range(2)]

        used = [0]

        def rt(n, *shape):
            a = RG[:, used[0]:used[0] + n]
            used[0] += n
            return a

        slot_hot = region(MR, "RG")[:, 0:1024].rearrange("p (k s) -> p k s", k=2 * TB)
        used[0] = 1024 + 2 * TB * (MAX_CHUNKS + 1)
        chunk_tok = region(MR, "RG")[:, 1024:used[0]].rearrange("p (k s) -> p k s", k=2 * TB)
        prob, sel, selm, score = (rt(TB * E) for _ in range(4))
        hot = [rt(TB * E) for _ in range(2)]
        pair6 = rt(TB * GROUPS * 6).rearrange("p (g s) -> p g s", s=6)
        gscore, ghot, gtie = (rt(TB * GROUPS) for _ in range(3))
        where = [rt(TB * E) for _ in range(2)]
        rout = RV[:, 0:512]

        ident = sb("ident", [P, P])
        ident_b = sb("ident_b", [P, P], BF16)
        mask_fox = sb("mask_fox", [P, P], BF16)
        mask_sb = sb("mask_sb", [P, P], BF16)
        neg_tri = sb("neg_tri", [P, P], F32R)
        neg_ones = sb("neg_ones", [P, P], F32R)
        one_col = sb("one_col", [P, 1])
        before = ident_b
        head_sel = sb("head_sel", [P, HEADS, P], BF16)
        f_split = sb("f_split", [P, T], BF16)
        col_stage = sb("col_stage", [N_COLS, P])
        cols = sb("cols", [P, N_COLS])
        modc = sb("modc", [P, N_ROWS * KT])
        cond = sb("cond", [P, 3, KT])
        w_forget = sb("w_forget", [P, KT, HEADS])
        bf_col = sb("bf_col", [HEADS, 1])
        lsum = sb("lsum", [P, HEADS, TB])
        nmax = sb("nmax", [P, 2, TB])
        rms_t = sb("rms_t", [P, 2, 3, TB])
        neg_half = sb("neg_half", [P, TB])
        stats = sb("stats", [P, 2, 6])
        mv = sb("mv", [P, TB, 2])
        rstd = sb("rstd", [P, 2, TB])
        in2 = modc[:, U2_SCALE * KT:(U2_SHIFT + 1) * KT].rearrange("p (a c) -> p a c", a=2)
        wr = f_split[:, 0:2 * KT * E].bitcast(F32).rearrange("p (c e) -> p c e", c=KT)
        small = sb("small", [P, 64])
        table = sb("table", [1, 64], I32)
        row_idx = sb("row_idx", [P, MAX_CHUNKS + 1], I32)
        row_now = sb("row_now", [P, 1], I32)
        dest = sb("dest", [P, 2 * TB], I32)
        ps = ctx.enter_context(nc.psum_tensor("ps", [P, 8, 512], F32))

        Z_AT = [(4, 0), (5, 0), (6, 0), (6, 2 * P)]
        z_part = [ps[:, (6, 5, 4)[n], span(n)] for n in range(3)]

        def wide_bank(n):
            return ps[:, n:n + 2, :].rearrange("p a n -> p (a n)")

        def mod_bank(pos):
            return 7 if pos < 2 else 6

        FOX_OUT, SB_OUT = 3, 7

        iota_r = head_sel[:, 0:2, :].rearrange("p h n -> p (h n)").bitcast(F32)
        iota_i = head_sel[:, 2:4, :].rearrange("p h n -> p (h n)").bitcast(I32)
        one_b = head_sel[:, 4, :]
        chosen = head_sel[:, 5, 0:TB * E].rearrange("p (b e) -> p b e", b=TB)
        fl = head_sel[:, 6:8, :].rearrange("p h n -> p (h n)").bitcast(F32)
        tie_e, tie_g, tok_id = fl[:, 0:E], fl[:, 16:16 + GROUPS], fl[:, 32:32 + TB]
        b_rout = fl[:, 48:48 + E]
        tok_i = fl[:, 64:64 + TB].bitcast(I32)

        S = {}
        for name in """rows_landed x_landed wf_landed bf_landed xr_landed br_landed wr_landed
            lnrow_landed lnrow0_landed consts cols_up cols_ready cond_exp cond_ready mod_summed mod_up mod_ready
            xT_up uT_ready f_up f_abs f_exp f_ready unit_done unit_ready gate_ready
            z_ready clamped sp_log sp_ready r_ready stick_ready
            s_ready max_ready prob_ready t_up pT_ready fox_ready sb_ready
            fox_sq sb_sq rms_ask rms_got fox_freed sb_freed fox_gated qk_dead
            oT_up oT_ready y_up ln_freed ln_ask ln_got normed
            nT_up u2T_ready logits_up rcopy_ready rank_up idx_up
            rconst routed_hot tables_ready idx_now dest_ready rexp slots_ready prob_e
            gathered rows_up xT_high xT_ready silu_done h_ready h_up hT_high hT_ready y_out rows_stored
            front_split_h front_freed first_half_used uT_high uT_split_done rows_turned rows_copied mod_stored x1_ready fin_scaled
            ga_landed u2row_landed gf_landed wout_split wout_free raw_freed split_h split_l piece_used u2_made oT_high
            sp_exp row_set spare_cleared uT_ready_d gather_go u2T_ready_d fin_ask fin_got fin_shift out_stored dve_step act_step pool_step""".split():
            S[name] = sem(name)
        front_landed = [sem(f"front_landed_{s}") for s in range(RAW_SLOTS)]
        wout_landed = [sem(f"wout_landed_{s}") for s in range(2)]
        fin_done = [sem(f"fin_done_{s}") for s in range(TB)]
        u2_stored = [sem(f"u2_stored_{s}") for s in range(2)]
        raw_landed = [sem(f"raw_landed_{s}") for s in range(RAW_SLOTS)]
        back_landed = [sem(f"back_landed_{s}") for s in range(2 * TB)]

        w_mod_v = w_mod[0].rearrange("(c p) n -> p c n", p=P)
        w_in_v = w_in[0].rearrange("(c p) n -> p c n", p=P)
        w_out_v = w_out[0].rearrange("(c p) n -> p c n", p=P)
        x_v = x[0].rearrange("(b p) n -> p b n", p=P)
        out_v = out[0].rearrange("(b p) n -> p b n", p=P)
        u2_v = u2_dram.rearrange("(b p) n -> p b n", p=P)

        def piece_source(w, e, n):
            return w[0, e, 2 * n * P:(2 * n + 2) * P, :].rearrange("(c p) n -> p c n", p=P)

        block = ctx.enter_context(nc.Block())

        def load_rows(engine, rows):
            for r0, src in rows:
                n = src.shape[1] // P
                engine.dma_start(col_stage[r0:r0 + n, :], src.rearrange("a (r n) -> (a r) n", n=P)
                                 ).then_inc(S["rows_landed"], 16)

        @block.sync
        def _(sp_):
            load_rows(sp_, ((COL_C, c), (COL_BMOD, b_mod)))

            for n, (kind, m) in enumerate(FRONT):
                if n == 3:
                    sp_.dma_start(x_tok, x_v).then_inc(S["x_landed"], 16)
                if n >= RAW_SLOTS:
                    sp_.wait_ge(S["front_freed"], n - RAW_SLOTS + 1)
                if kind == "mod":
                    seg, part = MOD_ORDER[m // 4], m % 4
                    src = w_mod_v[:, 2 * part:2 * part + 2, seg * D:(seg + 1) * D]
                    dst = tiles(raw_piece(n % RAW_SLOTS), 2)
                else:
                    col = GROUP_COLS[m // 2]
                    src = w_in_v[:, 4 * (m % 2):4 * (m % 2) + 4, col:col + DG]
                    dst = tiles(raw_piece(n % RAW_SLOTS), 4)
                sp_.dma_start(dst, src).then_inc(front_landed[n % RAW_SLOTS], 16)

            sp_.wait_ge(S["front_freed"], len(FRONT))
            for n in range(4):
                if n >= 2:
                    sp_.wait_ge(S["wout_split"], 2 * (n - 1))
                sp_.dma_start(tiles(raw_piece(4 + n % 2), 2), w_out_v[:, 2 * n:2 * n + 2, :]
                              ).then_inc(wout_landed[n % 2], 16)
                if n == 1:
                    sp_.wait_ge(S["mod_stored"], 16)
                    sp_.dma_start(ga_row, mod_dram[G_A:G_A + 1, :].to_broadcast([P, D])
                                  ).then_inc(S["ga_landed"], 16)
            sp_.wait_ge(S["qk_dead"], 1)
            sp_.dma_start(resid, x_v).then_inc(S["xr_landed"], 16)
            sp_.wait_ge(S["wout_split"], 8)
            for n in range(2):
                sp_.dma_start(u2_rows[n], mod_dram[U2_SCALE + n:U2_SCALE + n + 1, :].to_broadcast([P, D])
                              ).then_inc(S["u2row_landed"], 16)

            def load_piece(slot, w, e, m):
                sp_.dma_start(tiles(raw_piece(slot), 2),
                              w[0, e, :, :].rearrange("(c p) n -> p c n", p=P)[:, 2 * m:2 * m + 2, :]
                              ).then_inc(raw_landed[slot], 16)

            def load_gate_up(e, j, slot):
                load_piece(slot, (w_gate, w_up)[j % 2], e, j // 2)

            sp_.wait_ge(S["fox_freed"], HEADS)
            sp_.wait_ge(S["sb_freed"], HEADS)
            sp_.wait_ge(S["spare_cleared"], 16)
            for j in range(3):
                load_gate_up(0, j, j)
            for n, src in ((1, ln1_b), (2, ln2_g), (3, ln2_b)):
                sp_.dma_start(ln_rows[n], src.to_broadcast([P, D])).then_inc(S["lnrow_landed"], 16)
            sp_.wait_ge(S["ln_ask"], TB)
            load_gate_up(0, 3, 3)
            sp_.wait_ge(S["y_up"], TB)
            sp_.dma_start(gf_row, mod_dram[G_F:G_F + 1, :].to_broadcast([P, D])).then_inc(S["gf_landed"], 16)
            sp_.wait_ge(S["u2_made"], TB)
            load_gate_up(0, 4, 4)
            for n in range(2):
                sp_.wait_ge(u2_stored[n], 32)
            load_gate_up(0, 5, 5)
            for j in range(6, GU_PIECES):
                sp_.wait_ge(S["split_l"], j + 1 - RAW_SLOTS)
                load_gate_up(0, j, j % RAW_SLOTS)

            sp_.wait_ge(S["tables_ready"], 1)
            last = sp_.value_load(table[0:1, G_COL:G_COL + 1], min_val=E - 1, max_val=MAX_CHUNKS - 1)
            with sp_.Fori(0, last) as i:
                e_next = sp_.value_load(table[0:1, bass.ds(i + 1, 1)], min_val=0, max_val=E - 1)
                for j in range(GU_PIECES):
                    sp_.wait_ge(S["split_l"], CHUNK_PIECES * i + GU_PIECES + j + 1 - RAW_SLOTS)
                    load_gate_up(e_next, j, (GU_PIECES + j) % RAW_SLOTS)
                e_now = sp_.value_load(table[0:1, bass.ds(i, 1)], min_val=0, max_val=E - 1)
                for j in range(GU_PIECES, CHUNK_PIECES):
                    sp_.wait_ge(S["split_l"], CHUNK_PIECES * i + GU_PIECES + j + 1 - RAW_SLOTS)
                    load_piece((GU_PIECES + j) % RAW_SLOTS, w_down, e_now, j - GU_PIECES)
            e_last = sp_.value_load(table[0:1, bass.ds(last, 1)], min_val=0, max_val=E - 1)
            for j in range(DN_PIECES):
                sp_.wait_ge(S["split_l"], CHUNK_PIECES * last + GU_PIECES + j + 1 - RAW_SLOTS)
                load_piece((GU_PIECES + j) % RAW_SLOTS, w_down, e_last, j)
            for b in range(TB):
                sp_.wait_ge(fin_done[b], 1)
                sp_.dma_start(out_v[:, b, :], back[0][b]).then_inc(S["out_stored"], 16)
            sp_.wait_ge(S["out_stored"], 16 * TB)

        @block.gpsimd
        def _(pool):
            steps = [0]

            def step(ins):
                steps[0] += 1
                ins.then_inc(S["pool_step"], 1)
                pool.wait_ge(S["pool_step"], steps[0])

            pool.memset(ident[:], 0.0)
            pool.memset(ident_b[:], 0.0)
            pool.memset(mask_fox[:], 0.0)
            pool.memset(mask_sb[:], 0.0)
            pool.memset(tri_made, -1.0)
            pool.memset(ones_made, -1.0)
            pool.memset(one_col[:], 1.0)
            pool.memset(neg_half[:], -0.5)
            pool.memset(f_split[:], 0.0)
            step(pool.memset(head_sel[:], 0.0))
            pool.affine_select(out=ident[:], in_=ident[:], compare_op=ALU.not_equal, fill=1.0, base=0,
                               pattern=[[-1, P]], channel_multiplier=1)
            pool.affine_select(out=ident_b[:], in_=ident_b[:], compare_op=ALU.not_equal, fill=1.0, base=0,
                               pattern=[[-1, P]], channel_multiplier=1)
            pool.affine_select(out=mask_fox[:], in_=mask_fox[:], compare_op=ALU.is_ge, fill=NEG, base=0,
                               pattern=[[-1, P]], channel_multiplier=1)
            pool.affine_select(out=mask_sb[:], in_=mask_sb[:], compare_op=ALU.is_ge, fill=NEG, base=-1,
                               pattern=[[1, P]], channel_multiplier=-1)
            pool.affine_select(out=tri_made, in_=tri_made, compare_op=ALU.is_ge, fill=0.0, base=0,
                               pattern=[[-1, P]], channel_multiplier=1)
            for part in range(3):
                step(pool.affine_select(out=head_sel[:], in_=head_sel[:], compare_op=ALU.not_equal, fill=1.0,
                                        base=-32 * part, pattern=[[-1, HEADS], [0, P]],
                                        channel_multiplier=1))
            pool.tensor_copy(neg_tri[:], tri_made)
            step(pool.tensor_copy(neg_ones[:], ones_made))
            pool.memset(small[:], 0.0).then_inc(S["consts"], 1)

            for m in range(2):
                n = FRONT_AT["win", m]
                pool.wait_ge(S["front_split_h"], m + 1)
                pool.wait_ge(S["front_freed"], n)
                pool.tensor_tensor(split_piece(m, 1), raw_piece(n % RAW_SLOTS), as_f32(split_piece(m, 0)),
                                   ALU.subtract).then_inc(S["front_freed"], 1)

            pool.wait_ge(S["rows_copied"], 1)
            pool.dma_start(mod_dram.rearrange("s (c p) -> (s c) p", p=P), mod_rows).then_inc(S["mod_stored"], 16)

            pool.wait_ge(S["front_freed"], len(FRONT))
            step(pool.memset(zeros, 0.0))
            pool.dma_start(result_dram[(E + 1) * FC:, :].rearrange("(p q) (h n) -> p (q h) n", p=P, n=512),
                           zeros.unsqueeze(1).broadcast_to([P, 2 * (MAX_CHUNKS - E), 512])
                           ).then_inc(S["spare_cleared"], 16)

            def rms_power(n):
                pool.wait_ge(S["rms_ask"], n + 1)
                pool.tensor_tensor(rms_t[:, n % 2, 2, :], rms_t[:, n % 2, 1, :], neg_half[:], ALU.pow
                                   ).then_inc(S["rms_got"], 1)

            def fox_gate(h):
                pool.wait_ge(S["fox_freed"], h + 1)
                pool.wait_ge(S["gate_ready"], TB)
                cs = slice(h * HD, (h + 1) * HD)
                pool.tensor_tensor(o_tok[:, :, cs], o_tok[:, :, cs], gate[:, :, cs], ALU.mult
                                   ).then_inc(S["fox_gated"], 1)

            def split_wout(h):
                n, cs = h // 2, slice(h % 2 * D, (h % 2 + 1) * D)
                pool.wait_ge(wout_landed[n % 2], 16 * (n // 2 + 1))
                pool.wait_ge(S["unit_done"], UNITS)
                raw = raw_piece(4 + n % 2)[:, cs]
                step(pool.tensor_copy(split_piece(n, 0)[:, cs], raw))
                pool.tensor_tensor(split_piece(n, 1)[:, cs], raw, as_f32(split_piece(n, 0)[:, cs]), ALU.subtract
                                   ).then_inc(S["wout_split"], 1)

            for h in range(HEADS):
                if h:
                    rms_power(2 * h - 2)
                    rms_power(2 * h - 1)
                    fox_gate(h - 1)
                split_wout(h)
            rms_power(2 * HEADS - 2)
            rms_power(2 * HEADS - 1)
            fox_gate(HEADS - 1)

            pool.wait_ge(S["oT_up"], 1)
            step(pool.iota(iota_i, [[1, P]], base=0, channel_multiplier=0))
            step(pool.iota(tok_i, [[P, TB]], base=0, channel_multiplier=1))
            pool.tensor_copy(iota_r, iota_i)
            pool.tensor_copy(tok_id, tok_i)
            pool.memset(one_b, 1.0)
            step(pool.memset(before[:], 1.0))
            step(pool.affine_select(out=before[:], in_=before[:], compare_op=ALU.is_ge, fill=0.0, base=-1,
                                    pattern=[[1, P]], channel_multiplier=-1))
            pool.tensor_scalar(tie_e, iota_r[:, 0:E], -1.0, float(E), ALU.mult, ALU.add)
            step(pool.tensor_scalar(tie_g, iota_r[:, 0:GROUPS], -1.0, float(GROUPS), ALU.mult, ALU.add))
            pool.dma_start(wr, w_router.rearrange("(c p) e -> p c e", p=P)).then_inc(S["wr_landed"], 16)
            pool.dma_start(b_rout, b_router.rearrange("(a e) -> a e", a=1).to_broadcast([P, E])
                           ).then_inc(S["br_landed"], 16)
            pool.memset(small[:], 0.0).then_inc(S["rconst"], 1)

            for b in range(TB):
                pool.wait_ge(S["ln_ask"], b + 1)
                pool.tensor_tensor(rstd[:, 1, b:b + 1], rstd[:, 0, b:b + 1], neg_half[:, 0:1], ALU.pow
                                   ).then_inc(S["ln_got"], 1)
                if b == 0:
                    pool.wait_ge(S["u2row_landed"], 32)
                if b >= 2:
                    pool.wait_ge(u2_stored[b % 2], 16)
                pool.wait_ge(S["normed"], b + 1)
                step(pool.tensor_tensor(u2_tok[b % 2], resid[:, b, :], u2_rows[0], ALU.mult))
                pool.tensor_tensor(u2_tok[b % 2], u2_tok[b % 2], u2_rows[1], ALU.add).then_inc(S["u2_made"], 1)
                pool.wait_ge(S["u2_made"], b + 1)
                pool.dma_start(u2_v[:, b, :], u2_tok[b % 2]).then_inc(u2_stored[b % 2], 16)

            for j in range(SPLIT_SLOTS):
                pool.wait_ge(S["split_h"], j + 1)
                pool.tensor_tensor(split_piece(j, 1), raw_piece(j), as_f32(split_piece(j, 0)), ALU.subtract
                                   ).then_inc(S["split_l"], 1)


            def gather():
                pool.indirect_dma_start(out=rows_in, out_offset=None, in_=u2_dram,
                                        in_offset=bass.IndirectOffsetOnAxis(ap=row_now[:], axis=0)
                                        ).then_inc(S["gathered"], 16)

            pool.wait_ge(S["idx_now"], 1)
            for n in range(2):
                pool.wait_ge(u2_stored[n], 32)
            pool.tensor_copy(row_now[:], row_idx[:, 0:1]).then_inc(S["row_set"], 1)
            pool.wait_ge(S["row_set"], 1)
            gather()

            def next_rows(chunk):
                pool.wait_ge(S["gathered"], 16 * chunk)
                pool.wait_ge(S["rows_up"], chunk)
                pool.tensor_copy(row_now[:], row_idx[:, bass.ds(chunk, 1)]).then_inc(S["row_set"], 1)
                pool.wait_ge(S["row_set"], chunk + 1)
                pool.sem_inc(S["gather_go"], 1)
                gather()

            next_rows(1)
            pool.wait_ge(S["tables_ready"], 1)
            pool.dma_start(ln_rows[0], ln1_g.to_broadcast([P, D])).then_inc(S["lnrow0_landed"], 16)
            next_rows(2)
            pool.wait_ge(S["lnrow_landed"], 48)
            pool.wait_ge(S["lnrow0_landed"], 16)
            pool.wait_ge(S["nT_up"], 2 * TB)
            step(pool.tensor_scalar(RV[:, 0:2 * D], RV[:, 0:2 * D], ALPHA, None, ALU.mult))
            for b in range(TB):
                step(pool.tensor_tensor(resid[:, b, :], resid[:, b, :], ln_rows[0], ALU.mult))
                ins = pool.tensor_tensor(resid[:, b, :], resid[:, b, :], ln_rows[1], ALU.add)
            ins.then_inc(S["x1_ready"], 1)
            last = pool.value_load(table[0:1, G_COL:G_COL + 1], min_val=E - 1, max_val=MAX_CHUNKS - 1)
            with pool.Fori(0, last - 1) as i:
                next_rows(i + 3)

            pool.wait_ge(S["rows_stored"], 16 * last + 48)
            pool.wait_ge(S["split_l"], CHUNK_PIECES * last + CHUNK_PIECES)
            pool.sem_inc(S["gather_go"], 1)
            for b in range(TB):
                for k in range(2):
                    pool.indirect_dma_start(out=back[k][b], out_offset=None, in_=result_dram,
                                            in_offset=bass.IndirectOffsetOnAxis(
                                                ap=dest[:, k * TB + b:k * TB + b + 1], axis=0)
                                            ).then_inc(back_landed[2 * b + k], 16)
            def deviation(b):
                pool.wait_ge(S["fin_ask"], b + 1)
                pool.tensor_tensor(rstd[:, 1, b:b + 1], rstd[:, 0, b:b + 1], neg_half[:, 0:1], ALU.pow
                                   ).then_inc(S["fin_got"], 1)

            deviation(0)
            pool.wait_ge(S["fin_scaled"], 1)
            step(pool.tensor_tensor(back[0][0], back[0][0], ln_rows[2], ALU.mult))
            deviation(1)
            pool.tensor_tensor(back[0][0], back[0][0], ln_rows[3], ALU.add).then_inc(fin_done[0], 1)
            deviation(2)
            pool.wait_ge(S["fin_scaled"], 2)
            step(pool.tensor_tensor(back[0][1], back[0][1], ln_rows[2], ALU.mult))
            deviation(3)
            pool.tensor_tensor(back[0][1], back[0][1], ln_rows[3], ALU.add).then_inc(fin_done[1], 1)

        @block.scalar
        def _(act):
            load_rows(act, ((COL_LNG, ln1_g), (COL_LNB, ln1_b), (COL_ONG, out_norm_g)))
            act.dma_start(w_forget[:], w_in_v[:, :, 4 * DG:4 * DG + HEADS]).then_inc(S["wf_landed"], 16)
            act.dma_start(bf_col[:], b_forget.rearrange("a h -> h a")).then_inc(S["bf_landed"], 16)
            act.preload_act_table_set("natural_log_exp_and_others")
            act.wait_ge(S["cols_ready"], 1)
            act.activation(cond[:, 0, :], cols[:, COL_C:COL_C + KT], ACT.Exp, scale=-1.0
                           ).then_inc(S["cond_exp"], 1)

            def win_high(m):
                n = FRONT_AT["win", m]
                act.wait_ge(front_landed[n % RAW_SLOTS], 16 * (n // RAW_SLOTS + 1))
                if m >= SPLIT_SLOTS:
                    g = (m - SPLIT_SLOTS) // 2
                    act.wait_ge(*((S["first_half_used"], g + 1) if m % 2 == 0 else (S["unit_done"], 4 * g + 4)))
                act.activation(split_piece(m % SPLIT_SLOTS, 0), raw_piece(n % RAW_SLOTS), ACT.Copy
                               ).then_inc(S["front_split_h"], 1)

            win_high(0)
            act.wait_ge(S["mod_ready"], 2)
            def uT_even(t):
                act.wait_ge(S["xT_up"], t + 1)
                act.activation(uT[:, t, :], ps[:, t % 7, :], ACT.Identity,
                               scale=modc[:, SC_A * KT + t:SC_A * KT + t + 1],
                               bias=modc[:, SH_A * KT + t:SH_A * KT + t + 1]).then_inc(S["uT_ready"], 1)

            def uT_high(t):
                act.wait_ge(S["uT_ready"], t // 2 + 1)
                act.wait_ge(S["uT_ready_d"], t // 2 + 1)
                act.activation(uT_split[0][:, t:t + 2, :], uT[:, t:t + 2, :], ACT.Copy).then_inc(S["uT_high"], 1)

            for t in (0, 4):
                uT_even(t)
                uT_even(t + 2)
                uT_high(t)
                uT_high(t + 2)

            def forget_log():
                act.wait_ge(S["f_abs"], 1)
                act.activation(fgt[1], fgt[1], ACT.Exp, scale=-1.0).then_inc(S["act_step"], 1)
                act.wait_ge(S["act_step"], 1)
                act.activation(fgt[1], fgt[1], ACT.Ln, bias=1.0).then_inc(S["f_exp"], 1)

            def unit_out(u):
                g, r = divmod(u, 4)
                if u == 4 * SK:
                    act.wait_ge(S["f_ready"], 1)
                if u == 4 * GATE:
                    act.wait_ge(S["mod_up"], 6)
                act.wait_ge(S["unit_done"], u + 1)
                src = ps[:, u % 4, :]
                if g in (FQ, SQ):
                    ins = act.activation((qf if g == FQ else qs)[:, r, :], src, ACT.Copy, scale=HD ** -0.5)
                elif g in (FK, SK):
                    ins = act.activation((kf if g == FK else ks)[:, r, :], src, ACT.Copy)
                elif g in (FV, SV):
                    ins = act.activation((vf if g == FV else vs)[:, r, :], src, ACT.Copy)
                else:
                    ins = act.activation(gate[:, r, :], src, ACT.Exp, scale=-1.0)
                ins.then_inc(S["unit_ready"], 1)

            for m in range(1, 4):
                win_high(m)
            for g in range(len(GROUP_COLS)):
                if 2 * g + 4 < WIN_PIECES:
                    win_high(2 * g + 4)
                for r in range(4):
                    unit_out(4 * g + r)
                if g == 0:
                    forget_log()
                if 2 * g + 5 < WIN_PIECES:
                    win_high(2 * g + 5)

            def exp_clamped(h, n):
                act.wait_ge(S["clamped"], 3 * h + n + 1)
                act.activation(sp_part[n], sp_part[n], ACT.Exp).then_inc(S["sp_exp"], 1)

            def log_one(h, n):
                act.wait_ge(S["sp_exp"], 3 * h + n + 1)
                act.activation(sp_part[n], sp_part[n], ACT.Ln, bias=1.0).then_inc(S["sp_log"], 1)

            def stick(h, n):
                act.wait_ge(S["r_ready"], 3 * h + n + 1)
                if h:
                    act.wait_ge(S["sb_ready"], h)
                act.activation(wT_part[n], z_part[n], ACT.Exp).then_inc(S["stick_ready"], 1)

            def prob_exp(h, b):
                act.wait_ge(S["max_ready"], 4 * h + b + 1)
                if h:
                    act.wait_ge(S["t_up"], 4 * (h - 1) + b + 1)
                act.activation(pr[b], ps[:, b % 2, 0:(b + 1) * P], ACT.Exp, bias=nmax[:, h % 2, b:b + 1],
                               accum_out=lsum[:, h, b:b + 1]).then_inc(S["prob_ready"], 1)

            def square(kind, h):
                ready, done, freed, dst = ((S["fox_ready"], S["fox_sq"], S["rms_ask"], sq_fox),
                                           (S["sb_ready"], S["sb_sq"], S["rms_ask"], sq_sb))[kind]
                act.wait_ge(ready, h + 1)
                if h:
                    act.wait_ge(S["rms_ask"], 2 * h - 1 + kind)
                act.activation(dst, ps[:, (FOX_OUT, SB_OUT)[kind], 0:256], ACT.Square).then_inc(done, 1)

            for h in range(HEADS):
                for n in range(3):
                    exp_clamped(h, n)
                prob_exp(h, 0)
                if h:
                    square(0, h - 1)
                log_one(h, 0)
                prob_exp(h, 1)
                if h:
                    square(1, h - 1)
                log_one(h, 1)
                log_one(h, 2)
                prob_exp(h, 2)
                stick(h, 0)
                prob_exp(h, 3)
                stick(h, 1)
                stick(h, 2)
            square(0, HEADS - 1)
            square(1, HEADS - 1)

            for n, t in enumerate(OT_ORDER):
                act.wait_ge(S["oT_up"], n + 1)
                act.activation(oT_split[0][:, t, :], ps[:, n % 4, :], ACT.Copy,
                               scale=cols[:, COL_ONG + t:COL_ONG + t + 1]).then_inc(S["oT_high"], 1)
            def high(turn, j):
                n0 = j if turn is None else GU_PIECES + j
                landed = 16 * (n0 // RAW_SLOTS + 1)
                act.wait_ge(raw_landed[n0 % RAW_SLOTS],
                            landed if turn is None else 16 * (CHUNK_PIECES // RAW_SLOTS) * turn + landed)
                if turn is not None:
                    act.wait_ge(S["piece_used"], CHUNK_PIECES * turn + n0 - SPLIT_SLOTS + 1)
                elif j >= SPLIT_SLOTS:
                    act.wait_ge(S["piece_used"], j - SPLIT_SLOTS + 1)
                act.activation(split_piece(n0 % SPLIT_SLOTS, 0), raw_piece(n0 % RAW_SLOTS), ACT.Copy
                               ).then_inc(S["split_h"], 1)

            for b in range(TB):
                if b == TB - 1:
                    act.wait_ge(S["y_up"], TB)
                    for j in range(3):
                        high(None, j)
                act.wait_ge(S["nT_up"], 2 * b + 1)
                for t in range(4):
                    ins = act.activation(u2T[:, t, b * P:(b + 1) * P], ps[:, 0, t * P:(t + 1) * P],
                                         ACT.Identity, scale=in2[:, 0, t:t + 1], bias=in2[:, 1, t:t + 1])
                ins.then_inc(S["u2T_ready"], 1)
            high(None, 3)
            act.wait_ge(S["rcopy_ready"], 1)
            act.activation(prob, prob, ACT.Exp).then_inc(S["rexp"], 1)

            def hidden_silu(used, before=None):
                act.wait_ge(S["piece_used"], used)
                if before is not None:
                    act.wait_ge(S["h_ready"], before)
                act.activation(silu, wide_bank(0), ACT.Silu).then_inc(S["silu_done"], 1)

            def turned_high(up, count, part, done):
                act.wait_ge(up, count)
                act.activation(re_part(part), wide_bank(6), ACT.Copy).then_inc(done, 1)

            def store_rows(made, count):
                act.wait_ge(S["y_out"], count)
                act.dma_start(result_dram[made, :], rows_out).then_inc(S["rows_stored"], 16)

            act.preload_act_table_set("silu_and_others")
            turned_high(S["rows_up"], 1, XH, S["xT_high"])
            for j in range(SPLIT_SLOTS, GU_PIECES):
                high(None, j)
            for j in range(2):
                high(0, j)
            hidden_silu(GU_PIECES)
            turned_high(S["rows_up"], 2, XH, S["xT_high"])
            act.wait_ge(S["spare_cleared"], 16)
            act.sem_inc(S["rows_stored"], 16)
            last = act.value_load(table[0:1, G_COL:G_COL + 1], min_val=E - 1, max_val=MAX_CHUNKS - 1)

            def turn(i, split):
                for j in range(split, 4):
                    high(i, j)
                turned_high(S["h_up"], i + 1, HH, S["hT_high"])
                for j in range(4, 7):
                    high(i, j)
                store_rows(bass.ds(i * FC, FC), i + 1)
                for j in range(7, CHUNK_PIECES):
                    high(i, j)
                hidden_silu(CHUNK_PIECES * i + 2 * GU_PIECES, before=i + 1)
                turned_high(S["rows_up"], i + 3, XH, S["xT_high"])

            turn(0, 2)
            with act.Fori(0, last - 1) as n:
                turn(n + 1, 0)
            for j in range(DN_PIECES):
                high(last, j)
            turned_high(S["h_up"], last + 1, HH, S["hT_high"])
            store_rows(bass.ds(last * FC, FC), last + 1)
            store_rows(bass.ds(last * FC + FC, FC), last + 2)
            for b in range(TB):
                act.wait_ge(S["fin_shift"], b + 1)
                act.activation(back[0][b], resid[:, b, :], ACT.Identity, scale=rstd[:, 1, b:b + 1],
                               bias=rstd[:, 0, b:b + 1]).then_inc(S["fin_scaled"], 1)

        @block.tensor
        def _(pe):
            pe.wait_ge(S["consts"], 1)
            pe.wait_ge(S["rows_landed"], 80)
            pe.transpose(ps[:, 7, 0:N_COLS], col_stage[:], ident[0:N_COLS, 0:N_COLS]).then_inc(S["cols_up"], 1)
            pe.wait_ge(S["x_landed"], 16)

            def x_tile(t):
                for b in range(TB):
                    ins = pe.transpose(ps[:, t % 7, b * P:(b + 1) * P], x_tok[:, b, t * P:(t + 1) * P], ident[:])
                ins.then_inc(S["xT_up"], 1)

            def mod_column(pos):
                pe.wait_ge(S["mod_summed"], pos + 1)
                for t in range(KT):
                    ins = pe.matmul(ps[:, mod_bank(pos), pos * KT + t:pos * KT + t + 1], mod_sum(pos)[:, t * P:(t + 1) * P],
                                    one_col[:], start=True, stop=True)
                ins.then_inc(S["mod_up"], 1)

            for t in range(7):
                x_tile(t)
            mod_column(0)
            mod_column(1)
            pe.wait_ge(S["uT_ready"], 1)
            x_tile(7)
            pe.wait_ge(S["uT_ready"], KT // 2)
            pe.wait_ge(S["uT_ready_d"], KT // 2)

            def product(out, lhs, rhs, first, last):
                for n, (a, b) in enumerate(((0, 0), (0, 1), (1, 0))):
                    ins = pe.matmul(out, lhs[a], rhs[b], start=first and n == 0, stop=last and n == 2)
                return ins

            for m in range(WIN_PIECES):
                g, part = divmod(m, 2)
                if m in MOD_BEFORE:
                    mod_column(MOD_BEFORE[m])
                pe.wait_ge(S["front_freed"], FRONT_AT["win", m] + 1)
                w = [tiles(split_piece(m % SPLIT_SLOTS, n), 4) for n in range(2)]
                pe.wait_ge(S["uT_split_done"], 2 * part + 2 if m < 2 else 4)
                for r in range(4):
                    u = 4 * g + r
                    if g and part == 0:
                        pe.wait_ge(S["unit_ready"], u - 3)
                    for k in range(4):
                        t = 4 * part + k
                        tok = [uT_split[n][:, t, r * P:(r + 1) * P] for n in range(2)]
                        if g in (FV, SV, GATE):
                            lhs, rhs = tok, [w[n][:, k, :] for n in range(2)]
                        else:
                            lhs = [w[n][:, k, r * P:(r + 1) * P] for n in range(2)]
                            rhs = [uT_split[n][:, t, :] for n in range(2)]
                        ins = product(ps[:, r, :], lhs, rhs, t == 0, t == KT - 1)
                    if part == 1:
                        ins.then_inc(S["unit_done"], 1)
                if part == 0:
                    ins.then_inc(S["first_half_used"], 1)
                if m == 1:
                    pe.wait_ge(S["wf_landed"], 16)
                    pe.wait_ge(S["mod_ready"], 2)
                    for t in range(KT):
                        ins = pe.matmul(ps[0:HEADS, 7, :], w_forget[:, t, :], uT[:, t, :], start=(t == 0),
                                        stop=(t == KT - 1))
                    ins.then_inc(S["f_up"], 1)
            pe.wait_ge(S["mod_ready"], 7)
            pe.transpose(ps[0:N_ROWS * KT, 7, 0:P], modc[:], ident[:]).then_inc(S["rows_turned"], 1)

            def place(h):
                return slice(HD * (h % 2), HD * (h % 2) + HD), h // 2

            def stick_scores(h, n):
                rows, t = place(h)
                if h:
                    pe.wait_ge(S["stick_ready"], 3 * (h - 1) + n + 1)
                for i in ((2, 3), (1,), (0,))[n]:
                    bank, at = Z_AT[i]
                    pe.matmul(ps[:, bank, at:at + P], ident_b[:], mask_sb[:], start=(i != 3), stop=False,
                              skip_group_check=True)
                    ins = pe.matmul(ps[:, bank, at:at + (TB - i) * P], ks[rows, t, i * P:(i + 1) * P],
                                    qs[rows, t, i * P:T], start=False, stop=True, skip_group_check=True)
                ins.then_inc(S["z_ready"], 1)

            def fox_scores(h, b):
                rows, t = place(h)
                n = 4 * h + b
                if n >= 2:
                    pe.wait_ge(S["prob_ready"], n - 1)
                cols_ = (b + 1) * P
                pe.matmul(ps[:, b % 2, b * P:cols_], ident_b[:], mask_fox[:], start=True, stop=False,
                          skip_group_check=True)
                pe.matmul(ps[:, b % 2, 0:cols_], head_sel[:, h, :], f_split[:, 0:cols_], start=False,
                          stop=False, skip_group_check=True)
                pe.matmul(ps[:, b % 2, 0:cols_], qf[rows, t, b * P:(b + 1) * P], kf[rows, t, 0:cols_],
                          start=False, stop=True, skip_group_check=True).then_inc(S["s_ready"], 1)

            def fox_turn(h, b):
                n = 4 * h + b
                pe.wait_ge(S["prob_ready"], n + 1)
                pe.wait_ge(S["pT_ready"], n)
                for i in range(b + 1):
                    ins = pe.transpose(ps[:, 2, i * P:(i + 1) * P], pr[b][:, i * P:(i + 1) * P], ident[:])
                ins.then_inc(S["t_up"], 1)

            def fox_values(h, b):
                n = 4 * h + b
                pe.wait_ge(S["pT_ready"], n + 1)
                if b == 0 and h:
                    pe.wait_ge(S["fox_freed"], h)
                for i in range(b + 1):
                    ins = pe.matmul(ps[:, FOX_OUT, b * HD:(b + 1) * HD], pT[b][:, i * P:(i + 1) * P],
                                    vf[:, i, h * HD:(h + 1) * HD], start=(i == 0), stop=(i == b))
                if b == TB - 1:
                    ins.then_inc(S["fox_ready"], 1)

            def stick_sums(h, n):
                pe.wait_ge(S["sp_ready"], 3 * h + n + 1)
                for i in ((3, 2), (1,), (0,))[n]:
                    bank, at = Z_AT[i]
                    end = at + (TB - i) * P
                    for k in (0, 1):
                        for j in range(i + 1, TB):
                            pe.matmul(ps[:, bank, at + (j - i) * P:end], neg_ones[:], sp_split[k][j], start=False,
                                      stop=False, skip_group_check=True)
                        ins = pe.matmul(ps[:, bank, at:end], neg_tri[:], sp_split[k][i], start=False, stop=(k == 1),
                                        skip_group_check=True)
                ins.then_inc(S["r_ready"], 1)

            def stick_values(h):
                pe.wait_ge(S["stick_ready"], 3 * h + 3)
                if h:
                    pe.wait_ge(S["sb_freed"], h)
                for b in range(TB):
                    for i in range(b + 1):
                        ins = pe.matmul(ps[:, SB_OUT, b * HD:(b + 1) * HD],
                                        wT[i][:, (b - i) * P:(b - i + 1) * P], vs[:, i, h * HD:(h + 1) * HD],
                                        start=(i == 0), stop=(i == b))
                ins.then_inc(S["sb_ready"], 1)

            pe.wait_ge(S["f_ready"], 1)
            pe.wait_ge(S["mod_ready"], 6)
            for h in range(HEADS):
                for n in range(3):
                    stick_scores(h, n)
                if h == 0:
                    pe.wait_ge(S["unit_ready"], UNITS)
                if h == HEADS - 1:
                    pe.wait_ge(S["z_ready"], 3 * HEADS)
                    pe.nop().then_inc(S["qk_dead"], 1)
                fox_scores(h, 0)
                fox_scores(h, 1)
                if h:
                    stick_values(h - 1)
                fox_turn(h, 0)
                fox_scores(h, 2)
                stick_sums(h, 0)
                fox_turn(h, 1)
                fox_values(h, 0)
                fox_scores(h, 3)
                stick_sums(h, 1)
                fox_turn(h, 2)
                fox_values(h, 1)
                stick_sums(h, 2)
                fox_turn(h, 3)
                fox_values(h, 2)
                fox_values(h, 3)
            stick_values(HEADS - 1)

            for n, t in enumerate(OT_ORDER):
                if t == 0:
                    pe.wait_ge(S["fox_gated"], HEADS - 2)
                    pe.wait_ge(S["unit_ready"], UNITS)
                    pe.wait_ge(S["pT_ready"], TB * HEADS)
                    pe.wait_ge(S["fox_freed"], HEADS)
                if t == 4:
                    pe.wait_ge(S["sb_freed"], HEADS - 2)
                if t == 3:
                    pe.wait_ge(S["fox_gated"], HEADS)
                if t == 7:
                    pe.wait_ge(S["sb_freed"], HEADS)
                if n >= 4:
                    pe.wait_ge(S["oT_ready"], n - 3)
                for b in range(TB):
                    ins = pe.transpose(ps[:, n % 4, b * P:(b + 1) * P], o_tok[:, b, t * P:(t + 1) * P], ident[:])
                ins.then_inc(S["oT_up"], 1)
            pe.wait_ge(S["oT_ready"], KT)
            pe.wait_ge(S["wout_split"], 8)

            def project_out(b, between=None):
                bank = 6 - 2 * (b % 2)
                if b >= 2:
                    pe.wait_ge(S["ln_freed"], b - 1)
                for half in range(2):
                    if half and between:
                        between()
                    for t in range(KT):
                        at = (t % 2) * D + half * 512
                        ins = product(ps[:, bank + half, :], [oT_split[n][:, t, b * P:(b + 1) * P] for n in range(2)],
                                      [split_piece(t // 2, n)[:, at:at + 512] for n in range(2)],
                                      t == 0, t == KT - 1)
                ins.then_inc(S["y_up"], 1)

            def turn_normed(b):
                pe.wait_ge(S["normed"], b + 1)
                for half in range(2):
                    if b:
                        pe.wait_ge((S["u2T_ready"], S["u2T_ready_d"])[half], b)
                    for t in range(4):
                        ins = pe.transpose(ps[:, half, t * P:(t + 1) * P],
                                           resid[:, b, (4 * half + t) * P:(4 * half + t + 1) * P], ident[:])
                    ins.then_inc(S["nT_up"], 1)

            def route(b):
                pe.wait_ge(S["u2T_ready"], b + 1)
                pe.wait_ge(S["u2T_ready_d"], b + 1)
                if b == 0:
                    pe.wait_ge(S["wr_landed"], 16)
                for t in range(KT):
                    ins = pe.matmul(ps[:, 2, b * E:(b + 1) * E], u2T[:, t, b * P:(b + 1) * P], wr[:, t, :],
                                    start=(t == 0), stop=(t == KT - 1))
                ins.then_inc(S["logits_up"], 1)

            project_out(0)
            project_out(1)
            turn_normed(0)
            project_out(2)
            turn_normed(1)
            project_out(3, between=lambda: turn_normed(2))
            for b in range(3):
                route(b)
            turn_normed(3)
            route(3)

            pe.wait_ge(S["routed_hot"], 1)
            for b in range(TB):
                for prev in range(b):
                    pe.matmul(ps[:, 3, b * E:(b + 1) * E], one_b, chosen[:, prev, :], start=(prev == 0), stop=False)
                pe.matmul(ps[:, 3, b * E:(b + 1) * E], before[:], chosen[:, b, :], start=(b == 0), stop=True)
            for b in range(TB):
                ins = pe.matmul(ps[:, 3, TB * E:TB * E + E], one_b, chosen[:, b, :], start=(b == 0), stop=(b == TB - 1))
            ins.then_inc(S["rank_up"], 1)
            pe.wait_ge(S["slots_ready"], 1)
            for n in range(2 * TB):
                ins = pe.matmul(ps[:, 3, 128:128 + MAX_CHUNKS + 1], slot_hot[:, n, :], chunk_tok[:, n, :],
                                start=(n == 0), stop=(n == 2 * TB - 1))
            ins.then_inc(S["idx_up"], 1)

            def use_piece(split, j, x, x_tile, bank, first, last):
                pe.wait_ge(S["split_l"], split)
                for k in range(2):
                    for half in range(2):
                        at = k * D + half * 512
                        t = x_tile + k
                        ins = product(ps[:, bank + half, :],
                                      [re_part(x + n)[:, t * P:(t + 1) * P] for n in range(2)],
                                      [split_piece(j % SPLIT_SLOTS, n)[:, at:at + 512] for n in range(2)],
                                      first and k == 0, last and k == 1)
                ins.then_inc(S["piece_used"], 1)

            def gate_up(split, j):
                use_piece(split, j, XH, j // 2 * 2, (0, 2)[j % 2], j < 2, j >= GU_PIECES - 2)

            def down(split, j):
                use_piece(split, j, HH, 2 * j, 4, j == 0, j == DN_PIECES - 1)

            def turn(src, up):
                for t in range(KT):
                    ins = pe.transpose(ps[:, 6 + t // 4, (t % 4) * P:(t % 4 + 1) * P], src[:, t * P:(t + 1) * P],
                                       ident[:])
                ins.then_inc(up, 1)

            pe.wait_ge(S["gathered"], 16)
            turn(rows_in, S["rows_up"])
            pe.wait_ge(S["xT_ready"], 1)
            for j in range(GU_PIECES):
                gate_up(j + 1, j)
            pe.wait_ge(S["gathered"], 32)
            turn(rows_in, S["rows_up"])
            pe.wait_ge(S["h_ready"], 1)
            pe.wait_ge(S["xT_ready"], 2)
            turn(h_tok, S["h_up"])
            pe.wait_ge(S["tables_ready"], 1)
            last = pe.value_load(table[0:1, G_COL:G_COL + 1], min_val=E - 1, max_val=MAX_CHUNKS - 1)
            with pe.Fori(0, last) as i:
                split = pe.snap(CHUNK_PIECES * i + GU_PIECES + 1)
                for j in range(GU_PIECES):
                    gate_up(split + j, j)
                pe.wait_ge(S["gathered"], 16 * i + 48)
                pe.wait_ge(S["hT_ready"], i + 1)
                turn(rows_in, S["rows_up"])
                pe.wait_ge(S["y_out"], i + 1)
                for j in range(DN_PIECES):
                    down(split + GU_PIECES + j, j)
                pe.wait_ge(S["h_ready"], i + 2)
                pe.wait_ge(S["xT_ready"], i + 3)
                turn(h_tok, S["h_up"])
            pe.wait_ge(S["hT_ready"], last + 1)
            pe.wait_ge(S["y_out"], last + 1)
            split = pe.snap(CHUNK_PIECES * last + GU_PIECES + 1)
            for j in range(DN_PIECES):
                down(split + j, j)

        @block.vector
        def _(dve):
            steps = [0]

            def step(ins):
                steps[0] += 1
                ins.then_inc(S["dve_step"], 1)
                dve.wait_ge(S["dve_step"], steps[0])

            dve.wait_ge(S["cols_up"], 1)
            step(dve.tensor_copy(cols[:], ps[:, 7, 0:N_COLS]))
            dve.nop().then_inc(S["cols_ready"], 1)
            dve.wait_ge(S["cond_exp"], 1)
            step(dve.tensor_scalar(cond[:, 1, :], cond[:, 0, :], 1.0, None, ALU.add))
            step(dve.reciprocal(cond[:, 2, :], cond[:, 1, :]))
            step(dve.tensor_tensor(cond[:, 0, :], cond[:, 2, :], cols[:, COL_C:COL_C + KT], ALU.mult))

            def mod_segment(pos):
                for part in range(4):
                    mod_piece(4 * pos + part)

            def mod_piece(m):
                pos, part = divmod(m, 4)
                n, acc = FRONT_AT["mod", m], mod_sum(pos)
                home = tiles(raw_piece(n % RAW_SLOTS), 2)
                dve.wait_ge(front_landed[n % RAW_SLOTS], 16 * (n // RAW_SLOTS + 1))
                if part == 0 and pos >= 2:
                    dve.wait_ge(S["mod_up"], pos - 1)
                for k in range(2):
                    t = 2 * part + k
                    if t == 0:
                        step(dve.tensor_scalar(acc, home[:, 0, :], cond[:, 0, 0:1], None, ALU.mult))
                    else:
                        step(dve.scalar_tensor_tensor(out=acc, in0=home[:, k, :], scalar=cond[:, 0, t:t + 1],
                                                      in1=acc, op0=ALU.mult, op1=ALU.add))
                if part == 3:
                    dve.nop().then_inc(S["mod_summed"], 1)
                dve.nop().then_inc(S["front_freed"], 1)

            def win_low(m):
                n = FRONT_AT["win", m]
                dve.wait_ge(S["front_split_h"], m + 1)
                dve.tensor_tensor(split_piece(m % SPLIT_SLOTS, 1), raw_piece(n % RAW_SLOTS),
                                  as_f32(split_piece(m % SPLIT_SLOTS, 0)), ALU.subtract).then_inc(S["front_freed"], 1)

            def uT_low(pair):
                dve.wait_ge(S["uT_high"], pair + 1)
                ts = slice(2 * pair, 2 * pair + 2)
                dve.tensor_tensor(uT_split[1][:, ts, :], uT[:, ts, :], as_f32(uT_split[0][:, ts, :]), ALU.subtract
                                  ).then_inc(S["uT_split_done"], 1)

            def mod_column(pos):
                seg = MOD_ORDER[pos]
                cs = slice(seg * KT, (seg + 1) * KT)
                dve.scalar_tensor_tensor(out=modc[:, cs], in0=ps[:, mod_bank(pos), pos * KT:(pos + 1) * KT],
                                         scalar=0.0 if seg in (SH_A, SH_F) else 1.0, in1=cols[:, cs],
                                         op0=ALU.add, op1=ALU.add).then_inc(S["mod_ready"], 1)

            mod_segment(0)
            mod_segment(1)
            dve.wait_ge(S["mod_up"], 2)
            mod_column(0)
            mod_column(1)
            dve.wait_ge(S["mod_ready"], 2)
            def uT_odd(t):
                dve.wait_ge(S["xT_up"], t + 1)
                dve.tensor_scalar(uT[:, t, :], ps[:, t % 7, :], modc[:, SC_A * KT + t:SC_A * KT + t + 1],
                                  modc[:, SH_A * KT + t:SH_A * KT + t + 1], ALU.mult, ALU.add
                                  ).then_inc(S["uT_ready_d"], 1)

            for t in (1, 3, 5):
                uT_odd(t)
            uT_low(0)
            uT_low(1)
            uT_odd(7)
            uT_low(2)
            uT_low(3)

            def forget_rows():
                dve.wait_ge(S["f_up"], 1)
                dve.wait_ge(S["uT_split_done"], KT // 2)
                dve.wait_ge(S["bf_landed"], 16)
                step(dve.tensor_scalar(fgt[0], ps[0:HEADS, 7, :], bf_col[:, 0:1], None, ALU.add))
                dve.scalar_tensor_tensor(out=fgt[1], in0=fgt[0], scalar=-1.0, in1=fgt[0], op0=ALU.mult, op1=ALU.max
                                         ).then_inc(S["f_abs"], 1)
                step(dve.tensor_scalar(fgt[0], fgt[0], 0.0, None, ALU.min))
                dve.wait_ge(S["f_exp"], 1)
                step(dve.tensor_tensor(fgt[2], fgt[1], fgt[0], ALU.subtract))
                step(dve.memset(fgt[1], 1.0))
                step(dve.tensor_tensor_scan(fgt[3], fgt[1], fgt[2], 0.0, ALU.mult, ALU.add))
                cur, nxt = fgt[3], fgt[0]
                for part in range(3):
                    dst = f_split[32 * part:32 * part + HEADS, :]
                    if part == 2:
                        dve.tensor_copy(dst, cur).then_inc(S["f_ready"], 1)
                    else:
                        step(dve.tensor_copy(dst, cur))
                        step(dve.tensor_copy(fgt[1], dst))
                        step(dve.tensor_tensor(nxt, cur, fgt[1], ALU.subtract))
                        cur, nxt = nxt, fgt[2]

            dve.wait_ge(S["front_freed"], 10)
            for kind, m in FRONT[10:]:
                if (kind, m) == ("win", 4):
                    forget_rows()
                (mod_piece if kind == "mod" else win_low)(m)
            dve.wait_ge(S["mod_up"], 6)
            for pos in range(2, 6):
                mod_column(pos)
            dve.wait_ge(S["mod_ready"], 6)
            g_c, b_c = cols[:, COL_LNG:COL_LNG + KT], cols[:, COL_LNB:COL_LNB + KT]
            sc_c, sh_c = modc[:, SC_F * KT:(SC_F + 1) * KT], modc[:, SH_F * KT:(SH_F + 1) * KT]
            dve.tensor_tensor(in2[:, 0, :], g_c, sc_c, ALU.mult)
            step(dve.tensor_tensor(in2[:, 1, :], b_c, sc_c, ALU.mult))
            dve.tensor_tensor(in2[:, 1, :], in2[:, 1, :], sh_c, ALU.add).then_inc(S["mod_ready"], 1)
            for r in range(TB):
                dve.wait_ge(S["unit_ready"], 4 * GATE + r + 1)
                step(dve.tensor_scalar(gate[:, r, :], gate[:, r, :], 1.0, None, ALU.add))
                dve.reciprocal(gate[:, r, :], gate[:, r, :]).then_inc(S["gate_ready"], 1)
            dve.wait_ge(S["rows_turned"], 1)
            dve.tensor_copy(mod_rows, ps[0:N_ROWS * KT, 7, 0:P]).then_inc(S["rows_copied"], 1)

            def clamp(h, n):
                dve.wait_ge(S["z_ready"], 3 * h + n + 1)
                dve.tensor_scalar(sp_part[n], z_part[n], BIG_Z, None, ALU.min).then_inc(S["clamped"], 1)

            def softplus(h, n):
                dve.wait_ge(S["sp_log"], 3 * h + n + 1)
                step(dve.tensor_tensor(sp_part[n], z_part[n], sp_part[n], ALU.max))
                step(dve.tensor_copy(sp_split_part[n][0], sp_part[n]))
                dve.tensor_tensor(sp_split_part[n][1], sp_part[n], as_f32(sp_split_part[n][0]), ALU.subtract
                                  ).then_inc(S["sp_ready"], 1)

            def row_max(h, b):
                dve.wait_ge(S["s_ready"], 4 * h + b + 1)
                dve.tensor_reduce(nmax[:, h % 2, b:b + 1], ps[:, b % 2, 0:(b + 1) * P], AX_X, ALU.max,
                                  negate=True).then_inc(S["max_ready"], 1)

            def turned(h, b):
                dve.wait_ge(S["t_up"], 4 * h + b + 1)
                dve.tensor_copy(pT[b], ps[:, 2, 0:(b + 1) * P]).then_inc(S["pT_ready"], 1)

            def rms_sum(kind, h):
                n = 2 * h + kind
                t = rms_t[:, n % 2]
                dve.wait_ge(S["fox_sq"] if kind == 0 else S["sb_sq"], h + 1)
                src = (sq_fox, sq_sb)[kind].rearrange("p (b n) -> p b n", b=TB)
                step(dve.tensor_reduce(t[:, 0, :], src, AX_X, ALU.add))
                if kind == 0:
                    l = lsum[:, h, :]
                    step(dve.scalar_tensor_tensor(out=lsum[:, h, :], in0=l, scalar=RMS_EPS, in1=l, op0=ALU.mult,
                                                  op1=ALU.mult))
                    dve.scalar_tensor_tensor(out=t[:, 1, :], in0=t[:, 0, :], scalar=1.0 / HD, in1=l,
                                             op0=ALU.mult, op1=ALU.add).then_inc(S["rms_ask"], 1)
                else:
                    dve.tensor_scalar(t[:, 1, :], t[:, 0, :], 1.0 / HD, RMS_EPS, ALU.mult, ALU.add
                                      ).then_inc(S["rms_ask"], 1)

            def rms_scale(kind, h):
                n = 2 * h + kind
                dve.wait_ge(S["rms_got"], n + 1)
                src = ps[:, (FOX_OUT, SB_OUT)[kind], 0:256].rearrange("p (b n) -> p b n", b=TB)
                dst = o_tok[:, :, kind * DG + h * HD:kind * DG + (h + 1) * HD]
                dve.tensor_tensor(dst, src, rms_t[:, n % 2, 2, :].unsqueeze(2).broadcast_to([P, TB, HD]), ALU.mult
                                  ).then_inc(S["fox_freed"] if kind == 0 else S["sb_freed"], 1)

            for h in range(HEADS):
                for n in range(3):
                    clamp(h, n)
                row_max(h, 0)
                row_max(h, 1)
                if h:
                    rms_sum(0, h - 1)
                softplus(h, 0)
                turned(h, 0)
                if h:
                    rms_scale(0, h - 1)
                row_max(h, 2)
                softplus(h, 1)
                turned(h, 1)
                if h:
                    rms_sum(1, h - 1)
                softplus(h, 2)
                row_max(h, 3)
                if h:
                    rms_scale(1, h - 1)
                turned(h, 2)
                turned(h, 3)
            for kind in range(2):
                rms_sum(kind, HEADS - 1)
                rms_scale(kind, HEADS - 1)

            for n, t in enumerate(OT_ORDER):
                dve.wait_ge(S["oT_high"], n + 1)
                dve.scalar_tensor_tensor(out=oT_split[1][:, t, :], in0=ps[:, n % 4, :],
                                         scalar=cols[:, COL_ONG + t:COL_ONG + t + 1], in1=as_f32(oT_split[0][:, t, :]),
                                         op0=ALU.mult, op1=ALU.subtract).then_inc(S["oT_ready"], 1)

            def statistics(b, ask):
                for half in range(2):
                    ins = dve.bn_stats(stats[:, half, :], resid[:, b, half * 512:(half + 1) * 512])
                step(ins)
                step(dve.bn_aggr(mv[:, b, :], stats[:].rearrange("p a n -> p (a n)")))
                dve.tensor_scalar(rstd[:, 0, b:b + 1], mv[:, b, 1:2], LN_EPS, None, ALU.add).then_inc(ask, 1)

            def first_norm(b):
                bank = 6 - 2 * (b % 2)
                dve.wait_ge(S["y_up"], b + 1)
                ins = dve.tensor_tensor(ln_tmp, ps[:, bank:bank + 2, :].rearrange("p a n -> p (a n)"), ga_row,
                                        ALU.mult)
                ins.then_inc(S["ln_freed"], 1)
                dve.wait_ge(S["ln_freed"], b + 1)
                if b == 0:
                    dve.wait_ge(S["xr_landed"], 16)
                step(dve.scalar_tensor_tensor(out=resid[:, b, :], in0=resid[:, b, :], scalar=ALPHA, in1=ln_tmp,
                                              op0=ALU.mult, op1=ALU.add))
                statistics(b, S["ln_ask"])
                dve.wait_ge(S["ln_got"], b + 1)
                dve.tensor_scalar(resid[:, b, :], resid[:, b, :], mv[:, b, 0:1], rstd[:, 1, b:b + 1],
                                  ALU.subtract, ALU.mult).then_inc(S["normed"], 1)

            def u2_half(b):
                dve.wait_ge(S["nT_up"], 2 * b + 2)
                for t in range(4, KT):
                    ins = dve.tensor_scalar(u2T[:, t, b * P:(b + 1) * P], ps[:, 1, (t - 4) * P:(t - 3) * P],
                                            in2[:, 0, t:t + 1], in2[:, 1, t:t + 1], ALU.mult, ALU.add)
                ins.then_inc(S["u2T_ready_d"], 1)

            dve.wait_ge(S["ga_landed"], 16)
            first_norm(0)
            first_norm(1)
            u2_half(0)
            first_norm(2)
            u2_half(1)
            u2_half(2)
            first_norm(3)
            u2_half(3)

            dve.wait_ge(S["logits_up"], TB)
            dve.wait_ge(S["rconst"], 1)
            dve.wait_ge(S["br_landed"], 16)

            def v3(a, s=E):
                return a.rearrange("p (b e) -> p b e", e=s)

            def wide(a, s=E):
                return a.unsqueeze(2).broadcast_to([P, a.shape[1], s])

            def over_b(a):
                return a.unsqueeze(1).broadcast_to([P, TB, a.shape[1]])

            m4, n16 = rout[:, 0:TB], rout[:, 16:16 + TB * GROUPS]
            logits = ps[:, 2, 0:TB * E]
            step(dve.tensor_reduce(m4, v3(logits), AX_X, ALU.max))
            dve.tensor_tensor(v3(prob), v3(logits), wide(m4), ALU.subtract).then_inc(S["rcopy_ready"], 1)
            dve.wait_ge(S["rexp"], 1)
            step(dve.tensor_reduce(m4, v3(prob), AX_X, ALU.add))
            step(dve.reciprocal(rout[:, 4:8], m4))
            step(dve.tensor_tensor(v3(prob), v3(prob), wide(rout[:, 4:8]), ALU.mult))
            step(dve.tensor_tensor(v3(sel), v3(prob), over_b(b_rout), ALU.add))
            s4 = v3(sel, EPG)
            n = TB * GROUPS
            dve.tensor_tensor(pair6[:, :, 0:3], s4[:, :, 1:4], s4[:, :, 0:1].broadcast_to([P, n, 3]), ALU.add)
            dve.tensor_tensor(pair6[:, :, 3:5], s4[:, :, 2:4], s4[:, :, 1:2].broadcast_to([P, n, 2]), ALU.add)
            step(dve.tensor_tensor(pair6[:, :, 5:6], s4[:, :, 3:4], s4[:, :, 2:3], ALU.add))
            step(dve.tensor_reduce(gscore, pair6, AX_X, ALU.max))

            def first_largest(dst, vals, tie, size):
                step(dve.tensor_reduce(m4, v3(vals, size), AX_X, ALU.max))
                step(dve.tensor_tensor(v3(dst, size), v3(vals, size), wide(m4, size), ALU.is_equal))
                step(dve.tensor_tensor(v3(dst, size), v3(dst, size), over_b(tie), ALU.mult))
                step(dve.tensor_reduce(m4, v3(dst, size), AX_X, ALU.max))
                step(dve.tensor_tensor(v3(dst, size), v3(dst, size), wide(m4, size), ALU.is_equal))

            first_largest(ghot, gscore, tie_g, GROUPS)
            step(dve.tensor_scalar(gtie, ghot, -NEG, NEG, ALU.mult, ALU.add))
            step(dve.tensor_tensor(v3(selm, EPG), s4, wide(ghot, EPG), ALU.mult))
            step(dve.tensor_tensor(v3(selm, EPG), v3(selm, EPG), wide(gtie, EPG), ALU.add))
            first_largest(hot[0], selm, tie_e, E)
            step(dve.scalar_tensor_tensor(out=selm, in0=hot[0], scalar=2.0 * NEG, in1=selm, op0=ALU.mult,
                                          op1=ALU.add))
            first_largest(hot[1], selm, tie_e, E)
            dve.tensor_tensor(chosen, v3(hot[0]), v3(hot[1]), ALU.add).then_inc(S["routed_hot"], 1)
            weights = small[:, 16:16 + 2 * TB]
            for k in range(2):
                step(dve.tensor_tensor(score, hot[k], prob, ALU.mult))
                step(dve.tensor_reduce(rout[:, 32 + 4 * k:36 + 4 * k], v3(score), AX_X, ALU.add))
            step(dve.tensor_tensor(m4, rout[:, 32:36], rout[:, 36:40], ALU.add))
            step(dve.reciprocal(rout[:, 4:8], m4))
            for k in range(2):
                dve.tensor_tensor(weights[:, k * TB:(k + 1) * TB], rout[:, 32 + 4 * k:36 + 4 * k],
                                  rout[:, 4:8], ALU.mult)

            def overflow(dst, src):
                op = ALU.is_ge if dst is where[1] else ALU.is_gt
                step(dve.tensor_scalar(dst, src, float(FC), None, op))
                for k in (2, 3):
                    step(dve.scalar_tensor_tensor(out=dst, in0=src, scalar=float(k * FC), in1=dst, op0=op,
                                                  op1=ALU.add))

            dve.wait_ge(S["rank_up"], 1)
            count, more, base, upto = (rout[:, 64 + 16 * n:80 + 16 * n] for n in range(4))
            one16 = rout[:, 144:160]
            rank = score
            dve.memset(one16, 1.0)
            dve.tensor_copy(rank, ps[:, 3, 0:TB * E])
            step(dve.tensor_copy(count, ps[:, 3, TB * E:TB * E + E]))
            overflow(more, count)
            step(dve.tensor_scalar(base, more, 1.0, None, ALU.add))
            step(dve.tensor_tensor_scan(upto, one16, base, 0.0, ALU.mult, ALU.add))
            step(dve.tensor_tensor(base, upto, base, ALU.subtract))
            overflow(where[1], rank)
            step(dve.scalar_tensor_tensor(out=where[0], in0=where[1], scalar=-float(FC), in1=rank, op0=ALU.mult,
                                          op1=ALU.add))
            step(dve.tensor_tensor(v3(where[1]), v3(where[1]), over_b(base), ALU.add))
            pos8, chunk8, dest8 = rout[:, 160:168], rout[:, 168:176], rout[:, 176:184]
            for k in range(2):
                for dst, val in ((pos8, where[0]), (chunk8, where[1])):
                    step(dve.tensor_tensor(selm, hot[k], val, ALU.mult))
                    step(dve.tensor_reduce(dst[:, k * TB:(k + 1) * TB], v3(selm), AX_X, ALU.add))
            dve.tensor_tensor(slot_hot, iota_r.unsqueeze(1).broadcast_to([P, 2 * TB, P]), wide(pos8, P), ALU.is_equal)
            nch = MAX_CHUNKS + 1
            step(dve.tensor_tensor(chunk_tok, iota_r[:, 0:nch].unsqueeze(1).broadcast_to([P, 2 * TB, nch]),
                                   wide(chunk8, nch), ALU.is_equal))
            for k in range(2):
                ins = dve.tensor_tensor(chunk_tok[:, k * TB:(k + 1) * TB, :],
                                        as_f32(chunk_tok[:, k * TB:(k + 1) * TB, :]),
                                        wide(tok_id, nch), ALU.mult)
            step(ins)
            dve.nop().then_inc(S["slots_ready"], 1)
            step(dve.scalar_tensor_tensor(out=dest8, in0=chunk8, scalar=float(FC), in1=pos8, op0=ALU.mult,
                                          op1=ALU.add))
            step(dve.tensor_scalar(dest8, dest8, float(FC), None, ALU.add))
            step(dve.tensor_copy(dest[:], dest8))
            of_chunk = RV[0:1, 512:512 + G_COL * E].rearrange("p (c e) -> p c e", e=E)
            step(dve.tensor_tensor(of_chunk, iota_r[0:1, 0:G_COL].unsqueeze(2).broadcast_to([1, G_COL, E]),
                                   upto[0:1, :].unsqueeze(1).broadcast_to([1, G_COL, E]), ALU.is_ge))
            step(dve.tensor_reduce(rout[0:1, 192:192 + G_COL], of_chunk, AX_X, ALU.add))
            dve.tensor_scalar(table[0:1, 0:G_COL], rout[0:1, 192:192 + G_COL], float(E - 1), None, ALU.min)
            step(dve.tensor_scalar(table[0:1, G_COL:G_COL + 1], upto[0:1, E - 1:E], -1.0, None, ALU.add))
            dve.nop().then_inc(S["tables_ready"], 1)
            dve.wait_ge(S["idx_up"], 1)
            step(dve.tensor_copy(row_idx[:], ps[:, 3, 128:128 + nch]))
            dve.nop().then_inc(S["idx_now"], 1)

            def low(turn, j):
                n0 = j if turn is None else GU_PIECES + j
                dve.wait_ge(S["split_h"], n0 + 1 if turn is None else CHUNK_PIECES * turn + n0 + 1)
                dve.tensor_tensor(split_piece(n0 % SPLIT_SLOTS, 1), raw_piece(n0 % RAW_SLOTS),
                                  as_f32(split_piece(n0 % SPLIT_SLOTS, 0)), ALU.subtract).then_inc(S["split_l"], 1)

            def turned_low(high, count, part, done):
                dve.wait_ge(high, count)
                dve.tensor_tensor(re_part(part + 1), wide_bank(6), as_f32(re_part(part)), ALU.subtract).then_inc(done, 1)

            def hidden(count):
                dve.wait_ge(S["silu_done"], count)
                dve.tensor_tensor(h_tok, silu, wide_bank(2), ALU.mult).then_inc(S["h_ready"], 1)

            def result(used, stored):
                dve.wait_ge(S["piece_used"], used)
                dve.wait_ge(S["rows_stored"], stored)
                dve.tensor_tensor(rows_out, wide_bank(4), gf_row, ALU.mult).then_inc(S["y_out"], 1)

            turned_low(S["xT_high"], 1, XH, S["xT_ready"])
            dve.wait_ge(S["split_l"], SPLIT_SLOTS)
            for j in range(SPLIT_SLOTS, GU_PIECES):
                low(None, j)
            for j in range(2):
                low(0, j)
            hidden(1)
            turned_low(S["xT_high"], 2, XH, S["xT_ready"])
            dve.wait_ge(S["gf_landed"], 16)
            last = dve.value_load(table[0:1, G_COL:G_COL + 1], min_val=E - 1, max_val=MAX_CHUNKS - 1)

            def turn(i, split):
                for j in range(split, 4):
                    low(i, j)
                result(CHUNK_PIECES * i + GU_PIECES, 16 * i + 16)
                turned_low(S["hT_high"], i + 1, HH, S["hT_ready"])
                for j in range(4, CHUNK_PIECES):
                    low(i, j)
                hidden(i + 2)
                turned_low(S["xT_high"], i + 3, XH, S["xT_ready"])

            turn(0, 2)
            with dve.Fori(0, last - 1) as n:
                turn(n + 1, 0)
            for j in range(DN_PIECES):
                low(last, j)
            result(CHUNK_PIECES * last + GU_PIECES, 16 * last + 16)
            turned_low(S["hT_high"], last + 1, HH, S["hT_ready"])
            result(CHUNK_PIECES * last + CHUNK_PIECES, 16 * last + 32)

            dve.wait_ge(S["x1_ready"], 1)

            def accumulate(b):
                for k in range(2):
                    dve.wait_ge(back_landed[2 * b + k], 16)
                    ins = dve.scalar_tensor_tensor(out=resid[:, b, :], in0=back[k][b],
                                                   scalar=weights[:, k * TB + b:k * TB + b + 1], in1=resid[:, b, :],
                                                   op0=ALU.mult, op1=ALU.add)
                    step(ins)
                statistics(b, S["fin_ask"])

            def rescale(b):
                dve.wait_ge(S["fin_got"], b + 1)
                dve.scalar_tensor_tensor(out=rstd[:, 0, b:b + 1], in0=mv[:, b, 0:1], scalar=-1.0,
                                         in1=rstd[:, 1, b:b + 1], op0=ALU.mult, op1=ALU.mult
                                         ).then_inc(S["fin_shift"], 1)

            def affine(b):
                dve.wait_ge(S["fin_scaled"], b + 1)
                step(dve.tensor_tensor(back[0][b], back[0][b], ln_rows[2], ALU.mult))
                dve.tensor_tensor(back[0][b], back[0][b], ln_rows[3], ALU.add).then_inc(fin_done[b], 1)

            accumulate(0)
            rescale(0)
            accumulate(1)
            rescale(1)
            accumulate(2)
            rescale(2)
            accumulate(3)
            rescale(3)
            affine(2)
            affine(3)


_INS = ['x', 'c', 'w_mod', 'b_mod', 'w_in', 'b_forget', 'out_norm_g', 'w_out', 'ln1_g', 'ln1_b',
        'w_router', 'b_router', 'w_gate', 'w_up', 'w_down', 'ln2_g', 'ln2_b']


def kernel(**inputs):
    import numpy as _np
    import concourse.bacc as _bacc
    from concourse import mybir as _mybir
    from concourse.bass_utils import run_bass_kernel_spmd as _run

    nc = _bacc.Bacc("TRN2", target_bir_lowering=False, num_devices=1)
    arrays, args = {}, []
    for name in _INS:
        a = _np.ascontiguousarray(inputs[name])
        arrays[f"in_{name}_dram"] = a
        args.append(nc.dram_tensor(f"in_{name}_dram", a.shape, _mybir.dt.from_np(a.dtype), kind="ExternalInput").ap())
    out = nc.dram_tensor("out_0_dram", (1, T, D), _mybir.dt.float32, kind="ExternalOutput").ap()
    build(nc, *args, out)
    r = _run(nc, [arrays], core_ids=[0])
    return r.results[0]["out_0_dram"]
```
